# Optimizing a Trainium2 kernel written in Bass

```python
import functools
import jax, jax.numpy as jnp
from jax import lax
import numpy as np

D_MODEL = 1024
BATCH = 1
SEQ = 1024
DEPTH = 1
DEC_BATCH = 8
DEC_SEQ = 4
PAST_LEN = 512
PAGE_SIZE = 128

HEAD_DIM = 64
A_HEADS = 8
A_WIDTH = A_HEADS * HEAD_DIM
CHUNK = 128
B_HEADS = 8
B_KV_HEADS = 4
B_WIDTH = B_HEADS * HEAD_DIM
KV_WIDTH = B_KV_HEADS * HEAD_DIM
MIX_WIDTH = A_WIDTH + B_WIDTH
IDX_HEADS = 4
IDX_DIM = 64
TOPK_MAX = 256
Q_BLOCK = 128
ROPE_THETA = 500000.0
ROT_DIM = HEAD_DIM // 4
ATTN_SCALE = HEAD_DIM ** -0.5
N_GROUPS = 4
EXPERTS_PER_GROUP = 8
N_EXPERTS = N_GROUPS * EXPERTS_PER_GROUP
TOP_K_EXPERTS = 2
D_EXPERT = 512
DEEPNORM_ALPHA = (2.0 * DEPTH) ** 0.25
DEEPNORM_BETA = (8.0 * DEPTH) ** -0.25
LN_EPS = 1e-5
S_AU = A_WIDTH
S_AV = S_AU + A_WIDTH
S_Q = S_AV + B_WIDTH
S_K = S_Q + KV_WIDTH
S_V = S_K + KV_WIDTH
S_QI = S_V + IDX_HEADS * IDX_DIM
S_KI = S_QI + IDX_DIM
IN_WIDTH = S_KI + IDX_HEADS
IN_SPLITS = (S_AU, S_AV, S_Q, S_K, S_V, S_QI, S_KI)

kernel_name = 'hymba_gmlp_dsa_hmoe_step'

def layer_norm(x, g, b):
    xf = x.astype(jnp.float32)
    mu = jnp.mean(xf, axis=-1, keepdims=True)
    var = jnp.mean(jnp.square(xf - mu), axis=-1, keepdims=True)
    y = (xf - mu) * lax.rsqrt(var + LN_EPS)
    return (y * g.astype(jnp.float32) + b.astype(jnp.float32)).astype(x.dtype)

def rotary(x, pos):
    half = ROT_DIM // 2
    inv_freq = ROPE_THETA ** (-jnp.arange(half, dtype=jnp.float32) * 2.0 / ROT_DIM)
    ang = pos.astype(jnp.float32)[:, None] * inv_freq[None, :]
    cos = jnp.cos(ang)[:, None, :]
    sin = jnp.sin(ang)[:, None, :]
    x1 = x[..., :half].astype(jnp.float32)
    x2 = x[..., half:ROT_DIM].astype(jnp.float32)
    rot = jnp.concatenate([x1 * cos - x2 * sin, x2 * cos + x1 * sin], axis=-1).astype(x.dtype)
    return jnp.concatenate([rot, x[..., ROT_DIM:]], axis=-1)

def chunk_spatial_gate(u, v, w_s, b_s):
    B, T, H, Dh = v.shape
    C = min(T, CHUNK)
    nc = T // C
    w = jnp.tril(w_s[:, :C, :C])
    vb = v.reshape(B, nc, C, H, Dh)
    s = jnp.einsum('hts,bcshd->bcthd', w, vb) + jnp.transpose(b_s[:, :C])[:, :, None]
    return (u * s.reshape(B, T, H, Dh)).reshape(B, T, H * Dh)

def index_select(qi, ki_all, wi, tpos, topk):
    L = ki_all.shape[1]
    s = jax.nn.relu(jnp.einsum('bthd,bsd->bths', qi, ki_all).astype(jnp.float32))
    score = jnp.einsum('bths,bth->bts', s, wi.astype(jnp.float32))
    adm = jnp.arange(L)[None, :] <= tpos[:, None]
    score = jnp.where(adm[None], score, -jnp.inf)
    _, sel = lax.top_k(score, topk)
    valid = sel <= tpos[None, :, None]
    return sel, valid

def attend(q, ks, vs, valid):
    B, T, H, Dh = q.shape
    qg = q.reshape(B, T, B_KV_HEADS, H // B_KV_HEADS, Dh)
    s = jnp.einsum('btngd,btknd->btngk', qg, ks).astype(jnp.float32) * ATTN_SCALE
    s = jnp.where(valid[:, :, None, None, :], s, -jnp.inf)
    p = jax.nn.softmax(s, axis=-1).astype(vs.dtype)
    o = jnp.einsum('btngk,btknd->btngd', p, vs)
    return o.reshape(B, T, H * Dh)

def sparse_attention_prompt(q, k, v, qi, ki, wi):
    B, T = q.shape[:2]
    topk = min(TOPK_MAX, T // 4)
    nb = T // Q_BLOCK
    tpos = jnp.arange(T).reshape(nb, Q_BLOCK)
    bidx = jnp.arange(B)[:, None, None]

    def blocks(a):
        return a.reshape((B, nb, Q_BLOCK) + a.shape[2:]).swapaxes(0, 1)

    def one_block(args):
        qb, qib, wib, tb = args
        sel, valid = index_select(qib, ki, wib, tb, topk)
        return attend(qb, k[bidx, sel], v[bidx, sel], valid)

    out = lax.map(one_block, (blocks(q), blocks(qi), blocks(wi), tpos))
    return out.swapaxes(0, 1).reshape(B, T, B_WIDTH)

def sparse_attention_sample(q, k, v, qi, ki, wi, k_pool, v_pool, ki_pool, page_table):
    DB, T = q.shape[:2]
    page = k_pool.shape[1]
    past = page_table.shape[1] * page
    topk = min(TOPK_MAX, (past + T) // 4)
    ki_past = ki_pool[page_table].reshape(DB, past, IDX_DIM)
    ki_all = jnp.concatenate([ki_past, ki], axis=1)
    tpos = past + jnp.arange(T)
    sel, valid = index_select(qi, ki_all, wi, tpos, topk)
    bidx = jnp.arange(DB)[:, None, None]
    sp = jnp.minimum(sel, past - 1)
    phys = page_table[bidx, sp // page]
    off = sp % page
    sn = jnp.clip(sel - past, 0, T - 1)
    in_past = (sel < past)[..., None, None]
    ks = jnp.where(in_past, k_pool[phys, off], k[bidx, sn])
    vs = jnp.where(in_past, v_pool[phys, off], v[bidx, sn])
    return attend(q, ks, vs, valid)

def hier_moe(x, w_group_router, w_expert_router, w_gate, w_up, w_down):
    N = x.shape[0]
    gp = jax.nn.softmax((x @ w_group_router).astype(jnp.float32), axis=-1)
    g_sel = jnp.argmax(gp, axis=-1)
    g_w = jnp.take_along_axis(gp, g_sel[:, None], axis=-1)
    el = jnp.einsum('nd,dge->nge', x, w_expert_router).astype(jnp.float32)
    el = jnp.take_along_axis(el, g_sel[:, None, None], axis=1)[:, 0]
    top_p, top_e = lax.top_k(jax.nn.softmax(el, axis=-1), TOP_K_EXPERTS)
    wts = (g_w * top_p / jnp.sum(top_p, axis=-1, keepdims=True)).reshape(-1)
    eid = (g_sel[:, None] * EXPERTS_PER_GROUP + top_e).reshape(-1)
    tok = jnp.repeat(jnp.arange(N), TOP_K_EXPERTS)
    order = jnp.argsort(eid)
    tok_s = tok[order]
    sizes = jnp.bincount(eid, length=N_EXPERTS).astype(jnp.int32)
    xs = x[tok_s]
    hid = jax.nn.silu(lax.ragged_dot(xs, w_gate, sizes)) * lax.ragged_dot(xs, w_up, sizes)
    ys = lax.ragged_dot(hid, w_down, sizes) * wts[order][:, None].astype(x.dtype)
    return jax.ops.segment_sum(ys, tok_s, num_segments=N)

def decoder_layer(x, c, pos, attn_core, w_ada, b_ada, w_in, a_ln_g, a_ln_b, w_spatial, b_spatial,
                  w_out, ln1_g, ln1_b, w_group_router, w_expert_router, w_gate, w_up, w_down,
                  ln2_g, ln2_b):
    B, T, D = x.shape
    mod = (jax.nn.silu(c) @ w_ada + b_ada)[:, None, :]
    shift1, scale1, gate1, shift2, scale2, gate2 = jnp.split(mod, 6, axis=-1)
    h = x * (1 + scale1) + shift1
    au, av, q, k, v, qi, ki, wi = jnp.split(h @ w_in, IN_SPLITS, axis=-1)
    u = jax.nn.gelu(au).reshape(B, T, A_HEADS, HEAD_DIM)
    vg = layer_norm(jax.nn.gelu(av).reshape(B, T, A_HEADS, HEAD_DIM), a_ln_g, a_ln_b)
    q = rotary(q.reshape(B, T, B_HEADS, HEAD_DIM), pos)
    k = rotary(k.reshape(B, T, B_KV_HEADS, HEAD_DIM), pos)
    v = v.reshape(B, T, B_KV_HEADS, HEAD_DIM)
    qi = rotary(qi.reshape(B, T, IDX_HEADS, IDX_DIM), pos)
    ki = rotary(ki[:, :, None, :], pos)[:, :, 0, :]
    a_out = chunk_spatial_gate(u, vg, w_spatial, b_spatial)
    b_out = attn_core(q, k, v, qi, ki, wi)
    mixed = jnp.concatenate([a_out, b_out], axis=-1) @ w_out
    x = layer_norm(DEEPNORM_ALPHA * x + gate1 * mixed, ln1_g, ln1_b)
    h = x * (1 + scale2) + shift2
    f = hier_moe(h.reshape(B * T, D), w_group_router, w_expert_router, w_gate, w_up, w_down).reshape(B, T, D)
    x = layer_norm(DEEPNORM_ALPHA * x + gate2 * f, ln2_g, ln2_b)
    return x, (k, v, ki, vg)

def _normal(key, shape, scale):
    return jax.random.normal(key, shape, jnp.float32) * scale

def setup_inputs(seed: int = 0) -> dict:
    key = jax.random.key(seed)
    ks = jax.random.split(key, 26)
    n_pages = PAST_LEN // PAGE_SIZE
    n_used = DEC_BATCH * n_pages
    n_pool = n_used + max(1, n_used // 4)
    L, D = DEPTH, D_MODEL
    page_table = jax.random.permutation(ks[7], n_pool)[:n_used].reshape(DEC_BATCH, n_pages).astype(jnp.int32)
    return {
        'x_prompt': _normal(ks[0], (BATCH, SEQ, D), 1.0),
        'x_sample': _normal(ks[1], (DEC_BATCH, DEC_SEQ, D), 1.0),
        'cache_k': _normal(ks[2], (L, n_pool, PAGE_SIZE, B_KV_HEADS, HEAD_DIM), 1.0),
        'cache_v': _normal(ks[3], (L, n_pool, PAGE_SIZE, B_KV_HEADS, HEAD_DIM), 1.0),
        'cache_kidx': _normal(ks[4], (L, n_pool, PAGE_SIZE, IDX_DIM), 1.0),
        'page_table': page_table,
        'c_prompt': _normal(ks[5], (BATCH, D), 1.0),
        'c_sample': _normal(ks[6], (DEC_BATCH, D), 1.0),
        'w_ada': _normal(ks[8], (L, D, 6 * D), 0.5 * D ** -0.5),
        'b_ada': _normal(ks[9], (L, 6 * D), 0.02),
        'w_in': _normal(ks[10], (L, D, IN_WIDTH), D ** -0.5),
        'a_ln_g': 1.0 + _normal(ks[11], (L, A_HEADS, HEAD_DIM), 0.05),
        'a_ln_b': _normal(ks[12], (L, A_HEADS, HEAD_DIM), 0.02),
        'w_spatial': _normal(ks[13], (L, A_HEADS, CHUNK, CHUNK), 0.5 * CHUNK ** -0.5),
        'b_spatial': 1.0 + _normal(ks[14], (L, A_HEADS, CHUNK), 0.1),
        'w_out': _normal(ks[15], (L, MIX_WIDTH, D), DEEPNORM_BETA * MIX_WIDTH ** -0.5),
        'ln1_g': 1.0 + _normal(ks[16], (L, D), 0.05),
        'ln1_b': _normal(ks[17], (L, D), 0.02),
        'w_group_router': _normal(ks[18], (L, D, N_GROUPS), D ** -0.5),
        'w_expert_router': _normal(ks[19], (L, D, N_GROUPS, EXPERTS_PER_GROUP), D ** -0.5),
        'w_gate': _normal(ks[20], (L, N_EXPERTS, D, D_EXPERT), D ** -0.5),
        'w_up': _normal(ks[21], (L, N_EXPERTS, D, D_EXPERT), D ** -0.5),
        'w_down': _normal(ks[22], (L, N_EXPERTS, D_EXPERT, D), DEEPNORM_BETA * D_EXPERT ** -0.5),
        'ln2_g': 1.0 + _normal(ks[23], (L, D), 0.05),
        'ln2_b': _normal(ks[24], (L, D), 0.02),
    }

def reference(x_prompt, x_sample, cache_k, cache_v, cache_kidx, page_table, c_prompt, c_sample,
              w_ada, b_ada, w_in, a_ln_g, a_ln_b, w_spatial, b_spatial, w_out, ln1_g, ln1_b,
              w_group_router, w_expert_router, w_gate, w_up, w_down, ln2_g, ln2_b):
    past = page_table.shape[1] * cache_k.shape[2]
    pos_prompt = jnp.arange(x_prompt.shape[1])
    pos_sample = past + jnp.arange(x_sample.shape[1])
    y_prompt, y_sample = x_prompt, x_sample
    kp, vp, kip, ksm, vsm, kism, cvs = [], [], [], [], [], [], []
    for l in range(DEPTH):
        weights = (w_ada[l], b_ada[l], w_in[l], a_ln_g[l], a_ln_b[l], w_spatial[l], b_spatial[l],
                   w_out[l], ln1_g[l], ln1_b[l], w_group_router[l], w_expert_router[l],
                   w_gate[l], w_up[l], w_down[l], ln2_g[l], ln2_b[l])
        y_prompt, (k_p, v_p, ki_p, _) = decoder_layer(
            y_prompt, c_prompt, pos_prompt, sparse_attention_prompt, *weights)
        sample_core = functools.partial(sparse_attention_sample, k_pool=cache_k[l], v_pool=cache_v[l],
                                        ki_pool=cache_kidx[l], page_table=page_table)
        y_sample, (k_s, v_s, ki_s, cv_s) = decoder_layer(
            y_sample, c_sample, pos_sample, sample_core, *weights)
        kp.append(k_p); vp.append(v_p); kip.append(ki_p)
        ksm.append(k_s); vsm.append(v_s); kism.append(ki_s); cvs.append(cv_s)
    return (y_prompt, y_sample, jnp.stack(kp), jnp.stack(vp), jnp.stack(kip),
            jnp.stack(ksm), jnp.stack(vsm), jnp.stack(kism), jnp.stack(cvs))


_drawn_inputs = setup_inputs


def setup_inputs(seed=0):
    import zlib

    import numpy as np

    out = dict(_drawn_inputs(seed))
    spreads = {}
    factors = {'cache_k': 3.941,
     'cache_v': 3.166,
     'cache_kidx': 3.591,
     'a_ln_b': 2.877,
     'b_spatial': 6.038,
     'ln1_b': 2.727,
     'ln2_b': 2.849}
    for name, (base, spread) in spreads.items():
        noise = np.random.default_rng([zlib.crc32(name.encode()), seed]).standard_normal(out[name].shape)
        drawn = base * np.exp(spread * noise) if base else spread * noise
        out[name] = __import__('jax').numpy.asarray(drawn.astype(out[name].dtype))
    for name, factor in factors.items():
        out[name] = (out[name] * factor).astype(out[name].dtype)
    return out
```

```python
from contextlib import ExitStack

import numpy as np
import concourse.bass as bass
from concourse import mybir

F32 = mybir.dt.float32
I32 = mybir.dt.int32
U32 = mybir.dt.uint32
ALU = mybir.AluOpType
ACT = mybir.ActivationFunctionType
AX = mybir.AxisListType.X

P = 128
D = 1024
DC = D // P
SEQ = 1024
SEQS, DSEQ = 8, 4
NS = SEQS * DSEQ
TILES = SEQ // P
TOK = SEQ + NS
HD = 64
AH = 8
QH, KVH, IH = 8, 4, 4
PAST, PAGE = 512, 128
NPG = PAST // PAGE
TOPK_P, TOPK_S = 256, (PAST + DSEQ) // 4
HALF = 8
THETA = 500000.0
NG, EPG = 4, 8
NE = NG * EPG
DE = 512
ALPHA = 2.0 ** 0.25
EPS = 1e-5
NEG_MASK = -1.0e30
NEG_INADM = -3.0e38
NEG_TAKEN = -3.4e38
MAXEXTRA = (2 * TOK) // P
SLOTS = NE + MAXEXTRA

GROUPS = [("idx", 2048, 324), ("q", 1024, 512), ("kv", 1536, 512), ("au", 0, 512), ("av", 512, 512)]


def rows(t):
    return P if t < TILES else NS


def constants():
    p = np.arange(P)
    inv = np.float32(THETA) ** (-np.arange(HALF, dtype=np.float32) * np.float32(2.0) / np.float32(2 * HALF))
    pos = np.zeros((P, TILES + 1), np.float32)
    for t in range(TILES):
        pos[:, t] = t * P + p
    pos[:, TILES] = PAST + p % DSEQ
    ang = (pos[:, :, None] * inv[None, None, :]).astype(np.float32)
    own = (p[:, None] % NS // DSEQ == np.arange(SEQS)[None]).astype(np.float32)
    blk = np.zeros((P, NS))
    blk[:NS] = (p[:NS, None] // DSEQ == p[None, :NS] // DSEQ) & (p[:NS, None] >= p[None, :NS])
    later = p[None, :] > p[:, None]
    newer = np.arange(DSEQ)[None] > (p % DSEQ)[:, None]
    c = {
        "ident": np.eye(P),
        "before": p[:, None] < p[None],
        "ones": np.ones((P, P)),
        "sametok": p[:, None] % NS == p[None] % NS,
        "cos": np.cos(ang), "sin": np.sin(ang),
        "later": later,
        "newneg": newer * NEG_INADM,
        "tril": p[:, None] >= p[None],
        "blktril": blk,
        "seqcol": np.broadcast_to((p[None, None, :NS] // DSEQ == np.arange(SEQS)[None, :, None]), (P, SEQS, NS)),
        "own": own,
        "iota": np.broadcast_to(p[None], (P, P)),
        "token": (np.arange(TILES + 1)[None] * P + p[:, None]) * ((np.arange(TILES + 1)[None] < TILES) | (p[:, None] < NS)),
        "valid": np.concatenate([np.ones((P, TILES)), (p < NS)[:, None]], axis=1),
        "steps": np.broadcast_to(P * np.arange(1, 9)[None], (P, 8)),
        "first": np.broadcast_to(8 - np.arange(8)[None], (P, 8)),
        "minushalf": np.full((P, 16), -0.5),
    }
    at, parts, n = {}, [], 0
    for k, v in c.items():
        v = np.ascontiguousarray(v, dtype=np.float32).reshape(P, -1)
        at[k] = (n, v.shape[1])
        n += v.shape[1]
        parts.append(v)
    return at, np.concatenate(parts, axis=1)


def step_kernel(nc, a, outs):
    at, table = constants()
    xs = a["x_sample"].rearrange("b t d -> (b t) d")
    x_tile = [a["x_prompt"][0, t * P:(t + 1) * P, :] for t in range(TILES)] + [xs]
    w_in = a["w_in"][0].rearrange("(c p) n -> p c n", p=P)
    w_ada = a["w_ada"][0].rearrange("(c p) n -> p c n", p=P)
    b_ada = a["b_ada"][0]
    new_k = [outs[2].rearrange("a b t h d -> (a b t) (h d)")[t * P:(t + 1) * P, :] for t in range(TILES)] + \
            [outs[5].rearrange("a b t h d -> (a b t) (h d)")]
    new_v = [outs[3].rearrange("a b t h d -> (a b t) (h d)")[t * P:(t + 1) * P, :] for t in range(TILES)] + \
            [outs[6].rearrange("a b t h d -> (a b t) (h d)")]
    new_kidx = [outs[4].rearrange("a b t d -> (a b t) d")[t * P:(t + 1) * P, :] for t in range(TILES)] + \
               [outs[7].rearrange("a b t d -> (a b t) d")]
    chunk_v = outs[8].rearrange("a b t h d -> (a b t) (h d)")

    mod_dram = nc.dram_tensor("mod_dram", (1 + SEQS, 6 * D), F32).ap()

    x1_dram = nc.dram_tensor("x1_dram", (TOK, D), F32).ap()
    h2_dram = nc.dram_tensor("h2_dram", (TOK, D), F32).ap()
    ys_dram = nc.dram_tensor("ys_dram", (SLOTS * P, D), F32).ap()

    with ExitStack() as keep, ExitStack() as tail:
        def sb(ctx, name, shape, dt=F32):
            return ctx.enter_context(nc.sbuf_tensor(name, shape, dt))

        def sem(ctx, name):
            return ctx.enter_context(nc.semaphore(name))

        psum = keep.enter_context(nc.psum_tensor("psum", [P, 8 * 512], F32))
        bank = [psum[:, 512 * i:512 * (i + 1)] for i in range(8)]
        banks56 = psum[:, 5 * 512:7 * 512]
        const = sb(keep, "const", [P, table.shape[1]])

        def c(name, r=P):
            n, w = at[name]
            return const[0:r, n:n + w]

        logit = sb(keep, "logit", [P, TILES + 1, NG + NE])

        q_nat = sb(tail, "q_nat", [P, TILES + 1, QH * HD])
        kT = sb(tail, "kT", [P, 2, TOK])
        kiT = sb(tail, "kiT", [HD, TOK])
        v_nat = sb(tail, "v_nat", [P, TILES + 1, KVH * HD])
        mixa = sb(tail, "mixa", [P, 4, TOK])
        bias_at = [P * t * (t + 1) // 2 for t in range(TILES)]
        bias = sb(tail, "bias", [P, P * TILES * (TILES + 1) // 2])
        qi_s = sb(tail, "qi_s", [HD, IH, NS])
        w_i = sb(tail, "w_i", [P, TILES + 1, IH])

        with ExitStack() as ctx:
            w_sb = sb(ctx, "w_sb", [P, DC, 2372])
            ada = q_nat[:, :, :].rearrange("p t n -> p (t n)")[:, 0:4096].rearrange("p (c n) -> p c n", c=DC)
            ada2 = mixa[:, :, :].rearrange("p t n -> p (t n)")[:, 0:4096].rearrange("p (c n) -> p c n", c=DC)
            ada_ring = [ada, ada2]
            x_nat = sb(ctx, "x_nat", [P, 2, D])
            hT = sb(ctx, "hT", [P, 2, DC, P])
            scale1 = sb(ctx, "scale1", [P, D])
            shift1 = sb(ctx, "shift1", [P, D])
            idx_nat = sb(ctx, "idx_nat", [P, 2, 324])
            k_nat = sb(ctx, "k_nat", [P, 2, KVH * HD])
            u = sb(ctx, "u", [P, 2, 512])
            vg = sb(ctx, "vg", [P, 2, 512])
            spat = sb(ctx, "spat", [P, 512])
            tmp = sb(ctx, "tmp", [P, 512])
            rot = tmp[:, 0:4 * QH * HALF].rearrange("p (i n) -> p i n", i=4)
            st8 = sb(ctx, "st8", [P, 3, AH])
            wspT = sb(ctx, "wspT", [P, AH, P])
            wsb4 = sb(ctx, "wsb4", [NS, AH, DSEQ])
            wsbd = tmp[0:NS, 0:AH * NS].rearrange("p (h t) -> p h t", h=AH)
            wsbdT = sb(ctx, "wsbdT", [NS, AH, NS])
            bsp = sb(ctx, "bsp", [P, AH])
            bsp_s = sb(ctx, "bsp_s", [NS, AH])
            aln_g = sb(ctx, "aln_g", [P, 512])
            aln_b = sb(ctx, "aln_b", [P, 512])
            qiT = sb(ctx, "qiT", [HD, IH, P])
            top8 = sb(ctx, "top8", [P, 8])
            cnat = x_nat[0:1 + SEQS, 0, :]
            cT = sb(ctx, "cT", [P, DC, 1 + SEQS])
            modn = u[0:1 + SEQS, :, :]
            bada = vg[0:1 + SEQS, :, :]
            wsp = hT[:, 0, :, :]

            s_const = sem(ctx, "s_const")
            s_c = sem(ctx, "s_c")
            s_silu = sem(ctx, "s_silu")
            s_ada = [sem(ctx, f"s_ada{i}") for i in range(2)]
            s_adamm = sem(ctx, "s_adamm")
            s_modn = sem(ctx, "s_modn")
            s_modst = [sem(ctx, f"s_modst{i}") for i in range(2)]
            s_win = [sem(ctx, f"s_win{g}") for g in range(5)]
            s_bc = sem(ctx, "s_bc")
            s_sp = sem(ctx, "s_sp")
            s_aln = sem(ctx, "s_aln")
            s_tril = sem(ctx, "s_tril")
            s_x = [sem(ctx, f"s_x{i}") for i in range(2)]
            s_h = sem(ctx, "s_h")
            s_trf = sem(ctx, "s_trf")
            s_tre = sem(ctx, "s_tre")
            s_mm = sem(ctx, "s_mm")
            s_ev = sem(ctx, "s_ev")
            s_rot = sem(ctx, "s_rot")
            s_ln = sem(ctx, "s_ln")
            s_idxp = sem(ctx, "s_idxp")
            s_relu = sem(ctx, "s_relu")
            s_acc = sem(ctx, "s_acc")
            s_sel = sem(ctx, "s_sel")
            s_spm = sem(ctx, "s_spm")
            s_spe = sem(ctx, "s_spe")
            s_am = sem(ctx, "s_am")
            s_st = [sem(ctx, f"s_st{i}") for i in range(2)]
            s_stv = sem(ctx, "s_stv")
            dvec = sem(ctx, "dvec")
            poolc = sem(ctx, "poolc")
            CH = [2, 3, 0, 1, 4, 5, 6, 7, 8, 9, 10, 11]

            TR = [("c", 0, 0)] + [("sp", 0, i) for i in range(2)] + [("spbd", 0, 0)] + [("h", 0, 0), ("h", 0, 1)]
            STEPS = []
            for t in range(TILES + 3):
                if t <= TILES:
                    STEPS.append(("group", t, 0))
                    if t + 1 <= TILES:
                        STEPS.append(("h", t + 1, 0))
                    STEPS.append(("group", t, 1))
                if 1 <= t <= TILES + 1:
                    STEPS.append(("post", t - 1, 0))
                if t <= TILES:
                    STEPS.append(("group", t, 2))
                if 3 <= t <= TILES:
                    STEPS += [("score", t - 1, 0), ("score", t - 1, 1)]
                if 2 <= t:
                    STEPS.append(("aT", t - 2, 0))
                if t <= TILES:
                    STEPS.append(("group", t, 3))
                if 3 <= t <= TILES:
                    STEPS += [("score", t - 1, 2), ("score", t - 1, 3)]
                if t <= TILES:
                    STEPS.append(("group", t, 4))
                if 1 <= t <= TILES + 1:
                    STEPS.append(("mix", t - 1, 0))
            for kind, t, _ in STEPS:
                if kind == "h" or kind == "post":
                    TR += [(kind, t, 0), (kind, t, 1)]
                if kind == "aT":
                    TR.append((kind, t, 0))
            TRN = {k: n for n, k in enumerate(TR)}
            IDX0 = 2

            with nc.Block() as block:
                @block.sync
                def _(sp):
                    sp.dma_start(const[:, :], a["table"]).then_inc(s_const, 16)
                    sp.dma_start(cnat[0:1, :], a["c_prompt"]).then_inc(s_c, 16)
                    sp.dma_start(cnat[1:1 + SEQS, :], a["c_sample"]).then_inc(s_c, 16)

                    def ada_load(n):
                        j = CH[n]
                        if n >= 2:
                            sp.wait_ge(s_adamm, n - 1)
                            sp.wait_ge(s_modn, n - 1)
                        sp.dma_start(ada_ring[n % 2], w_ada[:, :, j * 512:(j + 1) * 512]).then_inc(s_ada[n % 2], 16)
                        sp.dma_start(bada[:, n % 2, :], b_ada[j * 512:(j + 1) * 512].partition_broadcast(1 + SEQS)).then_inc(s_ada[n % 2], 16)

                    def mod_store(n):
                        j = CH[n]
                        sp.wait_ge(s_modn, n + 1)
                        sp.dma_start(mod_dram[:, j * 512:(j + 1) * 512], modn[:, n % 2, :]).then_inc(s_modst[n % 2], 16)

                    ada_load(0)
                    ada_load(1)
                    sp.dma_start(wsp, a["w_spatial"][0].rearrange("h t s -> t h s")).then_inc(s_sp, 16)
                    sp.dma_start(bsp[:, :], a["b_spatial"][0].rearrange("h t -> t h"),
                                 allow_slow_non_contiguous=True).then_inc(s_sp, 16)
                    for s in range(SEQS):
                        sp.dma_start(wsb4[s * DSEQ:(s + 1) * DSEQ, :, :],
                                     a["w_spatial"][0, :, 0:DSEQ, 0:DSEQ].rearrange("h t s -> t h s")).then_inc(s_sp, 16)
                        sp.dma_start(bsp_s[s * DSEQ:(s + 1) * DSEQ, :],
                                     a["b_spatial"][0, :, 0:DSEQ].rearrange("h t -> t h"),
                                 allow_slow_non_contiguous=True).then_inc(s_sp, 16)
                    sp.dma_start(aln_g[:, :], a["a_ln_g"][0].rearrange("h d -> (h d)").partition_broadcast(P)).then_inc(s_aln, 16)
                    sp.dma_start(aln_b[:, :], a["a_ln_b"][0].rearrange("h d -> (h d)").partition_broadcast(P)).then_inc(s_aln, 16)
                    for g, (_, n0, w) in enumerate(GROUPS):
                        sp.dma_start(w_sb[:, :, n0:n0 + w], w_in[:, :, n0:n0 + w]).then_inc(s_win[g], 16)
                        if g < 2:
                            ada_load(g + 2)
                            mod_store(g)
                    for n in range(4, 12):
                        ada_load(n)
                        mod_store(n - 2)
                    mod_store(10)
                    mod_store(11)
                    for i in range(2):
                        sp.wait_ge(s_modst[i], 16 * 6)
                    sp.dma_start(shift1[:, :], mod_dram[0, 0:D].partition_broadcast(P)).then_inc(s_bc, 16)
                    sp.dma_start(scale1[:, :], mod_dram[0, D:2 * D].partition_broadcast(P)).then_inc(s_bc, 16)
                    sp.wait_ge(s_trf, 1)
                    for t in range(2):
                        sp.dma_start(x_nat[:, t, :], x_tile[t]).then_inc(s_x[t], 16)
                    for t in range(TILES + 1):
                        r = rows(t)
                        if t + 2 <= TILES:
                            sp.wait_ge(s_trf, TRN[("h", t, 1)] + 1)
                            sp.dma_start(x_nat[0:rows(t + 2), t % 2, :], x_tile[t + 2]).then_inc(s_x[t % 2], 16)
                        if t == TILES - 1:
                            sp.wait_ge(s_h, TILES)
                            for i in range(SEQS):
                                sp.dma_start(shift1[i * DSEQ:(i + 1) * DSEQ, :],
                                             mod_dram[1 + i, 0:D].partition_broadcast(DSEQ)).then_inc(s_bc, 16)
                                sp.dma_start(scale1[i * DSEQ:(i + 1) * DSEQ, :],
                                             mod_dram[1 + i, D:2 * D].partition_broadcast(DSEQ)).then_inc(s_bc, 16)
                        sp.wait_ge(s_rot, t + 1)
                        sp.dma_start(new_k[t], k_nat[0:r, t % 2, :]).then_inc(s_st[t % 2], 16)
                        sp.dma_start(new_kidx[t], idx_nat[0:r, t % 2, 256:320]).then_inc(s_st[t % 2], 16)
                        sp.dma_start(new_v[t], v_nat[0:r, t, :]).then_inc(s_stv, 16)
                    sp.wait_ge(s_ln, TILES + 1)
                    sp.dma_start(chunk_v, vg[0:NS, TILES % 2, :]).then_inc(s_stv, 16)
                    sp.wait_ge(s_stv, 16 * (TILES + 2))
                    sp.wait_ge(s_st[0], 32 * 5)
                    sp.wait_ge(s_st[1], 32 * 4)

                @block.gpsimd
                def _(pool):
                    g = nc.gpsimd
                    count = [0]

                    def then(ins):
                        count[0] += 1
                        ins.then_inc(poolc, 1)
                        pool.wait_ge(poolc, count[0])

                    pool.wait_ge(s_const, 16)
                    pool.wait_ge(s_sp, 16 * (2 + 2 * SEQS))
                    g.tensor_tensor(wsp, wsp, c("tril").unsqueeze(1).to_broadcast([P, AH, P]), ALU.mult).then_inc(s_tril, 1)
                    g.tensor_tensor(wsbd[:, :, :].rearrange("p h (s i) -> p h s i", i=DSEQ),
                                    wsb4[:, :, :].unsqueeze(2).to_broadcast([NS, AH, SEQS, DSEQ]),
                                    c("blktril", NS).rearrange("p (s i) -> p s i", i=DSEQ).unsqueeze(1).to_broadcast([NS, AH, SEQS, DSEQ]),
                                    ALU.mult).then_inc(s_tril, 1)

                    def modulate(t):
                        r = rows(t)
                        pool.wait_ge(s_x[t % 2], 16 * (t // 2 + 1))
                        pool.wait_ge(s_bc, 32 if t < TILES else 32 + 32 * SEQS)
                        then(g.tensor_tensor(x_nat[0:r, t % 2, :], x_nat[0:r, t % 2, :], scale1[0:r, :], ALU.mult))
                        g.tensor_tensor(x_nat[0:r, t % 2, :], x_nat[0:r, t % 2, :], shift1[0:r, :], ALU.add).then_inc(s_h, 1)

                    def rotate(x, t, r, n):
                        cos = c("cos", r).rearrange("p (t k) -> p t k", k=HALF)[:, t:t + 1, :].to_broadcast([r, n, HALF])
                        sin = c("sin", r).rearrange("p (t k) -> p t k", k=HALF)[:, t:t + 1, :].to_broadcast([r, n, HALF])
                        m = [rot[0:r, i, 0:n * HALF].rearrange("p (n k) -> p n k", k=HALF) for i in range(4)]
                        g.tensor_tensor(m[0], x[:, :, 0:HALF], cos, ALU.mult)
                        g.tensor_tensor(m[1], x[:, :, HALF:2 * HALF], sin, ALU.mult)
                        g.tensor_tensor(m[2], x[:, :, HALF:2 * HALF], cos, ALU.mult)
                        then(g.tensor_tensor(m[3], x[:, :, 0:HALF], sin, ALU.mult))
                        g.tensor_tensor(x[:, :, 0:HALF], m[0], m[1], ALU.subtract)
                        return g.tensor_tensor(x[:, :, HALF:2 * HALF], m[2], m[3], ALU.add)

                    def head_sums(dst, x, r):
                        half = HD // 2
                        y = tmp[0:r, 0:AH * half].rearrange("p (h d) -> p h d", h=AH)
                        then(g.tensor_tensor(y, x[:, :, 0:half], x[:, :, half:HD], ALU.add))
                        while half > 2:
                            half //= 2
                            then(g.tensor_tensor(y[:, :, 0:half], y[:, :, 0:half], y[:, :, half:2 * half], ALU.add))
                        then(g.tensor_tensor(dst, y[:, :, 0], y[:, :, 1], ALU.add))

                    def gate(t):
                        r = rows(t)
                        b = (bsp if t < TILES else bsp_s)[0:r, :].unsqueeze(2).to_broadcast([r, AH, HD])
                        s = spat[0:r, :].rearrange("p (h d) -> p h d", h=AH)
                        pool.wait_ge(s_spe, t + 1)
                        then(g.tensor_tensor(s, s, b, ALU.add))
                        g.tensor_tensor(u[0:r, t % 2, :], u[0:r, t % 2, :], spat[0:r, :], ALU.mult).then_inc(s_am, 1)

                    modulate(0)
                    modulate(1)
                    for t in range(TILES + 1):
                        r = rows(t)
                        pool.wait_ge(s_ev, 5 * t + 1)
                        then(rotate(idx_nat[0:r, t % 2, 0:320].rearrange("p (n d) -> p n d", d=HD), t, r, 5))
                        g.tensor_copy(w_i[0:r, t, :], idx_nat[0:r, t % 2, 320:324])
                        pool.wait_ge(s_ev, 5 * t + 2)
                        then(rotate(q_nat[0:r, t, :].rearrange("p (n d) -> p n d", d=HD), t, r, QH))
                        pool.wait_ge(s_ev, 5 * t + 3)
                        rotate(k_nat[0:r, t % 2, :].rearrange("p (n d) -> p n d", d=HD), t, r, KVH).then_inc(s_rot, 1)
                        if t + 2 <= TILES:
                            modulate(t + 2)
                        x = vg[0:r, t % 2, :]
                        x3 = x.rearrange("p (h d) -> p h d", h=AH)
                        sq = tmp[0:r, :]
                        mean, var = st8[0:r, 0, :], st8[0:r, 1, :]
                        bc = lambda y: y.unsqueeze(2).to_broadcast([r, AH, HD])
                        pool.wait_ge(s_ev, 5 * t + 5)
                        pool.wait_ge(s_aln, 32)
                        pool.wait_ge(s_rot, t + 1)
                        head_sums(mean, x3, r)
                        then(g.tensor_scalar(mean, mean, 1.0 / HD, None, ALU.mult))
                        then(g.tensor_tensor(x3, x3, bc(mean), ALU.subtract))
                        then(g.tensor_tensor(sq, x, x, ALU.mult))
                        head_sums(var, sq.rearrange("p (h d) -> p h d", h=AH), r)
                        then(g.tensor_scalar(var, var, 1.0 / HD, EPS, ALU.mult, ALU.add))
                        then(g.tensor_tensor(var, var, c("minushalf", r)[:, 0:AH], ALU.pow))
                        then(g.tensor_tensor(x3, x3, bc(var), ALU.mult))
                        then(g.tensor_tensor(x, x, aln_g[0:r, :], ALU.mult))
                        g.tensor_tensor(x, x, aln_b[0:r, :], ALU.add).then_inc(s_ln, 1)
                        if t >= 1:
                            gate(t - 1)
                    gate(TILES)

                @block.tensor
                def _(pe):
                    def fill(key, parts):
                        n = TRN[key]
                        if n >= 2:
                            pe.wait_ge(s_tre, n - 1)
                        for i, (col, src) in enumerate(parts):
                            r, w = src.shape[0], src.shape[-1]
                            last = nc.tensor.transpose(bank[n % 2][0:w, col:col + r], src, c("ident", r)[:, 0:r])
                        last.then_inc(s_trf, 1)

                    pe.wait_ge(s_const, 16)
                    pe.wait_ge(s_silu, 1)
                    fill(("c", 0, 0), [(16 * i, cnat[:, i * P:(i + 1) * P]) for i in range(DC)])
                    pe.wait_ge(s_tril, 2)
                    for j in range(2):
                        fill(("sp", 0, j), [(P * i, wsp[:, 4 * j + i, :]) for i in range(4)])
                    fill(("spbd", 0, 0), [(NS * i, wsbd[:, i, :]) for i in range(AH)])
                    pe.wait_ge(s_tre, 1)
                    for n in range(12):
                        pe.wait_ge(s_ada[n % 2], 32 * (n // 2 + 1))
                        if n >= 2:
                            pe.wait_ge(s_modn, n - 1)
                        for i in range(DC):
                            last = nc.tensor.matmul(bank[2 + n % 2][0:1 + SEQS, :], cT[:, i, :], ada_ring[n % 2][:, i, :],
                                                    start=(i == 0), stop=(i == DC - 1))
                        last.then_inc(s_adamm, 1)
                    pe.wait_ge(s_modn, 12)

                    def h_steps(t):
                        r = rows(t)
                        pe.wait_ge(s_h, t + 1)
                        for j in range(2):
                            fill(("h", t, j), [(P * i, x_nat[0:r, t % 2, (4 * j + i) * P:(4 * j + i + 1) * P]) for i in range(4)])

                    h_steps(0)
                    for kind, t, i in STEPS:
                        r = rows(t) if t <= TILES else 0
                        if kind == "h":
                            h_steps(t)
                        elif kind == "group":
                            n = 5 * t + i
                            _, n0, w = GROUPS[i]
                            if t == 0:
                                pe.wait_ge(s_win[i], 16)
                            if i == 0:
                                pe.wait_ge(s_tre, TRN[("h", t, 1)] + 1)
                            if n >= 3:
                                pe.wait_ge(s_ev, n - 2)
                            for k in range(DC):
                                last = nc.tensor.matmul(bank[2 + n % 3][0:r, 0:w], hT[:, t % 2, k, 0:r], w_sb[:, k, n0:n0 + w],
                                                        start=(k == 0), stop=(k == DC - 1))
                            last.then_inc(s_mm, 1)
                        elif kind == "post":
                            pe.wait_ge(s_rot, t + 1)
                            ix = idx_nat[0:r, t % 2, :]
                            fill(("post", t, 0), [(0, k_nat[0:r, t % 2, 0:P]), (P, k_nat[0:r, t % 2, P:2 * P]), (2 * P, ix[:, 256:320])])
                            fill(("post", t, 1), [(P * h, ix[:, h * HD:(h + 1) * HD]) for h in range(IH)])
                        elif kind == "score":
                            keys = (t + 1) * P
                            m = IH * (t - IDX0) + i
                            if i == 0:
                                pe.wait_ge(s_tre, TRN[("post", t, 1)] + 1)
                            if m >= 1:
                                pe.wait_ge(s_acc, m)
                            for b in range((keys + 511) // 512):
                                w = min(512, keys - 512 * b)
                                last = nc.tensor.matmul(bank[5 + b][:, 0:w], qiT[:, i, :], kiT[:, 512 * b:512 * b + w],
                                                        start=True, stop=True)
                            last.then_inc(s_idxp, 1)
                        elif kind == "mix":
                            pe.wait_ge(s_ln, t + 1)
                            if t >= 1:
                                pe.wait_ge(s_spe, t)
                            for h in range(AH):
                                w = wspT[:, h, :] if t < TILES else wsbdT[:, h, :]
                                last = nc.tensor.matmul(bank[7][0:r, h * HD:(h + 1) * HD], w, vg[0:r, t % 2, h * HD:(h + 1) * HD],
                                                        start=True, stop=True)
                            last.then_inc(s_spm, 1)
                        elif kind == "aT":
                            pe.wait_ge(s_am, t + 1)
                            fill(("aT", t, 0), [(P * j, u[0:r, t % 2, j * P:(j + 1) * P]) for j in range(4)])

                @block.scalar
                def _(act):
                    s = nc.scalar

                    def empty(key, parts):
                        n = TRN[key]
                        act.wait_ge(s_trf, n + 1)
                        for dst, src in parts:
                            last = s.activation(dst, src(bank[n % 2]), ACT.Copy)
                        last.then_inc(s_tre, 1)

                    act.wait_ge(s_c, 32)
                    s.activation(cnat, cnat, ACT.Silu).then_inc(s_silu, 1)
                    act.wait_ge(s_trf, 1)
                    s.activation(cT[:, :, :], bank[0][:, 0:16 * DC].rearrange("p (c n) -> p c n", n=16)[:, :, 0:1 + SEQS], ACT.Copy).then_inc(s_tre, 1)
                    for j in range(2):
                        empty(("sp", 0, j), [(wspT[:, 4 * j:4 * j + 4, :], lambda b: b[:, :].rearrange("p (h t) -> p h t", h=4))])
                    empty(("spbd", 0, 0), [(wsbdT[:, :, :], lambda b: b[0:NS, 0:AH * NS].rearrange("p (h t) -> p h t", h=AH))])

                    def h_steps(t):
                        r = rows(t)
                        if t >= 2:
                            act.wait_ge(s_mm, 5 * (t - 1))
                        for j in range(2):
                            empty(("h", t, j), [(hT[:, t % 2, 4 * j:4 * j + 4, 0:r],
                                                 lambda b: b[:, :].rearrange("p (i r) -> p i r", i=4)[:, :, 0:r])])

                    act.wait_ge(s_trf, TRN[("spbd", 0, 0)] + 1)
                    h_steps(0)
                    for kind, t, i in STEPS:
                        r = rows(t) if t <= TILES else 0
                        if kind == "h":
                            h_steps(t)
                        elif kind == "group":
                            n = 5 * t + i
                            name, n0, w = GROUPS[i]
                            act.wait_ge(s_mm, n + 1)
                            src = bank[2 + n % 3][0:r, 0:w]
                            if name == "idx":
                                if t >= 2:
                                    act.wait_ge(s_trf, TRN[("post", t - 2, 1)] + 1)
                                    act.wait_ge(s_st[t % 2], 32 * (t // 2))
                                last = s.activation(idx_nat[0:r, t % 2, :], src, ACT.Copy)
                            elif name == "q":
                                last = s.activation(q_nat[0:r, t, :], src, ACT.Copy)
                            elif name == "kv":
                                s.activation(k_nat[0:r, t % 2, :], src[:, 0:256], ACT.Copy)
                                last = s.activation(v_nat[0:r, t, :], src[:, 256:512], ACT.Copy)
                            elif name == "au":
                                if t >= 2:
                                    act.wait_ge(s_trf, TRN[("aT", t - 2, 0)] + 1)
                                last = s.activation(u[0:r, t % 2, :], src, ACT.Gelu_apprx_tanh)
                            else:
                                if t >= 2:
                                    act.wait_ge(s_spm, t - 1)
                                last = s.activation(vg[0:r, t % 2, :], src, ACT.Gelu_apprx_tanh)
                            last.then_inc(s_ev, 1)
                        elif kind == "post":
                            tok = slice(t * P, t * P + r)
                            empty(("post", t, 0), [(kT[:, :, tok], lambda b: b[:, 0:2 * P].rearrange("p (j r) -> p j r", j=2)[:, :, 0:r]),
                                                   (kiT[:, tok], lambda b: b[0:HD, 2 * P:2 * P + r])])
                            if IDX0 < t < TILES:
                                act.wait_ge(s_idxp, IH * (t - IDX0))
                            dst = qiT[:, :, :] if t < TILES else qi_s[:, :, :]
                            empty(("post", t, 1), [(dst, lambda b: b[0:HD, :].rearrange("p (h r) -> p h r", h=IH)[:, :, 0:r])])
                        elif kind == "score":
                            keys = (t + 1) * P
                            m = IH * (t - IDX0) + i
                            act.wait_ge(s_idxp, m + 1)
                            for b in range((keys + 511) // 512):
                                w = min(512, keys - 512 * b)
                                last = s.activation(bank[5 + b][:, 0:w], bank[5 + b][:, 0:w], ACT.Relu)
                            last.then_inc(s_relu, 1)
                        elif kind == "mix":
                            act.wait_ge(s_spm, t + 1)
                            if t >= 1:
                                act.wait_ge(s_am, t)
                            s.activation(spat[0:r, :], bank[7][0:r, :], ACT.Copy).then_inc(s_spe, 1)
                        elif kind == "aT":
                            empty(("aT", t, 0), [(mixa[:, :, t * P:t * P + r],
                                                  lambda b: b[:, :].rearrange("p (j r) -> p j r", j=4)[:, :, 0:r])])

                @block.vector
                def _(dve):
                    v = nc.vector
                    count = [0]

                    def then(ins):
                        count[0] += 1
                        ins.then_inc(dvec, 1)
                        dve.wait_ge(dvec, count[0])

                    for n in range(12):
                        dve.wait_ge(s_adamm, n + 1)
                        if n >= 2:
                            dve.wait_ge(s_modst[n % 2], 16 * (n // 2))
                        v.scalar_tensor_tensor(out=modn[:, n % 2, :], in0=bank[2 + n % 2][0:1 + SEQS, :],
                                               scalar=1.0 if CH[n] in (2, 3, 8, 9) else 0.0, in1=bada[:, n % 2, :],
                                               op0=ALU.add, op1=ALU.add).then_inc(s_modn, 1)
                    dve.wait_ge(s_const, 16)
                    v.memset(bias[:, 0:bias_at[IDX0]], 0.0).then_inc(dvec, 1)
                    count[0] += 1
                    dve.wait_ge(dvec, count[0])
                    for t in range(IDX0):
                        then(v.tensor_scalar(bias[:, bias_at[t] + t * P:bias_at[t] + (t + 1) * P], c("later"), NEG_MASK, None, ALU.mult))
                    for t in range(IDX0, TILES):
                        keys = (t + 1) * P
                        score = bias[:, bias_at[t]:bias_at[t] + keys]
                        for i in range(IH):
                            m = IH * (t - IDX0) + i
                            dve.wait_ge(s_relu, m + 1)
                            w = w_i[:, t, i:i + 1]
                            rl = banks56[:, 0:keys]
                            if i == 0:
                                v.tensor_scalar(score, rl, w, None, ALU.mult).then_inc(s_acc, 1)
                            else:
                                v.scalar_tensor_tensor(out=score, in0=rl, scalar=w, in1=score,
                                                       op0=ALU.mult, op1=ALU.add).then_inc(s_acc, 1)
                            dve.wait_ge(s_acc, m + 1)
                        diag = score[:, t * P:(t + 1) * P]
                        then(v.scalar_tensor_tensor(out=diag, in0=c("later"), scalar=NEG_INADM, in1=diag, op0=ALU.mult, op1=ALU.add))
                        for _ in range(TOPK_P // 8):
                            then(v.max(out=top8[:, :], in_=score))
                            then(v.match_replace(out=score, in_to_replace=top8[:, :], in_values=score, imm_value=NEG_TAKEN))
                        then(v.tensor_scalar(score, score, NEG_TAKEN, NEG_MASK, ALU.not_equal, ALU.mult))

        with ExitStack() as ctx:
            qz = sb(ctx, "qz", [P, 2, QH, P])
            qzT = sb(ctx, "qzT", [P, 2, QH, P])
            prob = sb(ctx, "prob", [P, 3, SEQ])
            pT = sb(ctx, "pT", [P, 2, TILES, P])
            o_nat = sb(ctx, "o_nat", [P, 2, QH * HD])
            mx = sb(ctx, "mx", [P, TILES * QH])
            nmx = sb(ctx, "nmx", [P, TILES * QH])
            den = sb(ctx, "den", [P, TILES * QH])
            rden = sb(ctx, "rden", [P, TILES * QH])
            zero = sb(ctx, "zero", [P, D])
            b_zero = sem(ctx, "b_zero")
            b_fill = sem(ctx, "b_fill")
            b_z = sem(ctx, "b_z")
            b_qz = sem(ctx, "b_qz")
            b_trf = sem(ctx, "b_trf")
            b_tre = [sem(ctx, f"b_tre{i}") for i in range(2)]
            b_s = sem(ctx, "b_s")
            b_add = sem(ctx, "b_add")
            b_nmx = sem(ctx, "b_nmx")
            b_exp = sem(ctx, "b_exp")
            b_pv = sem(ctx, "b_pv")
            b_rd = sem(ctx, "b_rd")
            b_o = sem(ctx, "b_o")
            ITEMS = [(t, h) for t in range(TILES) for h in range(QH)]
            ORDER = [("q", 0), ("S", 0), ("S", 1)]
            for m, (t, h) in enumerate(ITEMS):
                if h == 4 and t + 1 < TILES:
                    ORDER.append(("q", t + 1))
                if m + 2 < len(ITEMS):
                    ORDER.append(("S", m + 2))
                ORDER.append(("pT", m))
                if m >= 1:
                    ORDER.append(("pv", m - 1))
                if h == 3 and t >= 1:
                    ORDER.append(("oT", t - 1))
            ORDER += [("pv", len(ITEMS) - 1), ("oT", TILES - 1)]
            BTR = []
            for kind, m in ORDER:
                if kind == "q":
                    BTR += [("q", m, 0), ("q", m, 1)]
                elif kind == "oT":
                    BTR.append(("oT", m, 0))
                elif kind == "pT":
                    BTR += [("pT", m, i) for i in range(1 + ITEMS[m][0] // 4)]
            BTRN = {k: n for n, k in enumerate(BTR)}

            with nc.Block() as block:
                @block.sync
                def _(sp):
                    sp.wait_ge(b_zero, 1)
                    with sp.Fori(NE, SLOTS) as i:
                        sp.dma_start(ys_dram.rearrange("(e p) n -> e p n", p=P)[bass.ds(i, 1), :, :].rearrange("e p n -> p (e n)"),
                                     zero[:, :]).then_inc(b_fill, 16)
                    sp.wait_ge(b_fill, 16 * MAXEXTRA)

                @block.gpsimd
                def _(pool):
                    g = nc.gpsimd
                    g.memset(zero[:, :], 0.0).then_inc(b_zero, 1)
                    g.memset(qz[:, :, :, :], 0.0).then_inc(b_z, 1)
                    pool.wait_ge(b_z, 1)
                    for t in range(TILES):
                        if t >= 2:
                            pool.wait_ge(b_trf, BTRN[("q", t - 2, 1)] + 1)
                        dst = qz[:, t % 2, :, :].rearrange("p (j b i) w -> p j b i w", j=2, b=2)
                        src = q_nat[:, t, :].rearrange("p (j b i w) -> p j b i w", j=2, b=2, i=2)
                        for b in range(2):
                            g.tensor_copy(dst[:, :, b, :, b * HD:(b + 1) * HD], src[:, :, b, :, :]).then_inc(b_qz, 1)

                @block.tensor
                def _(pe):
                    def fill(key, parts):
                        n = BTRN[key]
                        if n >= 2:
                            pe.wait_ge(b_tre[n % 2], n // 2)
                        for i, src in enumerate(parts):
                            last = nc.tensor.transpose(bank[n % 2][:, i * P:(i + 1) * P], src, c("ident"))
                        last.then_inc(b_trf, 1)

                    for kind, m in ORDER:
                        t, h = ITEMS[m] if kind in ("S", "pT", "pv") else (m, 0)
                        if kind == "q":
                            pe.wait_ge(b_qz, 2 * (t + 1))
                            for i in range(2):
                                fill(("q", t, i), [qz[:, t % 2, 4 * i + k, :] for k in range(4)])
                        elif kind == "S":
                            if h == 0:
                                n = BTRN[("q", t, 1)]
                                pe.wait_ge(b_tre[n % 2], n // 2 + 1)
                                pe.wait_ge(b_tre[1 - n % 2], (n - 1) // 2 + 1)
                            if m >= 2:
                                pe.wait_ge(b_add, m - 1)
                            keys = (t + 1) * P
                            for b in range((keys + 511) // 512):
                                w = min(512, keys - 512 * b)
                                last = nc.tensor.matmul(bank[2 + 2 * (m % 2) + b][:, 0:w], qzT[:, t % 2, h, :],
                                                        kT[:, h // 4, 512 * b:512 * b + w], start=True, stop=True)
                            last.then_inc(b_s, 1)
                        elif kind == "pT":
                            pe.wait_ge(b_exp, m + 1)
                            for i in range(1 + t // 4):
                                fill(("pT", m, i), [prob[:, m % 3, k * P:(k + 1) * P] for k in range(4 * i, min(4 * i + 4, t + 1))])
                        elif kind == "pv":
                            n = BTRN[("pT", m, t // 4)]
                            pe.wait_ge(b_tre[n % 2], n // 2 + 1)
                            if t >= 4:
                                pe.wait_ge(b_tre[1 - n % 2], (n - 1) // 2 + 1)
                            if h == 0 and t >= 2:
                                pe.wait_ge(b_o, t - 1)
                            kv = h // 2
                            for k in range(t + 1):
                                last = nc.tensor.matmul(bank[6 + t % 2][:, h * HD:(h + 1) * HD], pT[:, m % 2, k, :],
                                                        v_nat[:, k, kv * HD:(kv + 1) * HD], start=(k == 0), stop=(k == t))
                            last.then_inc(b_pv, 1)
                        else:
                            pe.wait_ge(b_o, t + 1)
                            fill(("oT", t, 0), [o_nat[:, t % 2, k * P:(k + 1) * P] for k in range(4)])

                @block.scalar
                def _(act):
                    s = nc.scalar

                    def empty(key, dst, w):
                        n = BTRN[key]
                        act.wait_ge(b_trf, n + 1)
                        s.activation(dst, bank[n % 2][:, 0:w], ACT.Copy).then_inc(b_tre[n % 2], 1)

                    for kind, m in ORDER:
                        if kind == "q":
                            if m >= 2:
                                act.wait_ge(b_s, QH * (m - 1))
                            for i in range(2):
                                empty(("q", m, i), qzT[:, m % 2, 4 * i:4 * i + 4, :], 512)
                        elif kind == "oT":
                            empty(("oT", m, 0), q_nat[:, m, :], 512)
                        elif kind == "pT":
                            t, h = ITEMS[m]
                            keys = (t + 1) * P
                            act.wait_ge(b_nmx, m + 1)
                            s.activation(prob[:, m % 3, 0:keys], prob[:, m % 3, 0:keys], ACT.Exp, bias=nmx[:, m:m + 1],
                                         scale=HD ** -0.5, accum_out=den[:, m:m + 1]).then_inc(b_exp, 1)
                            if m >= 2:
                                act.wait_ge(b_pv, m - 1)
                            if m >= 1:
                                t1 = ITEMS[m - 1][0]
                            w = min(512, keys)
                            empty(("pT", m, 0), pT[:, m % 2, 0:w // P, :], w)

                @block.vector
                def _(dve):
                    v = nc.vector
                    for m in range(len(ITEMS) + 1):
                        if m < len(ITEMS):
                            t, h = ITEMS[m]
                            keys = (t + 1) * P
                            dve.wait_ge(b_s, m + 1)
                            if m >= 3:
                                t3 = ITEMS[m - 3][0]
                                dve.wait_ge(b_trf, BTRN[("pT", m - 3, t3 // 4)] + 1)
                            src = psum[:, 512 * (2 + 2 * (m % 2)):512 * (2 + 2 * (m % 2)) + keys]
                            v.tensor_tensor_reduce(out=prob[:, m % 3, 0:keys], in0=src, in1=bias[:, bias_at[t]:bias_at[t] + keys],
                                                   scale=1.0, scalar=NEG_TAKEN, op0=ALU.add, op1=ALU.max,
                                                   accum_out=mx[:, m:m + 1]).then_inc(b_add, 1)
                            dve.wait_ge(b_add, m + 1)
                            v.tensor_scalar(nmx[:, m:m + 1], mx[:, m:m + 1], -HD ** -0.5, None, ALU.mult).then_inc(b_nmx, 1)
                        if m >= 1:
                            t, h = ITEMS[m - 1]
                            if t >= 4:
                                n = BTRN[("pT", m - 1, 1)]
                                dve.wait_ge(b_trf, n + 1)
                                if m >= 3:
                                    dve.wait_ge(b_pv, m - 2)
                                w = (t + 1) * P - 512
                                v.tensor_copy(pT[:, (m - 1) % 2, 4:4 + w // P, :], bank[n % 2][:, 0:w]).then_inc(b_tre[n % 2], 1)
                            if h == QH - 1:
                                e = slice(t * QH, (t + 1) * QH)
                                dve.wait_ge(b_exp, m)
                                v.reciprocal(rden[:, e], den[:, e]).then_inc(b_rd, 1)
                                dve.wait_ge(b_rd, t + 1)
                                dve.wait_ge(b_pv, m)
                                if t >= 2:
                                    dve.wait_ge(b_trf, BTRN[("oT", t - 2, 0)] + 1)
                                v.tensor_tensor(o_nat[:, t % 2, :].rearrange("p (h d) -> p h d", h=QH),
                                                bank[6 + t % 2].rearrange("p (h d) -> p h d", h=QH),
                                                rden[:, e].unsqueeze(2).to_broadcast([P, QH, HD]), ALU.mult).then_inc(b_o, 1)

        L = PAST + DSEQ
        with ExitStack() as ctx:
            pt = sb(ctx, "pt", [1, SEQS * NPG], I32)
            ki_pg = sb(ctx, "ki_pg", [P, SEQS * NPG, HD])
            k_pg = sb(ctx, "k_pg", [P, SEQS * NPG, KVH * HD])
            v_pg = sb(ctx, "v_pg", [P, SEQS * NPG, KVH * HD])
            qzs = sb(ctx, "qzs", [NS, QH, P])
            qzsT = sb(ctx, "qzsT", [P, QH, NS])
            qsel = sb(ctx, "qsel", [P, 2, SEQS, P])
            isel = sb(ctx, "isel", [HD, SEQS, P])
            kipT = sb(ctx, "kipT", [HD, 2, PAST])
            kpT = sb(ctx, "kpT", [P, 2, 2, PAST])
            wrow = sb(ctx, "wrow", [P, 1])
            relw = sb(ctx, "relw", [P, L])
            sc = sb(ctx, "sc", [P, L])
            top = sb(ctx, "top", [P, 8])
            pr = sb(ctx, "pr", [P, 2, L])
            pn = sb(ctx, "pn", [P, 2, NS])
            prT = sb(ctx, "prT", [P, 2, NPG, P])
            pnT = sb(ctx, "pnT", [NS, 2, P])
            st = sb(ctx, "st", [P, 2, 4])
            c_pt = sem(ctx, "c_pt")
            c_pg = [sem(ctx, f"c_pg{i}") for i in range(3)]
            c_qz = sem(ctx, "c_qz")
            c_sel = sem(ctx, "c_sel")
            c_trf = sem(ctx, "c_trf")
            c_tre = sem(ctx, "c_tre")
            c_qk = sem(ctx, "c_qk")
            c_w = sem(ctx, "c_w")
            c_sum = sem(ctx, "c_sum")
            c_dve = sem(ctx, "c_dve")
            c_nmx = sem(ctx, "c_nmx")
            c_exp = sem(ctx, "c_exp")
            c_pn = sem(ctx, "c_pn")
            c_o = sem(ctx, "c_o")
            c_out = sem(ctx, "c_out")
            CTR = [("q", 0, 0)] + [(k, s, j) for s in range(SEQS) for k, j in (("ki", 0), ("k", 0), ("k", 1))]
            CTR += [x for j in range(2) for x in (("p", j, 0), ("pn", j, 0))]
            CTRN = {k: n for n, k in enumerate(CTR)}

            with nc.Block() as block:
                @block.sync
                def _(sp):
                    sp.dma_start(pt[:, :], a["page_table"].rearrange("b n -> (b n)").unsqueeze(0)).then_inc(c_pt, 16)
                    sp.wait_ge(c_pt, 16)
                    with sp.Fori(0, SEQS * NPG) as i:
                        page = sp.value_load(pt[0:1, bass.ds(i, 1)], min_val=0, max_val=a["cache_k"].shape[1] - 1)
                        sp.dma_start(ki_pg[:, bass.ds(i, 1), :], a["cache_kidx"][0, bass.ds(page, 1), :, :].rearrange("n p d -> p n d")).then_inc(c_pg[0], 16)
                        sp.dma_start(k_pg[:, bass.ds(i, 1), :], a["cache_k"][0, bass.ds(page, 1), :, :, :].rearrange("n p h d -> p n (h d)")).then_inc(c_pg[1], 16)
                        sp.dma_start(v_pg[:, bass.ds(i, 1), :], a["cache_v"][0, bass.ds(page, 1), :, :, :].rearrange("n p h d -> p n (h d)")).then_inc(c_pg[2], 16)

                @block.gpsimd
                def _(pool):
                    g = nc.gpsimd
                    g.memset(qzs[:, :, :], 0.0).then_inc(c_qz, 1)
                    pool.wait_ge(c_qz, 1)
                    dst = qzs[:, :, :].rearrange("p (j b i) w -> p j b i w", j=2, b=2)
                    src = q_nat[0:NS, TILES, :].rearrange("p (j b i w) -> p j b i w", j=2, b=2, i=2)
                    for b in range(2):
                        g.tensor_copy(dst[:, :, b, :, b * HD:(b + 1) * HD], src[:, :, b, :, :]).then_inc(c_qz, 1)

                @block.tensor
                def _(pe):
                    def fill(key, parts, w=P):
                        n = CTRN[key]
                        if n >= 2:
                            pe.wait_ge(c_tre, n - 1)
                        for i, src in enumerate(parts):
                            r, m = src.shape
                            last = nc.tensor.transpose(bank[n % 2][0:m, i * r:(i + 1) * r], src, c("ident", r)[:, 0:r])
                        last.then_inc(c_trf, 1)

                    pe.wait_ge(c_qz, 3)
                    fill(("q", 0, 0), [qzs[:, h, :] for h in range(QH)])
                    for i in range(3):
                        pe.wait_ge(c_pg[i], 16 * SEQS * NPG)
                    for s in range(SEQS + 1):
                        if s < SEQS:
                            fill(("ki", s, 0), [ki_pg[:, NPG * s + k, :] for k in range(NPG)])
                            for j in range(2):
                                fill(("k", s, j), [k_pg[:, NPG * s + k, j * P:(j + 1) * P] for k in range(NPG)])
                        if s >= 1:
                            r = s - 1
                            pe.wait_ge(c_tre, CTRN[("k", r, 1)] + 1)
                            if r == 0:
                                pe.wait_ge(c_sel, IH + QH)
                            new = slice(SEQ + r * DSEQ, SEQ + (r + 1) * DSEQ)
                            f = dict(start=(r == 0), stop=(r == SEQS - 1))
                            nc.tensor.matmul(bank[2][:, :], isel[:, r, :], kipT[:, r % 2, :], **f)
                            nc.tensor.matmul(bank[3][:, 0:DSEQ], isel[:, r, :], kiT[:, new], **f)
                            for j in range(2):
                                nc.tensor.matmul(bank[4 + j][:, :], qsel[:, j, r, :], kpT[:, r % 2, j, :], **f)
                                last = nc.tensor.matmul(bank[6 + j][:, 0:DSEQ], qsel[:, j, r, :], kT[:, j, new], **f)
                            last.then_inc(c_qk, 1)
                    pe.wait_ge(c_w, 2)
                    nc.tensor.matmul(bank[2][:, :], c("sametok"), relw[:, 0:PAST], start=True, stop=True)
                    nc.tensor.matmul(bank[3][:, 0:DSEQ], c("sametok"), relw[:, PAST:L], start=True, stop=True).then_inc(c_sum, 1)
                    for j in range(2):
                        pe.wait_ge(c_pn, j + 1)
                        fill(("p", j, 0), [pr[:, j, k * P:(k + 1) * P] for k in range(NPG)])
                        fill(("pn", j, 0), [pn[:, j, :]])
                    for j in range(2):
                        out = bank[2 + j][:, 0:P]
                        pe.wait_ge(c_tre, CTRN[("pn", j, 0)] + 1)
                        nc.tensor.matmul(out, v_nat[0:NS, TILES, j * P:(j + 1) * P], pnT[:, j, :], start=True, stop=False, skip_group_check=True)
                        o3 = out.rearrange("p (h n) -> p h n", h=4)
                        for s in range(SEQS):
                            for k in range(NPG):
                                m = prT[:, j, k, :].rearrange("p (h n) -> p h n", h=4)[:, :, s * DSEQ:(s + 1) * DSEQ]
                                last = nc.tensor.matmul(o3[:, :, s * DSEQ:(s + 1) * DSEQ], v_pg[:, NPG * s + k, j * P:(j + 1) * P], m,
                                                        start=False, stop=(s == SEQS - 1 and k == NPG - 1), skip_group_check=True)
                        last.then_inc(c_o, 1)

                @block.scalar
                def _(act):
                    s_ = nc.scalar

                    def empty(key, dst, src):
                        n = CTRN[key]
                        act.wait_ge(c_trf, n + 1)
                        s_.activation(dst, src(bank[n % 2]), ACT.Copy).then_inc(c_tre, 1)

                    empty(("q", 0, 0), qzsT[:, :, :], lambda b: b[:, 0:QH * NS].rearrange("p (h n) -> p h n", h=QH))
                    for s in range(SEQS):
                        if s >= 2:
                            act.wait_ge(c_qk, s - 1)
                        empty(("ki", s, 0), kipT[:, s % 2, :], lambda b: b[0:HD, :])
                        for j in range(2):
                            empty(("k", s, j), kpT[:, s % 2, j, :], lambda b: b)
                    for j in range(2):
                        act.wait_ge(c_nmx, j + 1)
                        s_.activation(pr[:, j, :], pr[:, j, :], ACT.Exp, bias=st[:, j, 1:2], scale=HD ** -0.5,
                                      accum_out=st[:, j, 2:3]).then_inc(c_exp, 1)
                    for j in range(2):
                        empty(("p", j, 0), prT[:, j, :, :], lambda b: b.rearrange("p (k n) -> p k n", k=NPG))
                        empty(("pn", j, 0), pnT[:, j, :], lambda b: b[0:NS, 0:P])
                    for j in range(2):
                        act.wait_ge(c_o, j + 1)
                        for hh in range(4):
                            src, dst = HD * (hh // 2), HD * (hh % 2)
                            chunk = 2 * j + hh // 2
                            s_.activation(q_nat[dst:dst + HD, TILES, chunk * P:chunk * P + NS],
                                          bank[2 + j][src:src + HD, hh * NS:(hh + 1) * NS], ACT.Copy).then_inc(c_out, 1)

                @block.vector
                def _(dve):
                    v = nc.vector
                    count = [0]

                    def then(ins):
                        count[0] += 1
                        ins.then_inc(c_dve, 1)
                        dve.wait_ge(c_dve, count[0])

                    def cols(name, r):
                        return c(name, r).rearrange("p (s n) -> p s n", s=SEQS)

                    for h in range(IH):
                        v.tensor_tensor(isel[:, :, h * NS:(h + 1) * NS], qi_s[:, h:h + 1, :].to_broadcast([HD, SEQS, NS]),
                                        cols("seqcol", HD), ALU.mult).then_inc(c_sel, 1)
                        v.tensor_copy(wrow[h * NS:(h + 1) * NS, :], w_i[0:NS, TILES, h:h + 1]).then_inc(c_dve, 1)
                        count[0] += 1
                    dve.wait_ge(c_tre, 1)
                    for h in range(QH):
                        v.tensor_tensor(qsel[:, h // 4, :, (h % 4) * NS:(h % 4 + 1) * NS], qzsT[:, h:h + 1, :].to_broadcast([P, SEQS, NS]),
                                        cols("seqcol", P), ALU.mult).then_inc(c_sel, 1)
                    dve.wait_ge(c_dve, count[0])
                    dve.wait_ge(c_qk, SEQS)
                    v.tensor_scalar(relw[:, 0:PAST], bank[2], 0.0, wrow[:, 0:1], ALU.max, ALU.mult).then_inc(c_w, 1)
                    v.tensor_scalar(relw[:, PAST:L], bank[3][:, 0:DSEQ], 0.0, wrow[:, 0:1], ALU.max, ALU.mult).then_inc(c_w, 1)
                    dve.wait_ge(c_sum, 1)
                    v.tensor_copy(sc[:, 0:PAST], bank[2])
                    then(v.tensor_tensor(sc[:, PAST:L], bank[3][:, 0:DSEQ], c("newneg"), ALU.add))
                    for _ in range(TOPK_S // 8):
                        then(v.max(out=top[:, :], in_=sc[:, :]))
                        then(v.match_replace(out=sc[:, :], in_to_replace=top[:, :], in_values=sc[:, :], imm_value=NEG_TAKEN))
                    then(v.max(out=top[:, :], in_=sc[:, :]))
                    then(v.memset(top[:, TOPK_S % 8:8], NEG_TAKEN))
                    then(v.match_replace(out=sc[:, :], in_to_replace=top[:, :], in_values=sc[:, :], imm_value=NEG_TAKEN))
                    then(v.tensor_scalar(sc[:, :], sc[:, :], NEG_TAKEN, NEG_MASK, ALU.not_equal, ALU.mult))
                    for j in range(2):
                        v.tensor_tensor(pr[:, j, 0:PAST], bank[4 + j], sc[:, 0:PAST], ALU.add)
                        then(v.tensor_tensor(pr[:, j, PAST:L], bank[6 + j][:, 0:DSEQ], sc[:, PAST:L], ALU.add))
                        then(v.tensor_reduce(st[:, j, 0:1], pr[:, j, :], AX, ALU.max))
                        v.tensor_scalar(st[:, j, 1:2], st[:, j, 0:1], -HD ** -0.5, None, ALU.mult).then_inc(c_nmx, 1)
                    for j in range(2):
                        dve.wait_ge(c_exp, j + 1)
                        then(v.reciprocal(st[:, j, 3:4], st[:, j, 2:3]))
                        then(v.tensor_scalar(pr[:, j, :], pr[:, j, :], st[:, j, 3:4], None, ALU.mult))
                        v.tensor_tensor(pn[:, j, :].rearrange("p (s n) -> p s n", s=SEQS),
                                        pr[:, j:j + 1, PAST:L].to_broadcast([P, SEQS, DSEQ]),
                                        c("own").unsqueeze(2).to_broadcast([P, SEQS, DSEQ]), ALU.mult).then_inc(c_pn, 1)

        TA = TILES + 1
        with ExitStack() as ctx:
            w_o = sb(ctx, "w_o", [P, DC, D])
            xr = sb(ctx, "xr", [P, 2, D])
            z = sb(ctx, "z", [P, 2, D])
            h2 = sb(ctx, "h2", [P, 2, D])
            h2T = sb(ctx, "h2T", [P, DC, P])
            vec = {n: sb(ctx, n, [P, D]) for n in ("gate1", "shift2", "scale2", "ln1_g", "ln1_b")}
            rw = sb(ctx, "rw", [P, DC, NG + NE])
            stat = sb(ctx, "stat", [P, 2, 2, 6])
            mv = sb(ctx, "mv", [P, 2, 2])
            d_w = sem(ctx, "d_w")
            d_v = sem(ctx, "d_v")
            d_x = [sem(ctx, f"d_xr{i}") for i in range(2)]
            d_mm = sem(ctx, "d_mm")
            d_z = sem(ctx, "d_z")
            d_dve = sem(ctx, "d_dve")
            d_mv = sem(ctx, "d_mv")
            d_pool = sem(ctx, "d_pool")
            d_rs = sem(ctx, "d_rs")
            d_x1 = sem(ctx, "d_x1")
            d_h2 = sem(ctx, "d_h2")
            d_st = [sem(ctx, f"d_st{i}") for i in range(2)]
            d_trf = sem(ctx, "d_trf")
            d_tre = sem(ctx, "d_tre")
            d_lg = sem(ctx, "d_lg")
            d_lge = sem(ctx, "d_lge")
            x1_tile = [x1_dram[t * P:t * P + rows(t), :] for t in range(TA)]
            h2_tile = [h2_dram[t * P:t * P + rows(t), :] for t in range(TA)]

            with nc.Block() as block:
                @block.sync
                def _(sp):
                    w = a["w_out"][0].rearrange("(c p) n -> p c n", p=P)
                    for i in range(2):
                        sp.dma_start(xr[:, i, :], x_tile[i]).then_inc(d_x[i], 16)
                        sp.dma_start(w_o[:, :, i * 512:(i + 1) * 512], w[:, :, i * 512:(i + 1) * 512]).then_inc(d_w, 16)
                    mods = (("gate1", 2), ("shift2", 3), ("scale2", 4))
                    for n, j in mods:
                        sp.dma_start(vec[n][:, :], mod_dram[0, j * D:(j + 1) * D].partition_broadcast(P)).then_inc(d_v, 16)
                    for n in ("ln1_g", "ln1_b"):
                        sp.dma_start(vec[n][:, :], a[n][0].partition_broadcast(P)).then_inc(d_v, 16)
                    sp.dma_start(rw[:, :, 0:NG], a["w_group_router"][0].rearrange("(c p) g -> p c g", p=P)).then_inc(d_v, 16)
                    sp.dma_start(rw[:, :, NG:NG + NE], a["w_expert_router"][0].rearrange("(c p) g e -> p c (g e)", p=P)).then_inc(d_v, 16)
                    for t in range(TA):
                        r = rows(t)
                        sp.wait_ge(d_x1, t + 1)
                        sp.dma_start(x1_tile[t], z[0:r, t % 2, :]).then_inc(d_st[t % 2], 16)
                        if t + 2 < TA:
                            sp.dma_start(xr[0:rows(t + 2), t % 2, :], x_tile[t + 2]).then_inc(d_x[t % 2], 16)
                        sp.wait_ge(d_h2, t + 1)
                        sp.dma_start(h2_tile[t], h2[0:r, t % 2, :]).then_inc(d_st[t % 2], 16)
                        if t == TILES - 1:
                            for n, j in mods:
                                for i in range(SEQS):
                                    sp.dma_start(vec[n][i * DSEQ:(i + 1) * DSEQ, :],
                                                 mod_dram[1 + i, j * D:(j + 1) * D].partition_broadcast(DSEQ)).then_inc(d_v, 16)
                    sp.wait_ge(d_st[0], 32 * 5)
                    sp.wait_ge(d_st[1], 32 * 4)

                @block.tensor
                def _(pe):
                    pe.wait_ge(d_w, 32)
                    for t in range(TA + 1):
                        if t < TA:
                            r = rows(t)
                            if t >= 2:
                                pe.wait_ge(d_z, t - 1)
                            for half in range(2):
                                for k in range(DC):
                                    lhs = mixa[:, k, t * P:t * P + r] if k < 4 else q_nat[:, t, (k - 4) * P:(k - 4) * P + r]
                                    last = nc.tensor.matmul(bank[2 + 2 * (t % 2) + half][0:r, :], lhs, w_o[:, k, half * 512:(half + 1) * 512],
                                                            start=(k == 0), stop=(k == DC - 1))
                            last.then_inc(d_mm, 1)
                        if t >= 1:
                            m, r = t - 1, rows(t - 1)
                            pe.wait_ge(d_h2, m + 1)
                            for j in range(2):
                                if m >= 1:
                                    pe.wait_ge(d_tre, 2 * m - 1 + j)
                                for k in range(4):
                                    last = nc.tensor.transpose(bank[j][:, k * P:k * P + r], h2[0:r, m % 2, (4 * j + k) * P:(4 * j + k + 1) * P],
                                                               c("ident", r)[:, 0:r])
                                last.then_inc(d_trf, 1)
                            pe.wait_ge(d_tre, 2 * m + 2)
                            pe.wait_ge(d_v, 16 * 7)
                            if m >= 1:
                                pe.wait_ge(d_lge, m)
                            for k in range(DC):
                                last = nc.tensor.matmul(bank[6][0:r, 0:NG + NE], h2T[:, k, 0:r], rw[:, k, :], start=(k == 0), stop=(k == DC - 1))
                            last.then_inc(d_lg, 1)

                @block.scalar
                def _(act):
                    for t in range(TA):
                        r = rows(t)
                        for j in range(2):
                            act.wait_ge(d_trf, 2 * t + j + 1)
                            if t >= 1:
                                act.wait_ge(d_lg, t)
                            nc.scalar.activation(h2T[:, 4 * j:4 * j + 4, 0:r], bank[j].rearrange("p (k r) -> p k r", k=4)[:, :, 0:r],
                                                 ACT.Copy).then_inc(d_tre, 1)
                        act.wait_ge(d_lg, t + 1)
                        nc.scalar.activation(logit[0:r, t, :], bank[6][0:r, 0:NG + NE], ACT.Copy).then_inc(d_lge, 1)

                @block.gpsimd
                def _(pool):
                    g = nc.gpsimd
                    for t in range(TA):
                        r, b = rows(t), t % 2
                        pool.wait_ge(d_mv, t + 1)
                        g.tensor_scalar(mv[0:r, b, 1:2], mv[0:r, b, 1:2], EPS, None, ALU.add).then_inc(d_pool, 1)
                        pool.wait_ge(d_pool, 2 * t + 1)
                        g.tensor_tensor(mv[0:r, b, 1:2], mv[0:r, b, 1:2], c("minushalf", r)[:, 0:1], ALU.pow).then_inc(d_rs, 1)
                        pool.wait_ge(d_x1, t + 1)
                        if t >= 2:
                            pool.wait_ge(d_st[b], 32 * (t // 2))
                            pool.wait_ge(d_trf, 2 * (t - 1))
                        if t == TILES:
                            pool.wait_ge(d_v, 16 * (7 + 3 * SEQS))
                        g.tensor_tensor(h2[0:r, b, :], z[0:r, b, :], vec["scale2"][0:r, :], ALU.mult).then_inc(d_pool, 1)
                        pool.wait_ge(d_pool, 2 * t + 2)
                        g.tensor_tensor(h2[0:r, b, :], h2[0:r, b, :], vec["shift2"][0:r, :], ALU.add).then_inc(d_h2, 1)

                @block.vector
                def _(dve):
                    v = nc.vector
                    count = [0]

                    def then(ins):
                        count[0] += 1
                        ins.then_inc(d_dve, 1)
                        dve.wait_ge(d_dve, count[0])

                    v.memset(logit[:, TILES, :], 0.0).then_inc(d_dve, 1)
                    count[0] += 1
                    for t in range(TA):
                        r, b = rows(t), t % 2
                        zz = z[0:r, b, :]
                        dve.wait_ge(d_mm, t + 1)
                        dve.wait_ge(d_v, 16 * 7 if t < TILES else 16 * (7 + 3 * SEQS))
                        if t >= 2:
                            dve.wait_ge(d_st[b], 32 * (t // 2))
                            dve.wait_ge(d_h2, t - 1)
                        v.tensor_tensor(zz, psum[0:r, 512 * (2 + 2 * b):512 * (4 + 2 * b)], vec["gate1"][0:r, :], ALU.mult).then_inc(d_z, 1)
                        dve.wait_ge(d_z, t + 1)
                        dve.wait_ge(d_x[b], 16 * (t // 2 + 1))
                        then(v.scalar_tensor_tensor(out=zz, in0=xr[0:r, b, :], scalar=ALPHA, in1=zz, op0=ALU.mult, op1=ALU.add))
                        v.bn_stats(stat[0:r, b, 0, :], z[0:r, b, 0:512])
                        then(v.bn_stats(stat[0:r, b, 1, :], z[0:r, b, 512:1024]))
                        v.bn_aggr(mv[0:r, b, :], stat[0:r, b, :, :]).then_inc(d_mv, 1)
                        dve.wait_ge(d_rs, t + 1)
                        then(v.tensor_scalar(zz, zz, mv[0:r, b, 0:1], mv[0:r, b, 1:2], ALU.subtract, ALU.mult))
                        then(v.tensor_tensor(zz, zz, vec["ln1_g"][0:r, :], ALU.mult))
                        v.tensor_tensor(zz, zz, vec["ln1_b"][0:r, :], ALU.add).then_inc(d_x1, 1)

        tail.close()
        vec2 = {n: sb(keep, "v2" + n, [P, D]) for n in ("gate2", "ln2_g", "ln2_b")}
        g_v = sem(keep, "g_v")
        weight = sb(keep, "weight", [P, 2, TILES + 1])
        slot = sb(keep, "slot", [P, 2, TILES + 1], I32)
        tokens = sb(keep, "tokens", [P, SLOTS], I32)
        exi = sb(keep, "exi", [1, MAXEXTRA + 1], I32)


        with ExitStack() as ctx:
            R = [P, TA]
            t3 = lambda n, k: sb(ctx, n, [P, TA, k])
            gmax, gsum, gw = sb(ctx, "gmax", R), sb(ctx, "gsum", R), sb(ctx, "gw", R)
            gs, ohg, gpri = t3("gs", NG), t3("ohg", NG), t3("gpri", NG)
            prod = sb(ctx, "prod", [P, TA, NG, EPG])
            el = t3("el", EPG)
            pri = t3("pri", EPG)
            oh = [t3("oh1", EPG), t3("oh2", EPG)]
            m12 = sb(ctx, "m12", [P, 2, TA])
            pm = sb(ctx, "pm", R)
            ex = sb(ctx, "ex", R)
            mk = [sb(ctx, f"mk{k}", [P, TA, NE]) for k in range(2)]
            msum = sb(ctx, "msum", [P, TA, NE])
            base = sb(ctx, "base", [P, TA + 1, NE])
            rank = sb(ctx, "rank", [P, TA, NE])
            over = sb(ctx, "over", [P, NE, 8])
            extra = sb(ctx, "extra", [P, NE])
            incl = sb(ctx, "incl", [P, NE])
            ebase = sb(ctx, "ebase", [P, NE])
            rr, eb, ei, jj, j0 = (sb(ctx, n, R) for n in ("rr", "eb", "ei", "jj", "j0"))
            ge = sb(ctx, "ge", [P, TA, 8])
            tile_of = sb(ctx, "tile_of", [P, 2, TA])
            pos_of = sb(ctx, "pos_of", [P, 2, TA])
            slot_f = sb(ctx, "slot_f", [P, 2, TA])
            onepos = sb(ctx, "onepos", [P, 2 * TA, P])
            onetile = sb(ctx, "onetile", [P, 2 * TA, SLOTS])
            below = sb(ctx, "below", [1, MAXEXTRA, NE])
            exf = sb(ctx, "exf", [1, MAXEXTRA + 1])
            prod2 = prod[:, :, :, :].rearrange("p t g e -> p t (g e)")
            e_dve = sem(ctx, "e_dve")
            e_exp = sem(ctx, "e_exp")
            e_m = sem(ctx, "e_m")
            e_pre = sem(ctx, "e_pre")
            e_one = sem(ctx, "e_one")
            e_list = sem(ctx, "e_list")
            DV = {}

            with nc.Block() as block:
                @block.vector
                def _(dve):
                    v = nc.vector
                    count = [0]

                    def then(ins):
                        count[0] += 1
                        ins.then_inc(e_dve, 1)
                        dve.wait_ge(e_dve, count[0])

                    def bc(x, *shape):
                        return x.to_broadcast(list(shape))

                    def one_hot(dst, x, top, n, priority, scratch):
                        then(v.tensor_tensor(scratch, x, bc(top.unsqueeze(2), P, TA, n), ALU.is_equal))
                        then(v.tensor_tensor(scratch, scratch, bc(priority.unsqueeze(1), P, TA, n), ALU.mult))
                        then(v.tensor_reduce(pm[:, :], scratch, AX, ALU.max))
                        then(v.tensor_tensor(dst, scratch, bc(pm[:, :].unsqueeze(2), P, TA, n), ALU.is_equal))

                    G = logit[:, :, 0:NG]
                    E = logit[:, :, NG:NG + NE].rearrange("p t (g e) -> p t g e", g=NG)
                    first = c("first")
                    then(v.tensor_reduce(gmax[:, :], G, AX, ALU.max))
                    then(v.tensor_tensor(gs[:, :, :], G, bc(gmax[:, :].unsqueeze(2), P, TA, NG), ALU.subtract))
                    DV["gs"] = count[0]
                    one_hot(ohg[:, :, :], G, gmax[:, :], NG, first[:, 0:NG], gpri[:, :, :])
                    then(v.tensor_tensor(prod[:, :, :, :], E, bc(ohg[:, :, :].unsqueeze(3), P, TA, NG, EPG), ALU.mult))
                    then(v.tensor_reduce(el[:, :, :], prod[:, :, :, :].rearrange("p t g e -> p t e g"), AX, ALU.add))
                    for k in range(2):
                        then(v.tensor_reduce(m12[:, k, :], el[:, :, :], AX, ALU.max))
                        one_hot(oh[k][:, :, :], el[:, :, :], m12[:, k, :], EPG, first, pri[:, :, :])
                        if k == 0:
                            then(v.scalar_tensor_tensor(out=el[:, :, :], in0=oh[0][:, :, :], scalar=NEG_INADM, in1=el[:, :, :],
                                                        op0=ALU.mult, op1=ALU.add))
                    then(v.tensor_tensor(ex[:, :], m12[:, 1, :], m12[:, 0, :], ALU.subtract))
                    DV["ex"] = count[0]
                    for k in range(2):
                        then(v.tensor_tensor(mk[k][:, :, :].rearrange("p t (g e) -> p t g e", g=NG),
                                             bc(oh[k][:, :, :].unsqueeze(2), P, TA, NG, EPG), bc(ohg[:, :, :].unsqueeze(3), P, TA, NG, EPG), ALU.mult))
                        then(v.tensor_tensor(mk[k][:, :, :], mk[k][:, :, :], bc(c("valid").unsqueeze(2), P, TA, NE), ALU.mult))
                    v.tensor_tensor(msum[:, :, :], mk[0][:, :, :], mk[1][:, :, :], ALU.add).then_inc(e_m, 1)
                    dve.wait_ge(e_exp, 2)
                    then(v.tensor_reduce(gsum[:, :], gs[:, :, :], AX, ALU.add))
                    then(v.reciprocal(gw[:, :], gsum[:, :]))
                    then(v.tensor_scalar(pm[:, :], ex[:, :], 1.0, None, ALU.add))
                    then(v.reciprocal(pm[:, :], pm[:, :]))
                    then(v.tensor_tensor(weight[:, 0, :], gw[:, :], pm[:, :], ALU.mult))
                    then(v.tensor_tensor(weight[:, 1, :], weight[:, 0, :], ex[:, :], ALU.mult))
                    dve.wait_ge(e_pre, 2)
                    then(v.memset(base[:, 0, :], 0.0))
                    for t in range(TA):
                        then(v.tensor_tensor(base[:, t + 1, :], base[:, t, :], bank[3][:, t * NE:(t + 1) * NE], ALU.add))
                    then(v.tensor_tensor(rank[:, :, :], bank[2][:, 0:TA * NE].rearrange("p (t e) -> p t e", e=NE), base[:, 0:TA, :], ALU.add))
                    then(v.tensor_tensor(over[:, :, :], bc(base[:, TA, :].unsqueeze(2), P, NE, 8), bc(c("steps").unsqueeze(1), P, NE, 8), ALU.is_gt))
                    then(v.tensor_reduce(extra[:, :], over[:, :, :], AX, ALU.add))
                    then(v.tensor_tensor_scan(incl[:, :], c("ones")[:, 0:NE], extra[:, :], 0.0, ALU.mult, ALU.add))
                    then(v.tensor_tensor(ebase[:, :], incl[:, :], extra[:, :], ALU.subtract))
                    then(v.tensor_scalar(ebase[:, :], ebase[:, :], float(NE - 1), None, ALU.add))
                    for k in range(2):
                        for dst, src in ((rr, rank[:, :, :]), (eb, bc(ebase[:, :].unsqueeze(1), P, TA, NE)),
                                         (ei, bc(c("iota")[:, 0:NE].unsqueeze(1), P, TA, NE))):
                            then(v.tensor_tensor(prod2, mk[k][:, :, :], src, ALU.mult))
                            then(v.tensor_reduce(dst[:, :], prod2, AX, ALU.add))
                        then(v.tensor_tensor(ge[:, :, :], bc(rr[:, :].unsqueeze(2), P, TA, 8), bc(c("steps").unsqueeze(1), P, TA, 8), ALU.is_ge))
                        then(v.tensor_reduce(jj[:, :], ge[:, :, :], AX, ALU.add))
                        then(v.tensor_scalar(j0[:, :], jj[:, :], 0.0, None, ALU.is_equal))
                        then(v.tensor_tensor(eb[:, :], eb[:, :], jj[:, :], ALU.add))
                        then(v.tensor_tensor(ei[:, :], ei[:, :], eb[:, :], ALU.subtract))
                        then(v.tensor_tensor(ei[:, :], ei[:, :], j0[:, :], ALU.mult))
                        then(v.tensor_tensor(tile_of[:, k, :], ei[:, :], eb[:, :], ALU.add))
                        then(v.scalar_tensor_tensor(out=pos_of[:, k, :], in0=jj[:, :], scalar=-float(P), in1=rr[:, :], op0=ALU.mult, op1=ALU.add))
                        then(v.scalar_tensor_tensor(out=slot_f[:, k, :], in0=tile_of[:, k, :], scalar=float(P), in1=pos_of[:, k, :],
                                                    op0=ALU.mult, op1=ALU.add))
                    then(v.tensor_copy(slot[:, :, :], slot_f[:, :, :]))
                    for k in range(2):
                        for t in range(TA):
                            v.tensor_scalar(onepos[:, k * TA + t, :], c("iota"), pos_of[:, k, t:t + 1], None, ALU.is_equal).then_inc(e_one, 1)
                            v.tensor_scalar(onetile[:, k * TA + t, :], c("iota")[:, 0:SLOTS], tile_of[:, k, t:t + 1], c("token")[:, t:t + 1],
                                            ALU.is_equal, ALU.mult).then_inc(e_one, 1)
                    then(v.tensor_tensor(below[:, :, :], bc(incl[0:1, :].unsqueeze(1), 1, MAXEXTRA, NE),
                                         bc(c("iota", 1)[:, 0:MAXEXTRA].unsqueeze(2), 1, MAXEXTRA, NE), ALU.is_le))
                    then(v.tensor_reduce(exf[:, 0:MAXEXTRA], below[:, :, :], AX, ALU.add))
                    then(v.tensor_scalar(exf[:, 0:MAXEXTRA], exf[:, 0:MAXEXTRA], float(NE - 1), None, ALU.min))
                    then(v.tensor_copy(exf[:, MAXEXTRA:MAXEXTRA + 1], incl[0:1, NE - 1:NE]))
                    then(v.tensor_copy(exi[:, :], exf[:, :]))
                    dve.wait_ge(e_list, 1)
                    then(v.tensor_copy(tokens[:, :], bank[4][:, 0:SLOTS]))

                @block.scalar
                def _(act):
                    act.wait_ge(e_dve, DV["gs"])
                    nc.scalar.activation(gs[:, :, :], gs[:, :, :], ACT.Exp).then_inc(e_exp, 1)
                    act.wait_ge(e_dve, DV["ex"])
                    nc.scalar.activation(ex[:, :], ex[:, :], ACT.Exp).then_inc(e_exp, 1)

                @block.tensor
                def _(pe):
                    pe.wait_ge(e_m, 1)
                    m = msum[:, :, :].rearrange("p t e -> p (t e)")
                    nc.tensor.matmul(bank[2][:, 0:TA * NE], c("before"), m, start=True, stop=True).then_inc(e_pre, 1)
                    nc.tensor.matmul(bank[3][:, 0:TA * NE], c("ones"), m, start=True, stop=True).then_inc(e_pre, 1)
                    for n in range(2 * TA):
                        pe.wait_ge(e_one, 2 * n + 2)
                        last = nc.tensor.matmul(bank[4][:, 0:SLOTS], onepos[:, n, :], onetile[:, n, :], start=(n == 0), stop=(n == 2 * TA - 1))
                    last.then_inc(e_list, 1)

        with ExitStack() as ctx:
            wg = sb(ctx, "wg", [P, 2, DC, DE])
            wu = sb(ctx, "wu", [P, 2, DC, DE])
            wd = sb(ctx, "wd", [P, 2, DE // P, D])
            xg = sb(ctx, "xg", [P, 2, D])
            xgT = sb(ctx, "xgT", [P, 2, DC, P])
            silu = sb(ctx, "silu", [P, 2, DE])
            hid = sb(ctx, "hid", [P, 2, DE])
            hidT = sb(ctx, "hidT", [P, 2, DE // P, P])
            yy = sb(ctx, "yy", [P, 2, D])
            KD = DE // P
            wg_v = a["w_gate"][0].rearrange("e (p k) f -> e p k f", k=DC)
            wu_v = a["w_up"][0].rearrange("e (p k) f -> e p k f", k=DC)
            wd_v = a["w_down"][0].rearrange("e (p k) n -> e p k n", k=KD)
            ys_v = ys_dram.rearrange("(e p) n -> e p n", p=P)
            f_w = {n: [sem(ctx, f"f_w{n}{i}") for i in range(2)] for n in "gud"}
            f_x = [sem(ctx, f"f_x{i}") for i in range(2)]
            f_tx = sem(ctx, "f_tx")
            f_xa = sem(ctx, "f_xa")
            f_xv = sem(ctx, "f_xv")
            f_g = sem(ctx, "f_g")
            f_u = sem(ctx, "f_u")
            f_silu = sem(ctx, "f_silu")
            f_hid = sem(ctx, "f_hid")
            f_th = sem(ctx, "f_th")
            f_ht = sem(ctx, "f_ht")
            f_d = sem(ctx, "f_d")
            f_ya = sem(ctx, "f_ya")
            f_yv = sem(ctx, "f_yv")
            f_st = [sem(ctx, f"f_st{i}") for i in range(2)]

            def steps(eng, step):
                step(0, 0, 0)
                step(1, 1, 0)
                step(2, 0, 1)
                with eng.Fori(1, (NE - 2) // 2) as i:
                    step(2 * i + 1, 1, i)
                    step(2 * i + 2, 0, i + 1)
                step(NE - 1, 1, (NE - 2) // 2)

            def at_least(e, n):
                return e >= n if type(e) is int else n <= 1

            def gate_mm(b, base_sem=None):
                for k in range(DC):
                    last = nc.tensor.matmul(bank[2], xgT[:, b, k, :], wg[:, b, k, :], start=(k == 0), stop=(k == DC - 1))
                return last

            def up_mm(b):
                for k in range(DC):
                    last = nc.tensor.matmul(bank[3], xgT[:, b, k, :], wu[:, b, k, :], start=(k == 0), stop=(k == DC - 1))
                return last

            def down_mm(b):
                for half in range(2):
                    for k in range(KD):
                        last = nc.tensor.matmul(bank[4 + half], hidT[:, b, k, :], wd[:, b, k, half * 512:(half + 1) * 512],
                                                start=(k == 0), stop=(k == KD - 1))
                return last

            def x_transposes(b):
                x = xg[:, b, :].rearrange("p (m k) -> p k m", k=DC)
                for k in range(DC):
                    last = nc.tensor.transpose(bank[1 if k < 4 else 7][:, (k % 4) * P:(k % 4 + 1) * P], x[:, k, :], c("ident"))
                return last

            def hid_transposes(b):
                h = hid[:, b, :].rearrange("p (m k) -> p k m", k=KD)
                for k in range(KD):
                    last = nc.tensor.transpose(bank[0][:, k * P:(k + 1) * P], h[:, k, :], c("ident"))
                return last

            with nc.Block() as block:
                @block.sync
                def _(sp):
                    def load(e, b):
                        return [(wg[:, b, :, :], wg_v[e], f_w["g"][b]), (wu[:, b, :, :], wu_v[e], f_w["u"][b]),
                                (wd[:, b, :, :], wd_v[e], f_w["d"][b])]

                    for e in range(2):
                        for dst, src, s in load(e, e):
                            sp.dma_start(dst, src).then_inc(s, 16)
                    with sp.Fori(0, (NE - 2) // 2) as i:
                        for b in range(2):
                            e = 2 * i + b
                            for n, w, used in (("g", wg, f_g), ("u", wu, f_u), ("d", wd, f_d)):
                                src = {"g": wg_v, "u": wu_v, "d": wd_v}[n][bass.ds(e + 2, 1), :, :, :].rearrange("e p k n -> p (e k) n")
                                sp.wait_ge(used, e + 1)
                                sp.dma_start(w[:, b, :, :], src).then_inc(f_w[n][b], 16)

                @block.gpsimd
                def _(pool):
                    for e in range(NE):
                        if e >= 2:
                            pool.wait_ge(f_tx, e - 1)
                        nc.gpsimd.indirect_dma_start(out=xg[:, e % 2, :], out_offset=None, in_=h2_dram[:, :],
                                                     in_offset=bass.IndirectOffsetOnAxis(ap=tokens[:, e:e + 1].bitcast(U32), axis=0)).then_inc(f_x[e % 2], 16)

                @block.tensor
                def _(pe):
                    pe.wait_ge(f_x[0], 16)
                    x_transposes(0).then_inc(f_tx, 1)

                    def step(e, b, half):
                        pe.wait_ge(f_xa, e + 1)
                        pe.wait_ge(f_xv, e + 1)
                        pe.wait_ge(f_w["g"][b], 16 * (half + 1))
                        if at_least(e, 1):
                            pe.wait_ge(f_silu, e)
                        gate_mm(b).then_inc(f_g, 1)
                        if at_least(e, 1):
                            pe.wait_ge(f_hid, e)
                            hid_transposes(1 - b).then_inc(f_th, 1)
                        pe.wait_ge(f_w["u"][b], 16 * (half + 1))
                        up_mm(b).then_inc(f_u, 1)
                        if not (type(e) is int and e == NE - 1):
                            pe.wait_ge(f_x[1 - b], 16 * (half + 1 + b))
                            x_transposes(1 - b).then_inc(f_tx, 1)
                        if at_least(e, 1):
                            down(e, 1 - b, half + (b - 1))

                    def down(e, b, half):
                        pe.wait_ge(f_ht, e)
                        pe.wait_ge(f_w["d"][b], 16 * (half + 1))
                        if type(e) is not int or e >= 2:
                            pe.wait_ge(f_ya, e - 1)
                            pe.wait_ge(f_yv, e - 1)
                        down_mm(b).then_inc(f_d, 1)

                    steps(pe, step)
                    pe.wait_ge(f_hid, NE)
                    hid_transposes(1).then_inc(f_th, 1)
                    down(NE, 1, NE // 2 - 1)

                @block.scalar
                def _(act):
                    s = nc.scalar

                    def x_part(e, b):
                        act.wait_ge(f_tx, e + 1)
                        s.activation(xgT[:, b, 0:4, :], bank[1], ACT.Copy).then_inc(f_xa, 1)

                    def hid_part(e, b):
                        act.wait_ge(f_th, e)
                        s.activation(hidT[:, b, :, :], bank[0], ACT.Copy).then_inc(f_ht, 1)

                    def y_part(e, b, half):
                        act.wait_ge(f_d, e)
                        if type(e) is not int or e >= 3:
                            act.wait_ge(f_st[b], 16 * half)
                        s.activation(yy[:, b, 0:512], bank[4], ACT.Copy).then_inc(f_ya, 1)
                        act.wait_ge(f_ya, e)
                        act.wait_ge(f_yv, e)
                        dst = ys_v[e - 1] if type(e) is int else ys_v[bass.ds(e - 1, 1), :, :].rearrange("e p n -> p (e n)")
                        act.dma_start(dst, yy[:, b, :]).then_inc(f_st[b], 16)

                    x_part(0, 0)

                    def step(e, b, half):
                        act.wait_ge(f_g, e + 1)
                        s.activation(silu[:, b, :], bank[2], ACT.Silu).then_inc(f_silu, 1)
                        if at_least(e, 1):
                            hid_part(e, 1 - b)
                        if not (type(e) is int and e == NE - 1):
                            x_part(e + 1, 1 - b)
                        if at_least(e, 1):
                            y_part(e, 1 - b, half + b - 1)

                    steps(act, step)
                    hid_part(NE, 1)
                    y_part(NE, 1, NE // 2 - 1)
                    for b in range(2):
                        act.wait_ge(f_st[b], 16 * NE // 2)

                @block.vector
                def _(dve):
                    v = nc.vector

                    def x_part(e, b):
                        dve.wait_ge(f_tx, e + 1)
                        v.tensor_copy(xgT[:, b, 4:8, :], bank[7]).then_inc(f_xv, 1)

                    def y_part(e, b, half):
                        dve.wait_ge(f_d, e)
                        if type(e) is not int or e >= 3:
                            dve.wait_ge(f_st[b], 16 * half)
                        v.tensor_copy(yy[:, b, 512:1024], bank[5]).then_inc(f_yv, 1)

                    x_part(0, 0)

                    def step(e, b, half):
                        dve.wait_ge(f_silu, e + 1)
                        dve.wait_ge(f_u, e + 1)
                        v.tensor_tensor(hid[:, b, :], silu[:, b, :], bank[3], ALU.mult).then_inc(f_hid, 1)
                        if not (type(e) is int and e == NE - 1):
                            x_part(e + 1, 1 - b)
                        if at_least(e, 1):
                            y_part(e, 1 - b, half + b - 1)

                    steps(dve, step)
                    y_part(NE, 1, NE // 2 - 1)

            x_w = sem(ctx, "x_w")
            x_x = sem(ctx, "x_x")
            x_tx = sem(ctx, "x_tx")
            x_xe = sem(ctx, "x_xe")
            x_gu = sem(ctx, "x_gu")
            x_silu = sem(ctx, "x_silu")
            x_hid = sem(ctx, "x_hid")
            x_th = sem(ctx, "x_th")
            x_ht = sem(ctx, "x_ht")
            x_d = sem(ctx, "x_d")
            x_y = sem(ctx, "x_y")
            x_st = sem(ctx, "x_st")

            def extras(eng, body):
                n = eng.value_load(exi[0:1, MAXEXTRA:MAXEXTRA + 1], min_val=0, max_val=MAXEXTRA)
                with eng.Fori(0, MAXEXTRA) as i:
                    with eng.If(n > i):
                        body(i)
                return n

            with nc.Block() as block:
                @block.sync
                def _(sp):
                    def body(i):
                        e = sp.value_load(exi[0:1, bass.ds(i, 1)], min_val=0, max_val=NE - 1)
                        for w, view in ((wg, wg_v), (wu, wu_v), (wd, wd_v)):
                            sp.dma_start(w[:, 0, :, :], view[bass.ds(e, 1), :, :, :].rearrange("e p k n -> p (e k) n")).then_inc(x_w, 16)
                        sp.wait_ge(x_y, 2 * (i + 1))
                        sp.dma_start(ys_v[bass.ds(i + NE, 1), :, :].rearrange("e p n -> p (e n)"), yy[:, 0, :]).then_inc(x_st, 16)
                    sp.dma_start(vec2["gate2"][:, :], mod_dram[0, 5 * D:6 * D].partition_broadcast(P)).then_inc(x_st, 16)
                    n = extras(sp, body)
                    sp.wait_ge(x_st, 16 * (n + 1))
                    for n in ("ln2_g", "ln2_b"):
                        sp.dma_start(vec2[n][:, :], a[n][0].partition_broadcast(P)).then_inc(g_v, 16)

                @block.gpsimd
                def _(pool):
                    n = pool.value_load(exi[0:1, MAXEXTRA:MAXEXTRA + 1], min_val=0, max_val=MAXEXTRA)
                    for i in range(MAXEXTRA):
                        with pool.If(n > i):
                            if i >= 1:
                                pool.wait_ge(x_tx, i)
                            nc.gpsimd.indirect_dma_start(out=xg[:, 0, :], out_offset=None, in_=h2_dram[:, :],
                                                         in_offset=bass.IndirectOffsetOnAxis(ap=tokens[:, NE + i:NE + i + 1].bitcast(U32), axis=0)).then_inc(x_x, 16)

                @block.tensor
                def _(pe):
                    def body(i):
                        pe.wait_ge(x_x, 16 * (i + 1))
                        x_transposes(0).then_inc(x_tx, 1)
                        pe.wait_ge(x_xe, 2 * (i + 1))
                        pe.wait_ge(x_w, 48 * (i + 1))
                        gate_mm(0)
                        up_mm(0).then_inc(x_gu, 1)
                        pe.wait_ge(x_hid, i + 1)
                        hid_transposes(0).then_inc(x_th, 1)
                        pe.wait_ge(x_ht, i + 1)
                        down_mm(0).then_inc(x_d, 1)
                    extras(pe, body)

                @block.scalar
                def _(act):
                    def body(i):
                        act.wait_ge(x_tx, i + 1)
                        nc.scalar.activation(xgT[:, 0, 0:4, :], bank[1], ACT.Copy).then_inc(x_xe, 1)
                        act.wait_ge(x_gu, i + 1)
                        nc.scalar.activation(silu[:, 0, :], bank[2], ACT.Silu).then_inc(x_silu, 1)
                        act.wait_ge(x_th, i + 1)
                        nc.scalar.activation(hidT[:, 0, :, :], bank[0], ACT.Copy).then_inc(x_ht, 1)
                        act.wait_ge(x_st, 16 * (i + 1))
                        act.wait_ge(x_d, i + 1)
                        nc.scalar.activation(yy[:, 0, 0:512], bank[4], ACT.Copy).then_inc(x_y, 1)
                    extras(act, body)

                @block.vector
                def _(dve):
                    def body(i):
                        dve.wait_ge(x_tx, i + 1)
                        nc.vector.tensor_copy(xgT[:, 0, 4:8, :], bank[7]).then_inc(x_xe, 1)
                        dve.wait_ge(x_silu, i + 1)
                        nc.vector.tensor_tensor(hid[:, 0, :], silu[:, 0, :], bank[3], ALU.mult).then_inc(x_hid, 1)
                        dve.wait_ge(x_st, 16 * (i + 1))
                        dve.wait_ge(x_d, i + 1)
                        nc.vector.tensor_copy(yy[:, 0, 512:1024], bank[5]).then_inc(x_y, 1)
                    extras(dve, body)

        with ExitStack() as ctx:
            y1 = sb(ctx, "y1", [P, 3, D])
            y2 = sb(ctx, "y2", [P, 3, D])
            x1 = sb(ctx, "x1", [P, 3, D])
            stat = sb(ctx, "stat2", [P, 2, 6])
            mv = sb(ctx, "mv2", [P, 2, 2])
            y_tile = [outs[0][0, t * P:(t + 1) * P, :] for t in range(TILES)] + [outs[1].rearrange("b t d -> (b t) d")]
            g_gv = sem(ctx, "g_gv")
            g_y = [sem(ctx, f"g_y{i}") for i in range(3)]
            g_x = [sem(ctx, f"g_x{i}") for i in range(3)]
            g_dve = sem(ctx, "g_dve")
            g_w1 = sem(ctx, "g_w1")
            g_gated = sem(ctx, "g_gated")
            g_mv = sem(ctx, "g_mv")
            g_pool = sem(ctx, "g_pool")
            g_rs = sem(ctx, "g_rs")
            g_out = sem(ctx, "g_out")
            g_st = [sem(ctx, f"g_st{i}") for i in range(3)]

            with nc.Block() as block:
                @block.sync
                def _(sp):
                    for t in range(3):
                        sp.dma_start(x1[:, t, :], x1_dram[t * P:(t + 1) * P, :]).then_inc(g_x[t], 16)
                    for t in range(TA):
                        r = rows(t)
                        sp.wait_ge(g_out, t + 1)
                        sp.dma_start(y_tile[t], x1[0:r, t % 3, :]).then_inc(g_st[t % 3], 16)
                        if t == TILES - 1:
                            sp.wait_ge(g_gated, TILES)
                            for i in range(SEQS):
                                sp.dma_start(vec2["gate2"][i * DSEQ:(i + 1) * DSEQ, :],
                                             mod_dram[1 + i, 5 * D:6 * D].partition_broadcast(DSEQ)).then_inc(g_gv, 16)
                        if t + 3 < TA:
                            sp.wait_ge(g_st[t % 3], 16 * (t // 3 + 1))
                            r3 = rows(t + 3)
                            sp.dma_start(x1[0:r3, t % 3, :], x1_dram[(t + 3) * P:(t + 3) * P + r3, :]).then_inc(g_x[t % 3], 16)
                    for i in range(3):
                        sp.wait_ge(g_st[i], 16 * 3)

                @block.gpsimd
                def _(pool):
                    g = nc.gpsimd

                    def gather(t):
                        r = rows(t)
                        for k, y in enumerate((y1, y2)):
                            g.indirect_dma_start(out=y[0:r, t % 3, :], out_offset=None, in_=ys_dram[:, :],
                                                 in_offset=bass.IndirectOffsetOnAxis(ap=slot[0:r, k, t:t + 1].bitcast(U32), axis=0)).then_inc(g_y[t % 3], 16)

                    for t in range(3):
                        gather(t)
                    for t in range(TA):
                        r, b = rows(t), t % 2
                        pool.wait_ge(g_mv, t + 1)
                        g.tensor_scalar(mv[0:r, b, 1:2], mv[0:r, b, 1:2], EPS, None, ALU.add).then_inc(g_pool, 1)
                        pool.wait_ge(g_pool, t + 1)
                        g.tensor_tensor(mv[0:r, b, 1:2], mv[0:r, b, 1:2], c("minushalf", r)[:, 0:1], ALU.pow).then_inc(g_rs, 1)
                        if t + 3 < TA:
                            gather(t + 3)

                @block.scalar
                def _(act):
                    for t in range(TA):
                        r, b = rows(t), t % 3
                        act.wait_ge(g_y[b], 32 * (t // 3 + 1))
                        nc.scalar.activation(y1[0:r, b, :], y1[0:r, b, :], ACT.Copy, scale=weight[0:r, 0, t:t + 1]).then_inc(g_w1, 1)

                @block.vector
                def _(dve):
                    v = nc.vector
                    count = [0]

                    def then(ins):
                        count[0] += 1
                        ins.then_inc(g_dve, 1)
                        dve.wait_ge(g_dve, count[0])

                    dve.wait_ge(g_v, 32)
                    for t in range(TA):
                        r, b = rows(t), t % 3
                        f, x, m = y1[0:r, b, :], x1[0:r, b, :], mv[0:r, t % 2, :]
                        dve.wait_ge(g_w1, t + 1)
                        dve.wait_ge(g_y[b], 32 * (t // 3 + 1))
                        then(v.scalar_tensor_tensor(out=f, in0=y2[0:r, b, :], scalar=weight[0:r, 1, t:t + 1], in1=f, op0=ALU.mult, op1=ALU.add))
                        if t == TILES:
                            dve.wait_ge(g_gv, 16 * SEQS)
                        v.tensor_tensor(f, f, vec2["gate2"][0:r, :], ALU.mult).then_inc(g_gated, 1)
                        dve.wait_ge(g_gated, t + 1)
                        dve.wait_ge(g_x[b], 16 * (t // 3 + 1))
                        then(v.scalar_tensor_tensor(out=x, in0=x, scalar=ALPHA, in1=f, op0=ALU.mult, op1=ALU.add))
                        v.bn_stats(stat[0:r, 0, :], x[:, 0:512])
                        then(v.bn_stats(stat[0:r, 1, :], x[:, 512:1024]))
                        v.bn_aggr(m, stat[0:r, :, :]).then_inc(g_mv, 1)
                        dve.wait_ge(g_rs, t + 1)
                        then(v.tensor_scalar(x, x, m[:, 0:1], m[:, 1:2], ALU.subtract, ALU.mult))
                        then(v.tensor_tensor(x, x, vec2["ln2_g"][0:r, :], ALU.mult))
                        v.tensor_tensor(x, x, vec2["ln2_b"][0:r, :], ALU.add).then_inc(g_out, 1)


_INS = ['x_prompt', 'x_sample', 'cache_k', 'cache_v', 'cache_kidx', 'page_table', 'c_prompt', 'c_sample',
        'w_ada', 'b_ada', 'w_in', 'a_ln_g', 'a_ln_b', 'w_spatial', 'b_spatial', 'w_out', 'ln1_g', 'ln1_b',
        'w_group_router', 'w_expert_router', 'w_gate', 'w_up', 'w_down', 'ln2_g', 'ln2_b']
_OUTS = [(1, SEQ, D), (SEQS, DSEQ, D), (1, 1, SEQ, KVH, HD), (1, 1, SEQ, KVH, HD), (1, 1, SEQ, HD),
         (1, SEQS, DSEQ, KVH, HD), (1, SEQS, DSEQ, KVH, HD), (1, SEQS, DSEQ, HD), (1, SEQS, DSEQ, AH, HD)]


def kernel(**inputs):
    import concourse.bacc as _bacc
    from concourse.bass_utils import run_bass_kernel_spmd as _run

    nc = _bacc.Bacc("TRN2", target_bir_lowering=False, num_devices=1)
    arrays, args = {}, {}
    given = {name: np.ascontiguousarray(inputs[name]) for name in _INS}
    given["table"] = constants()[1]
    for name, x in given.items():
        arrays[f"in_{name}_dram"] = x
        args[name] = nc.dram_tensor(f"in_{name}_dram", x.shape, mybir.dt.from_np(x.dtype), kind="ExternalInput").ap()
    outs = [nc.dram_tensor(f"out_{i}_dram", shape, F32, kind="ExternalOutput").ap() for i, shape in enumerate(_OUTS)]
    step_kernel(nc, args, outs)
    r = _run(nc, [arrays], core_ids=[0])
    return tuple(r.results[0][f"out_{i}_dram"] for i in range(len(_OUTS)))
```

```python
from contextlib import ExitStack

import numpy as np
import concourse.bass as bass
from concourse import mybir

F32 = mybir.dt.float32
I32 = mybir.dt.int32
U32 = mybir.dt.uint32
ALU = mybir.AluOpType
ACT = mybir.ActivationFunctionType
AX = mybir.AxisListType.X

P = 128
D = 1024
DC = D // P
SEQ = 1024
SEQS, DSEQ = 8, 4
NS = SEQS * DSEQ
TILES = SEQ // P
TOK = SEQ + NS
HD = 64
AH = 8
QH, KVH, IH = 8, 4, 4
PAST, PAGE = 512, 128
NPG = PAST // PAGE
TOPK_P, TOPK_S = 256, (PAST + DSEQ) // 4
HALF = 8
THETA = 500000.0
NG, EPG = 4, 8
NE = NG * EPG
DE = 512
ALPHA = 2.0 ** 0.25
EPS = 1e-5
NEG_MASK = -1.0e30
NEG_INADM = -3.0e38
NEG_TAKEN = -3.4e38
MAXEXTRA = (2 * TOK) // P
SLOTS = NE + MAXEXTRA

GROUPS = [("idx", 2048, 324), ("q", 1024, 512), ("kv", 1536, 512), ("au", 0, 512), ("av", 512, 512)]


SEARCH = 32
ROUTING = ("before", "ones", "iota", "token", "valid", "steps", "first")
BIG = 3.0e38


def rows(t):
    return P if t < TILES else NS


def constants():
    p = np.arange(P)
    inv = np.float32(THETA) ** (-np.arange(HALF, dtype=np.float32) * np.float32(2.0) / np.float32(2 * HALF))
    pos = np.zeros((P, TILES + 1), np.float32)
    for t in range(TILES):
        pos[:, t] = t * P + p
    pos[:, TILES] = PAST + p % DSEQ
    ang = (pos[:, :, None] * inv[None, None, :]).astype(np.float32)
    own = (p[:, None] % NS // DSEQ == np.arange(SEQS)[None]).astype(np.float32)
    blk = np.zeros((P, NS))
    blk[:NS] = (p[:NS, None] // DSEQ == p[None, :NS] // DSEQ) & (p[:NS, None] >= p[None, :NS])
    later = p[None, :] > p[:, None]
    newer = np.arange(DSEQ)[None] > (p % DSEQ)[:, None]
    c = {
        "ident": np.eye(P),
        "before": p[:, None] < p[None],
        "ones": np.ones((P, P)),
        "sametok": p[:, None] % NS == p[None] % NS,
        "cos": np.cos(ang), "sin": np.sin(ang),
        "later": later,
        "newneg": newer * NEG_INADM,
        "tril": p[:, None] >= p[None],
        "blktril": blk,
        "seqcol": np.broadcast_to((p[None, None, :NS] // DSEQ == np.arange(SEQS)[None, :, None]), (P, SEQS, NS)),
        "own": own,
        "iota": np.broadcast_to(p[None], (P, P)),
        "token": (np.arange(TILES + 1)[None] * P + p[:, None]) * ((np.arange(TILES + 1)[None] < TILES) | (p[:, None] < NS)),
        "valid": np.concatenate([np.ones((P, TILES)), (p < NS)[:, None]], axis=1),
        "steps": np.broadcast_to(P * np.arange(1, 9)[None], (P, 8)),
        "first": np.broadcast_to(8 - np.arange(8)[None], (P, 8)),
        "one": np.ones((P, 1)),
        "minushalf": np.full((P, 16), -0.5),
    }
    c["halvings"] = np.broadcast_to(2.0 ** (1 - np.arange(SEARCH + 1))[None], (P, SEARCH + 1))
    order = [k for k in c if k not in ROUTING] + [k for k in c if k in ROUTING]
    at, parts, n = {}, [], 0
    for k, v in ((k, c[k]) for k in order):
        v = np.ascontiguousarray(v, dtype=np.float32).reshape(P, -1)
        at[k] = (n, v.shape[1])
        n += v.shape[1]
        parts.append(v)
    return at, np.concatenate(parts, axis=1)


def step_kernel(nc, a, outs):
    at, table = constants()
    xs = a["x_sample"].rearrange("b t d -> (b t) d")
    x_tile = [a["x_prompt"][0, t * P:(t + 1) * P, :] for t in range(TILES)] + [xs]
    w_in = a["w_in"][0].rearrange("(c p) n -> p c n", p=P)
    w_ada = a["w_ada"][0].rearrange("(c p) n -> p c n", p=P)
    b_ada = a["b_ada"][0]
    new_k = [outs[2].rearrange("a b t h d -> (a b t) (h d)")[t * P:(t + 1) * P, :] for t in range(TILES)] + \
            [outs[5].rearrange("a b t h d -> (a b t) (h d)")]
    new_v = [outs[3].rearrange("a b t h d -> (a b t) (h d)")[t * P:(t + 1) * P, :] for t in range(TILES)] + \
            [outs[6].rearrange("a b t h d -> (a b t) (h d)")]
    new_kidx = [outs[4].rearrange("a b t d -> (a b t) d")[t * P:(t + 1) * P, :] for t in range(TILES)] + \
               [outs[7].rearrange("a b t d -> (a b t) d")]
    chunk_v = outs[8].rearrange("a b t h d -> (a b t) (h d)")

    mod_dram = nc.dram_tensor("mod_dram", (1 + SEQS, 6 * D), F32).ap()

    x1_dram = nc.dram_tensor("x1_dram", (TOK, D), F32).ap()
    h2_dram = nc.dram_tensor("h2_dram", (TOK, D), F32).ap()
    ys_dram = nc.dram_tensor("ys_dram", (SLOTS * P, D), F32).ap()

    with ExitStack() as keep, ExitStack() as tail:
        def sb(ctx, name, shape, dt=F32):
            return ctx.enter_context(nc.sbuf_tensor(name, shape, dt))

        def sem(ctx, name):
            return ctx.enter_context(nc.semaphore(name))

        psum = keep.enter_context(nc.psum_tensor("psum", [P, 8 * 512], F32))
        bank = [psum[:, 512 * i:512 * (i + 1)] for i in range(8)]
        banks56 = psum[:, 5 * 512:7 * 512]
        early = at[ROUTING[0]][0]
        const = sb(keep, "const", [P, early])
        consts = [const]

        def c(name, r=P):
            n, w = at[name]
            return consts[0][0:r, n:n + w] if n < early else consts[1][0:r, n - early:n - early + w]

        logit = sb(keep, "logit", [P, TILES + 1, NG + NE])

        q_nat = sb(tail, "q_nat", [P, TILES + 1, QH * HD])
        kT = sb(tail, "kT", [P, 2, TOK])
        kiT = sb(tail, "kiT", [HD, TOK])
        v_nat = sb(tail, "v_nat", [P, TILES + 1, KVH * HD])
        mixa = sb(tail, "mixa", [P, 4, TOK])
        bias_at = [P * (t * (t + 1) // 2 - 3) for t in range(TILES)]
        bias = sb(tail, "bias", [P, bias_at[TILES - 1] + P * TILES])
        qi_s = sb(tail, "qi_s", [HD, IH, NS])
        w_i = sb(tail, "w_i", [P, TILES + 1, IH])

        with ExitStack() as ctx:
            w_sb = sb(ctx, "w_sb", [P, DC, 2372])
            ada = q_nat[:, :, :].rearrange("p t n -> p (t n)")[:, 0:4096].rearrange("p (c n) -> p c n", c=DC)
            ada2 = mixa[:, :, :].rearrange("p t n -> p (t n)")[:, 0:4096].rearrange("p (c n) -> p c n", c=DC)
            ada_ring = [ada, ada2]
            x_nat = sb(ctx, "x_nat", [P, 2, D])
            hT = sb(ctx, "hT", [P, 2, DC, P])
            scale1 = sb(ctx, "scale1", [P, D])
            shift1 = sb(ctx, "shift1", [P, D])
            idx_nat = sb(ctx, "idx_nat", [P, 2, 324])
            k_nat = sb(ctx, "k_nat", [P, 2, KVH * HD])
            u = sb(ctx, "u", [P, 2, 512])
            vg = sb(ctx, "vg", [P, 2, 512])
            spat = sb(ctx, "spat", [P, 512])
            tmp = sb(ctx, "tmp", [P, 512])
            rot = tmp[:, 0:4 * QH * HALF].rearrange("p (i n) -> p i n", i=4)
            st8 = sb(ctx, "st8", [P, 3, AH])
            wspT = sb(ctx, "wspT", [P, AH, P])
            wsb4 = sb(ctx, "wsb4", [NS, AH, DSEQ])
            wsbd = tmp[0:NS, 0:AH * NS].rearrange("p (h t) -> p h t", h=AH)
            wsbdT = sb(ctx, "wsbdT", [NS, AH, NS])
            bsp = sb(ctx, "bsp", [P, AH])
            bsp_s = sb(ctx, "bsp_s", [NS, AH])
            aln_g = sb(ctx, "aln_g", [P, 512])
            aln_b = sb(ctx, "aln_b", [P, 512])
            qiT = sb(ctx, "qiT", [HD, IH, P])
            above = sb(ctx, "above", [P, SEQ], mybir.dt.int8)
            near = sb(ctx, "near", [P, SEQ], mybir.dt.int8)
            steps_ = sb(ctx, "steps_", [P, 2, SEARCH + 1])
            low = sb(ctx, "low", [P, 2])
            cand = sb(ctx, "cand", [P, 2])
            under = sb(ctx, "under", [P, 2])
            miss = sb(ctx, "miss", [P, 2])
            nabove = sb(ctx, "nabove", [P, 2])
            cnat = x_nat[0:1 + SEQS, 0, :]
            cT = sb(ctx, "cT", [P, DC, 1 + SEQS])
            modn = u[0:1 + SEQS, :, :]
            bada = vg[0:1 + SEQS, :, :]
            wsp = hT[:, 0, :, :]

            s_const = sem(ctx, "s_const")
            s_c = sem(ctx, "s_c")
            s_silu = sem(ctx, "s_silu")
            s_ada = [sem(ctx, f"s_ada{i}") for i in range(2)]
            s_adamm = sem(ctx, "s_adamm")
            s_modn = sem(ctx, "s_modn")
            s_modst = [sem(ctx, f"s_modst{i}") for i in range(2)]
            s_win = [sem(ctx, f"s_win{g}") for g in range(5)]
            s_bc = sem(ctx, "s_bc")
            s_sp = sem(ctx, "s_sp")
            s_aln = sem(ctx, "s_aln")
            s_tril = sem(ctx, "s_tril")
            s_x = [sem(ctx, f"s_x{i}") for i in range(2)]
            s_h = sem(ctx, "s_h")
            s_trf = sem(ctx, "s_trf")
            s_tre = sem(ctx, "s_tre")
            s_mm = sem(ctx, "s_mm")
            s_ev = sem(ctx, "s_ev")
            s_rot = sem(ctx, "s_rot")
            s_ln = sem(ctx, "s_ln")
            s_idxp = sem(ctx, "s_idxp")
            s_relu = sem(ctx, "s_relu")
            s_acc = sem(ctx, "s_acc")
            s_cand = sem(ctx, "s_cand")
            s_under = sem(ctx, "s_under")
            s_adax = [sem(ctx, f"s_adax{i}") for i in range(2)]
            s_adamm2 = sem(ctx, "s_adamm2")
            s_modn2 = sem(ctx, "s_modn2")
            s_modst2 = [sem(ctx, f"s_modst2{i}") for i in range(2)]
            s_spm = sem(ctx, "s_spm")
            s_spe = sem(ctx, "s_spe")
            s_am = sem(ctx, "s_am")
            s_st = [sem(ctx, f"s_st{i}") for i in range(2)]
            s_stv = sem(ctx, "s_stv")
            dvec = sem(ctx, "dvec")
            poolc = sem(ctx, "poolc")
            IDX0 = 2
            PER_GROUP = 3
            CH = [2, 3, 0, 1, 4, 5, 6, 7, 8, 9, 10, 11]

            TR = [("c", 0, 0)] + [("sp", 0, i) for i in range(2)] + [("spbd", 0, 0)] + [("h", 0, 0), ("h", 0, 1)]
            STEPS = []
            for t in range(TILES + 3):
                if t <= TILES:
                    STEPS.append(("group", t, 0))
                    if t + 1 <= TILES:
                        STEPS.append(("h", t + 1, 0))
                    STEPS.append(("group", t, 1))
                if 1 <= t <= TILES + 1:
                    STEPS.append(("post", t - 1, 0))
                if t <= TILES:
                    STEPS.append(("group", t, 2))
                if 3 <= t <= TILES:
                    STEPS += [("score", t - 1, 0), ("score", t - 1, 1)]
                if 2 <= t:
                    STEPS.append(("aT", t - 2, 0))
                if t <= TILES:
                    STEPS.append(("group", t, 3))
                if 3 <= t <= TILES:
                    STEPS += [("score", t - 1, 2), ("score", t - 1, 3)]
                if t <= TILES:
                    STEPS.append(("group", t, 4))
                if 1 <= t <= TILES + 1:
                    STEPS.append(("mix", t - 1, 0))
            merged, queue, since = [], [], 0
            for x in STEPS:
                if x == ("score", 5, 0) or x == ("score", 7, 0):
                    merged += queue
                    queue = []
                merged.append(x)
                if x[0] == "score" and x[2] == IH - 1 and x[1] % 2 == 1:
                    m = x[1] // 2
                    queue = [("begin", m, 0)] + [("try", m, i) for i in range(SEARCH)] + [("pick", m, 0)]
                elif x[0] == "group":
                    merged += queue[0:PER_GROUP]
                    queue = queue[PER_GROUP:]
            for n in range(4, 12):
                merged.append(("ada", n, 0))
                merged += queue[0:4]
                queue = queue[4:]
            STEPS = merged + queue
            for kind, t, _ in STEPS:
                if kind == "h" or kind == "post":
                    TR += [(kind, t, 0), (kind, t, 1)]
                if kind == "aT":
                    TR.append((kind, t, 0))
            TRN = {k: n for n, k in enumerate(TR)}

            with nc.Block() as block:
                @block.sync
                def _(sp):
                    sp.dma_start(const[:, :], a["table"][:, 0:early]).then_inc(s_const, 16)
                    sp.dma_start(cnat[0:1, :], a["c_prompt"]).then_inc(s_c, 16)
                    sp.dma_start(cnat[1:1 + SEQS, :], a["c_sample"]).then_inc(s_c, 16)

                    def ada_load(n):
                        j = CH[n]
                        if n >= 2:
                            sp.wait_ge(s_adamm, n - 1)
                            sp.wait_ge(s_modn, n - 1)
                        sp.dma_start(ada_ring[n % 2], w_ada[:, :, j * 512:(j + 1) * 512]).then_inc(s_ada[n % 2], 16)
                        sp.dma_start(bada[:, n % 2, :], b_ada[j * 512:(j + 1) * 512].partition_broadcast(1 + SEQS)).then_inc(s_ada[n % 2], 16)

                    def mod_store(n):
                        j = CH[n]
                        sp.wait_ge(s_modn, n + 1)
                        sp.dma_start(mod_dram[:, j * 512:(j + 1) * 512], modn[:, n % 2, :]).then_inc(s_modst[n % 2], 16)

                    def mod_store2(n):
                        j = CH[n]
                        sp.wait_ge(s_modn2, n - 3)
                        sp.dma_start(mod_dram[:, j * 512:(j + 1) * 512], x_nat[0:1 + SEQS, 0, n % 2 * 512:(n % 2 + 1) * 512]).then_inc(s_modst2[n % 2], 16)

                    ada_load(0)
                    ada_load(1)
                    sp.dma_start(wsp, a["w_spatial"][0].rearrange("h t s -> t h s")).then_inc(s_sp, 16)
                    sp.dma_start(bsp[:, :], a["b_spatial"][0].rearrange("h t -> t h"),
                                 allow_slow_non_contiguous=True).then_inc(s_sp, 16)
                    for s in range(SEQS):
                        sp.dma_start(wsb4[s * DSEQ:(s + 1) * DSEQ, :, :],
                                     a["w_spatial"][0, :, 0:DSEQ, 0:DSEQ].rearrange("h t s -> t h s")).then_inc(s_sp, 16)
                        sp.dma_start(bsp_s[s * DSEQ:(s + 1) * DSEQ, :],
                                     a["b_spatial"][0, :, 0:DSEQ].rearrange("h t -> t h"),
                                 allow_slow_non_contiguous=True).then_inc(s_sp, 16)
                    sp.dma_start(aln_g[:, :], a["a_ln_g"][0].rearrange("h d -> (h d)").partition_broadcast(P)).then_inc(s_aln, 16)
                    sp.dma_start(aln_b[:, :], a["a_ln_b"][0].rearrange("h d -> (h d)").partition_broadcast(P)).then_inc(s_aln, 16)
                    for g, (_, n0, w) in enumerate(GROUPS):
                        sp.dma_start(w_sb[:, :, n0:n0 + w], w_in[:, :, n0:n0 + w]).then_inc(s_win[g], 16)
                        if g < 2:
                            ada_load(g + 2)
                            mod_store(g)
                    mod_store(2)
                    mod_store(3)
                    for i in range(2):
                        sp.wait_ge(s_modst[i], 32)
                    sp.dma_start(shift1[:, :], mod_dram[0, 0:D].partition_broadcast(P)).then_inc(s_bc, 16)
                    sp.dma_start(scale1[:, :], mod_dram[0, D:2 * D].partition_broadcast(P)).then_inc(s_bc, 16)
                    sp.wait_ge(s_trf, 1)
                    for t in range(2):
                        sp.dma_start(x_nat[:, t, :], x_tile[t]).then_inc(s_x[t], 16)
                    for t in range(TILES + 1):
                        r = rows(t)
                        if t + 2 <= TILES:
                            sp.wait_ge(s_trf, TRN[("h", t, 1)] + 1)
                            sp.dma_start(x_nat[0:rows(t + 2), t % 2, :], x_tile[t + 2]).then_inc(s_x[t % 2], 16)
                        if t == TILES - 1:
                            sp.wait_ge(s_h, TILES)
                            for i in range(SEQS):
                                sp.dma_start(shift1[i * DSEQ:(i + 1) * DSEQ, :],
                                             mod_dram[1 + i, 0:D].partition_broadcast(DSEQ)).then_inc(s_bc, 16)
                                sp.dma_start(scale1[i * DSEQ:(i + 1) * DSEQ, :],
                                             mod_dram[1 + i, D:2 * D].partition_broadcast(DSEQ)).then_inc(s_bc, 16)
                        sp.wait_ge(s_rot, t + 1)
                        sp.dma_start(new_k[t], k_nat[0:r, t % 2, :]).then_inc(s_st[t % 2], 16)
                        sp.dma_start(new_kidx[t], idx_nat[0:r, t % 2, 256:320]).then_inc(s_st[t % 2], 16)
                        sp.dma_start(new_v[t], v_nat[0:r, t, :]).then_inc(s_stv, 16)
                    for n in range(4, 12):
                        j = CH[n]
                        if n < 6:
                            sp.wait_ge(s_mm, 5 * (TILES + 1))
                        else:
                            sp.wait_ge(s_adamm2, n - 5)
                            sp.wait_ge(s_modn2, n - 5)
                        sp.dma_start(w_sb[:, :, n % 2 * 512:(n % 2 + 1) * 512], w_ada[:, :, j * 512:(j + 1) * 512]).then_inc(s_adax[n % 2], 16)
                        sp.dma_start(x_nat[0:1 + SEQS, 1, n % 2 * 512:(n % 2 + 1) * 512],
                                     b_ada[j * 512:(j + 1) * 512].partition_broadcast(1 + SEQS)).then_inc(s_adax[n % 2], 16)
                        if n >= 6:
                            mod_store2(n - 2)
                    mod_store2(10)
                    mod_store2(11)
                    for i in range(2):
                        sp.wait_ge(s_modst2[i], 16 * 4)
                    sp.wait_ge(s_ln, TILES + 1)
                    sp.dma_start(chunk_v, vg[0:NS, TILES % 2, :]).then_inc(s_stv, 16)
                    sp.wait_ge(s_stv, 16 * (TILES + 2))
                    sp.wait_ge(s_st[0], 32 * 5)
                    sp.wait_ge(s_st[1], 32 * 4)

                @block.gpsimd
                def _(pool):
                    g = nc.gpsimd
                    count = [0]

                    def then(ins):
                        count[0] += 1
                        ins.then_inc(poolc, 1)
                        pool.wait_ge(poolc, count[0])

                    pool.wait_ge(s_const, 16)
                    pool.wait_ge(s_sp, 16 * (2 + 2 * SEQS))
                    g.tensor_tensor(wsp, wsp, c("tril").unsqueeze(1).to_broadcast([P, AH, P]), ALU.mult).then_inc(s_tril, 1)
                    g.tensor_tensor(wsbd[:, :, :].rearrange("p h (s i) -> p h s i", i=DSEQ),
                                    wsb4[:, :, :].unsqueeze(2).to_broadcast([NS, AH, SEQS, DSEQ]),
                                    c("blktril", NS).rearrange("p (s i) -> p s i", i=DSEQ).unsqueeze(1).to_broadcast([NS, AH, SEQS, DSEQ]),
                                    ALU.mult).then_inc(s_tril, 1)

                    def modulate(t):
                        r = rows(t)
                        pool.wait_ge(s_x[t % 2], 16 * (t // 2 + 1))
                        pool.wait_ge(s_bc, 32 if t < TILES else 32 + 32 * SEQS)
                        then(g.tensor_tensor(x_nat[0:r, t % 2, :], x_nat[0:r, t % 2, :], scale1[0:r, :], ALU.mult))
                        g.tensor_tensor(x_nat[0:r, t % 2, :], x_nat[0:r, t % 2, :], shift1[0:r, :], ALU.add).then_inc(s_h, 1)

                    def rotate(x, t, r, n):
                        cos = c("cos", r).rearrange("p (t k) -> p t k", k=HALF)[:, t:t + 1, :].to_broadcast([r, n, HALF])
                        sin = c("sin", r).rearrange("p (t k) -> p t k", k=HALF)[:, t:t + 1, :].to_broadcast([r, n, HALF])
                        m = [rot[0:r, i, 0:n * HALF].rearrange("p (n k) -> p n k", k=HALF) for i in range(4)]
                        g.tensor_tensor(m[0], x[:, :, 0:HALF], cos, ALU.mult)
                        g.tensor_tensor(m[1], x[:, :, HALF:2 * HALF], sin, ALU.mult)
                        g.tensor_tensor(m[2], x[:, :, HALF:2 * HALF], cos, ALU.mult)
                        then(g.tensor_tensor(m[3], x[:, :, 0:HALF], sin, ALU.mult))
                        g.tensor_tensor(x[:, :, 0:HALF], m[0], m[1], ALU.subtract)
                        return g.tensor_tensor(x[:, :, HALF:2 * HALF], m[2], m[3], ALU.add)

                    def head_sums(dst, x, r):
                        half = HD // 2
                        y = tmp[0:r, 0:AH * half].rearrange("p (h d) -> p h d", h=AH)
                        then(g.tensor_tensor(y, x[:, :, 0:half], x[:, :, half:HD], ALU.add))
                        while half > 2:
                            half //= 2
                            then(g.tensor_tensor(y[:, :, 0:half], y[:, :, 0:half], y[:, :, half:2 * half], ALU.add))
                        then(g.tensor_tensor(dst, y[:, :, 0], y[:, :, 1], ALU.add))

                    def gate(t):
                        r = rows(t)
                        b = (bsp if t < TILES else bsp_s)[0:r, :].unsqueeze(2).to_broadcast([r, AH, HD])
                        s = spat[0:r, :].rearrange("p (h d) -> p h d", h=AH)
                        pool.wait_ge(s_spe, t + 1)
                        then(g.tensor_tensor(s, s, b, ALU.add))
                        g.tensor_tensor(u[0:r, t % 2, :], u[0:r, t % 2, :], spat[0:r, :], ALU.mult).then_inc(s_am, 1)

                    modulate(0)
                    modulate(1)
                    for t in range(TILES + 1):
                        r = rows(t)
                        pool.wait_ge(s_ev, 5 * t + 1)
                        then(rotate(idx_nat[0:r, t % 2, 0:320].rearrange("p (n d) -> p n d", d=HD), t, r, 5))
                        g.tensor_copy(w_i[0:r, t, :], idx_nat[0:r, t % 2, 320:324])
                        pool.wait_ge(s_ev, 5 * t + 2)
                        then(rotate(q_nat[0:r, t, :].rearrange("p (n d) -> p n d", d=HD), t, r, QH))
                        pool.wait_ge(s_ev, 5 * t + 3)
                        rotate(k_nat[0:r, t % 2, :].rearrange("p (n d) -> p n d", d=HD), t, r, KVH).then_inc(s_rot, 1)
                        if t + 2 <= TILES:
                            modulate(t + 2)
                        x = vg[0:r, t % 2, :]
                        x3 = x.rearrange("p (h d) -> p h d", h=AH)
                        sq = tmp[0:r, :]
                        mean, var = st8[0:r, 0, :], st8[0:r, 1, :]
                        bc = lambda y: y.unsqueeze(2).to_broadcast([r, AH, HD])
                        pool.wait_ge(s_ev, 5 * t + 5)
                        pool.wait_ge(s_aln, 32)
                        pool.wait_ge(s_rot, t + 1)
                        head_sums(mean, x3, r)
                        then(g.tensor_scalar(mean, mean, 1.0 / HD, None, ALU.mult))
                        then(g.tensor_tensor(x3, x3, bc(mean), ALU.subtract))
                        then(g.tensor_tensor(sq, x, x, ALU.mult))
                        head_sums(var, sq.rearrange("p (h d) -> p h d", h=AH), r)
                        then(g.tensor_scalar(var, var, 1.0 / HD, EPS, ALU.mult, ALU.add))
                        then(g.tensor_tensor(var, var, c("minushalf", r)[:, 0:AH], ALU.pow))
                        then(g.tensor_tensor(x3, x3, bc(var), ALU.mult))
                        then(g.tensor_tensor(x, x, aln_g[0:r, :], ALU.mult))
                        g.tensor_tensor(x, x, aln_b[0:r, :], ALU.add).then_inc(s_ln, 1)
                        if t >= 1:
                            gate(t - 1)
                    gate(TILES)

                @block.tensor
                def _(pe):
                    def fill(key, parts):
                        n = TRN[key]
                        if n >= 2:
                            pe.wait_ge(s_tre, n - 1)
                        for i, (col, src) in enumerate(parts):
                            r, w = src.shape[0], src.shape[-1]
                            last = nc.tensor.transpose(bank[n % 2][0:w, col:col + r], src, c("ident", r)[:, 0:r])
                        last.then_inc(s_trf, 1)

                    pe.wait_ge(s_const, 16)
                    pe.wait_ge(s_silu, 1)
                    fill(("c", 0, 0), [(16 * i, cnat[:, i * P:(i + 1) * P]) for i in range(DC)])
                    pe.wait_ge(s_tril, 2)
                    for j in range(2):
                        fill(("sp", 0, j), [(P * i, wsp[:, 4 * j + i, :]) for i in range(4)])
                    fill(("spbd", 0, 0), [(NS * i, wsbd[:, i, :]) for i in range(AH)])
                    pe.wait_ge(s_tre, 1)
                    for n in range(4):
                        pe.wait_ge(s_ada[n % 2], 32 * (n // 2 + 1))
                        if n >= 2:
                            pe.wait_ge(s_modn, n - 1)
                        for i in range(DC):
                            last = nc.tensor.matmul(bank[2 + n % 2][0:1 + SEQS, :], cT[:, i, :], ada_ring[n % 2][:, i, :],
                                                    start=(i == 0), stop=(i == DC - 1))
                        last.then_inc(s_adamm, 1)
                    pe.wait_ge(s_modn, 4)

                    def h_steps(t):
                        r = rows(t)
                        pe.wait_ge(s_h, t + 1)
                        for j in range(2):
                            fill(("h", t, j), [(P * i, x_nat[0:r, t % 2, (4 * j + i) * P:(4 * j + i + 1) * P]) for i in range(4)])

                    h_steps(0)
                    for kind, t, i in STEPS:
                        r = rows(t) if t <= TILES else 0
                        if kind == "h":
                            h_steps(t)
                        elif kind == "group":
                            n = 5 * t + i
                            _, n0, w = GROUPS[i]
                            if t == 0:
                                pe.wait_ge(s_win[i], 16)
                            if i == 0:
                                pe.wait_ge(s_tre, TRN[("h", t, 1)] + 1)
                            if n >= 3:
                                pe.wait_ge(s_ev, n - 2)
                            for k in range(DC):
                                last = nc.tensor.matmul(bank[2 + n % 3][0:r, 0:w], hT[:, t % 2, k, 0:r], w_sb[:, k, n0:n0 + w],
                                                        start=(k == 0), stop=(k == DC - 1))
                            last.then_inc(s_mm, 1)
                        elif kind == "post":
                            pe.wait_ge(s_rot, t + 1)
                            ix = idx_nat[0:r, t % 2, :]
                            fill(("post", t, 0), [(0, k_nat[0:r, t % 2, 0:P]), (P, k_nat[0:r, t % 2, P:2 * P]), (2 * P, ix[:, 256:320])])
                            fill(("post", t, 1), [(P * h, ix[:, h * HD:(h + 1) * HD]) for h in range(IH)])
                        elif kind == "score":
                            keys = (t + 1) * P
                            m = IH * (t - IDX0) + i
                            if i == 0:
                                pe.wait_ge(s_tre, TRN[("post", t, 1)] + 1)
                            if m >= 1:
                                pe.wait_ge(s_acc, m)
                            for b in range((keys + 511) // 512):
                                w = min(512, keys - 512 * b)
                                last = nc.tensor.matmul(bank[5 + b][:, 0:w], qiT[:, i, :], kiT[:, 512 * b:512 * b + w],
                                                        start=True, stop=True)
                            last.then_inc(s_idxp, 1)
                        elif kind == "mix":
                            pe.wait_ge(s_ln, t + 1)
                            if t >= 1:
                                pe.wait_ge(s_spe, t)
                            for h in range(AH):
                                w = wspT[:, h, :] if t < TILES else wsbdT[:, h, :]
                                last = nc.tensor.matmul(bank[7][0:r, h * HD:(h + 1) * HD], w, vg[0:r, t % 2, h * HD:(h + 1) * HD],
                                                        start=True, stop=True)
                            last.then_inc(s_spm, 1)
                        elif kind == "ada":
                            n = t
                            pe.wait_ge(s_adax[n % 2], 32 * (n // 2 - 1))
                            pe.wait_ge(s_ev, 5 * (TILES + 1))
                            if n >= 6:
                                pe.wait_ge(s_modn2, n - 5)
                            for k in range(DC):
                                last = nc.tensor.matmul(bank[2 + n % 2][0:1 + SEQS, :], cT[:, k, :], w_sb[:, k, n % 2 * 512:(n % 2 + 1) * 512],
                                                        start=(k == 0), stop=(k == DC - 1))
                            last.then_inc(s_adamm2, 1)
                        elif kind == "aT":
                            pe.wait_ge(s_am, t + 1)
                            fill(("aT", t, 0), [(P * j, u[0:r, t % 2, j * P:(j + 1) * P]) for j in range(4)])

                @block.scalar
                def _(act):
                    s = nc.scalar

                    def empty(key, parts):
                        n = TRN[key]
                        act.wait_ge(s_trf, n + 1)
                        for dst, src in parts:
                            last = s.activation(dst, src(bank[n % 2]), ACT.Copy)
                        last.then_inc(s_tre, 1)

                    act.wait_ge(s_c, 32)
                    s.activation(cnat, cnat, ACT.Silu).then_inc(s_silu, 1)
                    act.wait_ge(s_trf, 1)
                    s.activation(cT[:, :, :], bank[0][:, 0:16 * DC].rearrange("p (c n) -> p c n", n=16)[:, :, 0:1 + SEQS], ACT.Copy).then_inc(s_tre, 1)
                    for j in range(2):
                        empty(("sp", 0, j), [(wspT[:, 4 * j:4 * j + 4, :], lambda b: b[:, :].rearrange("p (h t) -> p h t", h=4))])
                    empty(("spbd", 0, 0), [(wsbdT[:, :, :], lambda b: b[0:NS, 0:AH * NS].rearrange("p (h t) -> p h t", h=AH))])

                    def h_steps(t):
                        r = rows(t)
                        if t >= 2:
                            act.wait_ge(s_mm, 5 * (t - 1))
                        for j in range(2):
                            empty(("h", t, j), [(hT[:, t % 2, 4 * j:4 * j + 4, 0:r],
                                                 lambda b: b[:, :].rearrange("p (i r) -> p i r", i=4)[:, :, 0:r])])

                    act.wait_ge(s_trf, TRN[("spbd", 0, 0)] + 1)
                    h_steps(0)
                    for kind, t, i in STEPS:
                        r = rows(t) if t <= TILES else 0
                        if kind == "h":
                            h_steps(t)
                        elif kind == "group":
                            n = 5 * t + i
                            name, n0, w = GROUPS[i]
                            act.wait_ge(s_mm, n + 1)
                            src = bank[2 + n % 3][0:r, 0:w]
                            if name == "idx":
                                if t >= 2:
                                    act.wait_ge(s_trf, TRN[("post", t - 2, 1)] + 1)
                                    act.wait_ge(s_st[t % 2], 32 * (t // 2))
                                last = s.activation(idx_nat[0:r, t % 2, :], src, ACT.Copy)
                            elif name == "q":
                                last = s.activation(q_nat[0:r, t, :], src, ACT.Copy)
                            elif name == "kv":
                                s.activation(k_nat[0:r, t % 2, :], src[:, 0:256], ACT.Copy)
                                last = s.activation(v_nat[0:r, t, :], src[:, 256:512], ACT.Copy)
                            elif name == "au":
                                if t >= 2:
                                    act.wait_ge(s_trf, TRN[("aT", t - 2, 0)] + 1)
                                last = s.activation(u[0:r, t % 2, :], src, ACT.Gelu_apprx_tanh)
                            else:
                                if t >= 2:
                                    act.wait_ge(s_spm, t - 1)
                                last = s.activation(vg[0:r, t % 2, :], src, ACT.Gelu_apprx_tanh)
                            last.then_inc(s_ev, 1)
                        elif kind == "post":
                            tok = slice(t * P, t * P + r)
                            empty(("post", t, 0), [(kT[:, :, tok], lambda b: b[:, 0:2 * P].rearrange("p (j r) -> p j r", j=2)[:, :, 0:r]),
                                                   (kiT[:, tok], lambda b: b[0:HD, 2 * P:2 * P + r])])
                            if IDX0 < t < TILES:
                                act.wait_ge(s_idxp, IH * (t - IDX0))
                            dst = qiT[:, :, :] if t < TILES else qi_s[:, :, :]
                            empty(("post", t, 1), [(dst, lambda b: b[0:HD, :].rearrange("p (h r) -> p h r", h=IH)[:, :, 0:r])])
                        elif kind == "score":
                            keys = (t + 1) * P
                            m = IH * (t - IDX0) + i
                            act.wait_ge(s_idxp, m + 1)
                            for b in range((keys + 511) // 512):
                                w = min(512, keys - 512 * b)
                                last = s.activation(bank[5 + b][:, 0:w], bank[5 + b][:, 0:w], ACT.Relu)
                            last.then_inc(s_relu, 1)
                        elif kind == "try":
                            b = 2 * t + 1
                            keys = (b + 1) * P
                            act.wait_ge(s_cand, SEARCH * (t - 1) + i + 1)
                            s.activation(near[:, 0:keys], bias[:, bias_at[b]:bias_at[b] + keys], ACT.Sign, bias=cand[:, 1:2], scale=-1.0,
                                         accum_out=under[:, 1:2]).then_inc(s_under, 1)
                        elif kind == "mix":
                            act.wait_ge(s_spm, t + 1)
                            if t >= 1:
                                act.wait_ge(s_am, t)
                            s.activation(spat[0:r, :], bank[7][0:r, :], ACT.Copy).then_inc(s_spe, 1)
                        elif kind == "aT":
                            empty(("aT", t, 0), [(mixa[:, :, t * P:t * P + r],
                                                  lambda b: b[:, :].rearrange("p (j r) -> p j r", j=4)[:, :, 0:r])])

                @block.vector
                def _(dve):
                    v = nc.vector
                    count = [0]

                    def then(ins):
                        count[0] += 1
                        ins.then_inc(dvec, 1)
                        dve.wait_ge(dvec, count[0])

                    for n in range(4):
                        dve.wait_ge(s_adamm, n + 1)
                        if n >= 2:
                            dve.wait_ge(s_modst[n % 2], 16 * (n // 2))
                        v.scalar_tensor_tensor(out=modn[:, n % 2, :], in0=bank[2 + n % 2][0:1 + SEQS, :],
                                               scalar=1.0 if CH[n] in (2, 3, 8, 9) else 0.0, in1=bada[:, n % 2, :],
                                               op0=ALU.add, op1=ALU.add).then_inc(s_modn, 1)
                    dve.wait_ge(s_const, 16)

                    def score_of(b):
                        return bias[:, bias_at[b]:bias_at[b] + (b + 1) * P]

                    for kind, t, i in STEPS:
                        if kind == "score":
                            keys = (t + 1) * P
                            m = IH * (t - IDX0) + i
                            score, w = score_of(t), w_i[:, t, i:i + 1]
                            dve.wait_ge(s_relu, m + 1)
                            if i == 0:
                                v.tensor_scalar(score, banks56[:, 0:keys], w, None, ALU.mult).then_inc(s_acc, 1)
                            else:
                                v.scalar_tensor_tensor(out=score, in0=banks56[:, 0:keys], scalar=w, in1=score,
                                                       op0=ALU.mult, op1=ALU.add).then_inc(s_acc, 1)
                            dve.wait_ge(s_acc, m + 1)
                        elif kind == "begin":
                            for k in range(2):
                                b = 2 * t + k
                                score = score_of(b)
                                diag = score[:, b * P:(b + 1) * P]
                                then(v.tensor_reduce(low[:, k:k + 1], score, AX, ALU.max, apply_absolute_value=True))
                                then(v.scalar_tensor_tensor(out=diag, in0=c("later"), scalar=NEG_INADM, in1=diag, op0=ALU.mult, op1=ALU.add))
                            then(v.tensor_scalar(low[:, :].bitcast(I32), low[:, :].bitcast(I32), 0x7F800000, None, ALU.bitwise_and))
                            for k in range(2):
                                then(v.tensor_scalar(steps_[:, k, :], c("halvings"), low[:, k:k + 1], None, ALU.mult))
                            then(v.tensor_scalar(low[:, :], steps_[:, :, 0], -1.0, None, ALU.mult))
                            v.tensor_tensor(cand[:, :], low[:, :], steps_[:, :, 0], ALU.add).then_inc(s_cand, 1)
                            dve.wait_ge(s_cand, SEARCH * (t - 1) + 1)
                        elif kind == "try":
                            na, nb = (2 * t + 1) * P, (2 * t + 2) * P
                            bound = float(nb - 2 * TOPK_P + 1)
                            then(v.tensor_scalar(above[:, 0:na], score_of(2 * t), cand[:, 0:1], bound - (na - TOPK_P), ALU.is_lt, ALU.add,
                                                 accum_out=under[:, 0:1]))
                            dve.wait_ge(s_under, SEARCH * (t - 1) + i + 1)
                            then(v.tensor_scalar(miss[:, :], under[:, :], bound, -BIG, ALU.is_gt, ALU.mult))
                            then(v.tensor_tensor(miss[:, :], cand[:, :], miss[:, :], ALU.add))
                            then(v.tensor_tensor(low[:, :], low[:, :], miss[:, :], ALU.max))
                            if i + 1 < SEARCH:
                                v.tensor_tensor(cand[:, :], low[:, :], steps_[:, :, i + 1], ALU.add).then_inc(s_cand, 1)
                                dve.wait_ge(s_cand, SEARCH * (t - 1) + i + 2)
                        elif kind == "pick":
                            then(v.tensor_tensor(cand[:, :], low[:, :], steps_[:, :, SEARCH - 1], ALU.add))
                            then(v.tensor_scalar(miss[:, 1:2].bitcast(I32), low[:, 1:2].bitcast(I32), 0x7FFFFFFF, None, ALU.bitwise_and))
                            then(v.scalar_tensor_tensor(out=miss[:, 1:2], in0=miss[:, 1:2], scalar=2.0 ** -23, in1=low[:, 1:2], op0=ALU.mult, op1=ALU.add))
                            then(v.tensor_tensor(cand[:, 1:2], cand[:, 1:2], miss[:, 1:2], ALU.max))
                            for k in range(2):
                                b = 2 * t + k
                                n = (b + 1) * P
                                score = score_of(b)
                                then(v.tensor_scalar(above[:, 0:n], score, cand[:, k:k + 1], 0.0, ALU.is_gt, ALU.add, accum_out=nabove[:, k:k + 1]))
                                then(v.scalar_tensor_tensor(out=near[:, 0:n], in0=score, scalar=low[:, k:k + 1], in1=above[:, 0:n],
                                                            op0=ALU.is_ge, op1=ALU.subtract))
                                then(v.tensor_scalar(nabove[:, k:k + 1], nabove[:, k:k + 1], -1.0, float(TOPK_P), ALU.mult, ALU.add))
                                then(v.tensor_tensor_scan(score, c("one").to_broadcast([P, n]), near[:, 0:n], 0.0, ALU.mult, ALU.add))
                                then(v.scalar_tensor_tensor(out=near[:, 0:n], in0=score, scalar=nabove[:, k:k + 1], in1=near[:, 0:n],
                                                            op0=ALU.is_le, op1=ALU.mult))
                                then(v.tensor_tensor(above[:, 0:n], above[:, 0:n], near[:, 0:n], ALU.add))
                                then(v.tensor_scalar(score, above[:, 0:n], -1.0, -NEG_MASK, ALU.add, ALU.mult))
                        elif kind == "ada":
                            n = t
                            dve.wait_ge(s_adamm2, n - 3)
                            if n >= 6:
                                dve.wait_ge(s_modst2[n % 2], 16 * (n // 2 - 2))
                            half = slice(n % 2 * 512, (n % 2 + 1) * 512)
                            v.scalar_tensor_tensor(out=x_nat[0:1 + SEQS, 0, half], in0=bank[2 + n % 2][0:1 + SEQS, :],
                                                   scalar=1.0 if CH[n] in (2, 3, 8, 9) else 0.0, in1=x_nat[0:1 + SEQS, 1, half],
                                                   op0=ALU.add, op1=ALU.add).then_inc(s_modn2, 1)

        pages = tail.enter_context(ExitStack())
        pt = sb(pages, "pt", [1, SEQS * NPG], I32)
        ki_pg = sb(pages, "ki_pg", [P, SEQS * NPG, HD])
        k_pg = sb(pages, "k_pg", [P, SEQS * NPG, KVH * HD])
        v_pg = sb(pages, "v_pg", [P, SEQS * NPG, KVH * HD])
        c_pt = sem(pages, "c_pt")
        c_pg = [sem(pages, f"c_pg{i}") for i in range(3)]

        with ExitStack() as ctx:
            qz = sb(ctx, "qz", [P, 2, QH, P])
            qzT = sb(ctx, "qzT", [P, 2, QH, P])
            prob = sb(ctx, "prob", [P, 3, SEQ])
            pT = sb(ctx, "pT", [P, 2, TILES, P])
            o_nat = sb(ctx, "o_nat", [P, 2, QH * HD])
            mx = sb(ctx, "mx", [P, TILES * QH])
            nmx = sb(ctx, "nmx", [P, TILES * QH])
            den = sb(ctx, "den", [P, TILES * QH])
            rden = sb(ctx, "rden", [P, TILES * QH])
            zero = sb(ctx, "zero", [P, D])
            causal = sb(ctx, "causal", [P, 3 * P])
            b_causal = sem(ctx, "b_causal")
            b_zero = sem(ctx, "b_zero")
            b_fill = sem(ctx, "b_fill")
            b_z = sem(ctx, "b_z")
            b_qz = sem(ctx, "b_qz")
            b_trf = sem(ctx, "b_trf")
            b_tre = [sem(ctx, f"b_tre{i}") for i in range(2)]
            b_s = sem(ctx, "b_s")
            b_add = sem(ctx, "b_add")
            b_nmx = sem(ctx, "b_nmx")
            b_exp = sem(ctx, "b_exp")
            b_pv = sem(ctx, "b_pv")
            b_rd = sem(ctx, "b_rd")
            b_o = sem(ctx, "b_o")
            ITEMS = [(t, h) for t in range(TILES) for h in range(QH)]
            ORDER = [("q", 0), ("S", 0), ("S", 1)]
            for m, (t, h) in enumerate(ITEMS):
                if h == 4 and t + 1 < TILES:
                    ORDER.append(("q", t + 1))
                if m + 2 < len(ITEMS):
                    ORDER.append(("S", m + 2))
                ORDER.append(("pT", m))
                if m >= 1:
                    ORDER.append(("pv", m - 1))
                if h == 3 and t >= 1:
                    ORDER.append(("oT", t - 1))
            ORDER += [("pv", len(ITEMS) - 1), ("oT", TILES - 1)]
            BTR = []
            for kind, m in ORDER:
                if kind == "q":
                    BTR += [("q", m, 0), ("q", m, 1)]
                elif kind == "oT":
                    BTR.append(("oT", m, 0))
                elif kind == "pT":
                    BTR += [("pT", m, i) for i in range(1 + ITEMS[m][0] // 4)]
            BTRN = {k: n for n, k in enumerate(BTR)}

            with nc.Block() as block:
                @block.sync
                def _(sp):
                    sp.dma_start(pt[:, :], a["page_table"].rearrange("b n -> (b n)").unsqueeze(0)).then_inc(c_pt, 16)
                    sp.wait_ge(c_pt, 16)
                    with sp.Fori(0, SEQS * NPG) as i:
                        page = sp.value_load(pt[0:1, bass.ds(i, 1)], min_val=0, max_val=a["cache_k"].shape[1] - 1)
                        sp.dma_start(ki_pg[:, bass.ds(i, 1), :], a["cache_kidx"][0, bass.ds(page, 1), :, :].rearrange("n p d -> p n d")).then_inc(c_pg[0], 16)
                        sp.dma_start(k_pg[:, bass.ds(i, 1), :], a["cache_k"][0, bass.ds(page, 1), :, :, :].rearrange("n p h d -> p n (h d)")).then_inc(c_pg[1], 16)
                        sp.dma_start(v_pg[:, bass.ds(i, 1), :], a["cache_v"][0, bass.ds(page, 1), :, :, :].rearrange("n p h d -> p n (h d)")).then_inc(c_pg[2], 16)
                    sp.wait_ge(b_zero, 1)
                    with sp.Fori(NE, SLOTS) as i:
                        sp.dma_start(ys_dram.rearrange("(e p) n -> e p n", p=P)[bass.ds(i, 1), :, :].rearrange("e p n -> p (e n)"),
                                     zero[:, :]).then_inc(b_fill, 16)
                    sp.wait_ge(b_fill, 16 * MAXEXTRA)

                @block.gpsimd
                def _(pool):
                    g = nc.gpsimd
                    g.memset(zero[:, :], 0.0).then_inc(b_zero, 1)
                    g.memset(qz[:, :, :, :], 0.0).then_inc(b_z, 1)
                    pool.wait_ge(b_z, 1)
                    for t in range(TILES):
                        if t >= 2:
                            pool.wait_ge(b_trf, BTRN[("q", t - 2, 1)] + 1)
                        dst = qz[:, t % 2, :, :].rearrange("p (j b i) w -> p j b i w", j=2, b=2)
                        src = q_nat[:, t, :].rearrange("p (j b i w) -> p j b i w", j=2, b=2, i=2)
                        for b in range(2):
                            g.tensor_copy(dst[:, :, b, :, b * HD:(b + 1) * HD], src[:, :, b, :, :]).then_inc(b_qz, 1)

                @block.tensor
                def _(pe):
                    def fill(key, parts):
                        n = BTRN[key]
                        if n >= 2:
                            pe.wait_ge(b_tre[n % 2], n // 2)
                        for i, src in enumerate(parts):
                            last = nc.tensor.transpose(bank[n % 2][:, i * P:(i + 1) * P], src, c("ident"))
                        last.then_inc(b_trf, 1)

                    for kind, m in ORDER:
                        t, h = ITEMS[m] if kind in ("S", "pT", "pv") else (m, 0)
                        if kind == "q":
                            pe.wait_ge(b_qz, 2 * (t + 1))
                            for i in range(2):
                                fill(("q", t, i), [qz[:, t % 2, 4 * i + k, :] for k in range(4)])
                        elif kind == "S":
                            if h == 0:
                                n = BTRN[("q", t, 1)]
                                pe.wait_ge(b_tre[n % 2], n // 2 + 1)
                                pe.wait_ge(b_tre[1 - n % 2], (n - 1) // 2 + 1)
                            if m >= 2:
                                pe.wait_ge(b_add, m - 1)
                            keys = (t + 1) * P
                            for b in range((keys + 511) // 512):
                                w = min(512, keys - 512 * b)
                                last = nc.tensor.matmul(bank[2 + 2 * (m % 2) + b][:, 0:w], qzT[:, t % 2, h, :],
                                                        kT[:, h // 4, 512 * b:512 * b + w], start=True, stop=True)
                            last.then_inc(b_s, 1)
                        elif kind == "pT":
                            pe.wait_ge(b_exp, m + 1)
                            for i in range(1 + t // 4):
                                fill(("pT", m, i), [prob[:, m % 3, k * P:(k + 1) * P] for k in range(4 * i, min(4 * i + 4, t + 1))])
                        elif kind == "pv":
                            n = BTRN[("pT", m, t // 4)]
                            pe.wait_ge(b_tre[n % 2], n // 2 + 1)
                            if t >= 4:
                                pe.wait_ge(b_tre[1 - n % 2], (n - 1) // 2 + 1)
                            if h == 0 and t >= 2:
                                pe.wait_ge(b_o, t - 1)
                            kv = h // 2
                            for k in range(t + 1):
                                last = nc.tensor.matmul(bank[6 + t % 2][:, h * HD:(h + 1) * HD], pT[:, m % 2, k, :],
                                                        v_nat[:, k, kv * HD:(kv + 1) * HD], start=(k == 0), stop=(k == t))
                            last.then_inc(b_pv, 1)
                        else:
                            pe.wait_ge(b_o, t + 1)
                            fill(("oT", t, 0), [o_nat[:, t % 2, k * P:(k + 1) * P] for k in range(4)])

                @block.scalar
                def _(act):
                    s = nc.scalar

                    def empty(key, dst, w):
                        n = BTRN[key]
                        act.wait_ge(b_trf, n + 1)
                        s.activation(dst, bank[n % 2][:, 0:w], ACT.Copy).then_inc(b_tre[n % 2], 1)

                    for kind, m in ORDER:
                        if kind == "q":
                            if m >= 2:
                                act.wait_ge(b_s, QH * (m - 1))
                            for i in range(2):
                                empty(("q", m, i), qzT[:, m % 2, 4 * i:4 * i + 4, :], 512)
                        elif kind == "oT":
                            empty(("oT", m, 0), q_nat[:, m, :], 512)
                        elif kind == "pT":
                            t, h = ITEMS[m]
                            keys = (t + 1) * P
                            act.wait_ge(b_nmx, m + 1)
                            s.activation(prob[:, m % 3, 0:keys], prob[:, m % 3, 0:keys], ACT.Exp, bias=nmx[:, m:m + 1],
                                         scale=HD ** -0.5, accum_out=den[:, m:m + 1]).then_inc(b_exp, 1)
                            if m >= 2:
                                act.wait_ge(b_pv, m - 1)
                            if m >= 1:
                                t1 = ITEMS[m - 1][0]
                            w = min(512, keys)
                            empty(("pT", m, 0), pT[:, m % 2, 0:w // P, :], w)

                @block.vector
                def _(dve):
                    v = nc.vector
                    v.memset(causal[:, P:2 * P], 0.0).then_inc(b_causal, 1)
                    for k in (0, 2):
                        v.tensor_scalar(causal[:, k * P:(k + 1) * P], c("later"), NEG_MASK, None, ALU.mult).then_inc(b_causal, 1)
                    dve.wait_ge(b_causal, 3)
                    for m in range(len(ITEMS) + 1):
                        if m < len(ITEMS):
                            t, h = ITEMS[m]
                            keys = (t + 1) * P
                            dve.wait_ge(b_s, m + 1)
                            if m >= 3:
                                t3 = ITEMS[m - 3][0]
                                dve.wait_ge(b_trf, BTRN[("pT", m - 3, t3 // 4)] + 1)
                            src = psum[:, 512 * (2 + 2 * (m % 2)):512 * (2 + 2 * (m % 2)) + keys]
                            v.tensor_tensor_reduce(out=prob[:, m % 3, 0:keys], in0=src, in1=(bias[:, bias_at[t]:bias_at[t] + keys] if t >= 2 else causal[:, t * P:t * P + keys]),
                                                   scale=1.0, scalar=NEG_TAKEN, op0=ALU.add, op1=ALU.max,
                                                   accum_out=mx[:, m:m + 1]).then_inc(b_add, 1)
                            dve.wait_ge(b_add, m + 1)
                            v.tensor_scalar(nmx[:, m:m + 1], mx[:, m:m + 1], -HD ** -0.5, None, ALU.mult).then_inc(b_nmx, 1)
                        if m >= 1:
                            t, h = ITEMS[m - 1]
                            if t >= 4:
                                n = BTRN[("pT", m - 1, 1)]
                                dve.wait_ge(b_trf, n + 1)
                                if m >= 3:
                                    dve.wait_ge(b_pv, m - 2)
                                w = (t + 1) * P - 512
                                v.tensor_copy(pT[:, (m - 1) % 2, 4:4 + w // P, :], bank[n % 2][:, 0:w]).then_inc(b_tre[n % 2], 1)
                            if h == QH - 1:
                                e = slice(t * QH, (t + 1) * QH)
                                dve.wait_ge(b_exp, m)
                                v.reciprocal(rden[:, e], den[:, e]).then_inc(b_rd, 1)
                                dve.wait_ge(b_rd, t + 1)
                                dve.wait_ge(b_pv, m)
                                if t >= 2:
                                    dve.wait_ge(b_trf, BTRN[("oT", t - 2, 0)] + 1)
                                v.tensor_tensor(o_nat[:, t % 2, :].rearrange("p (h d) -> p h d", h=QH),
                                                bank[6 + t % 2].rearrange("p (h d) -> p h d", h=QH),
                                                rden[:, e].unsqueeze(2).to_broadcast([P, QH, HD]), ALU.mult).then_inc(b_o, 1)

        L = PAST + DSEQ
        with ExitStack() as ctx:
            qzs = sb(ctx, "qzs", [NS, QH, P])
            qzsT = sb(ctx, "qzsT", [P, QH, NS])
            qsel = sb(ctx, "qsel", [P, 2, SEQS, P])
            isel = sb(ctx, "isel", [HD, SEQS, P])
            kipT = sb(ctx, "kipT", [HD, 2, PAST])
            kpT = sb(ctx, "kpT", [P, 2, 2, PAST])
            wrow = sb(ctx, "wrow", [P, 1])
            relw = sb(ctx, "relw", [P, L])
            sc = sb(ctx, "sc", [P, L])
            top = sb(ctx, "top", [P, 8])
            pr = sb(ctx, "pr", [P, 2, L])
            pn = sb(ctx, "pn", [P, 2, NS])
            prT = sb(ctx, "prT", [P, 2, NPG, P])
            pnT = sb(ctx, "pnT", [NS, 2, P])
            st = sb(ctx, "st", [P, 2, 4])
            c_qz = sem(ctx, "c_qz")
            c_sel = sem(ctx, "c_sel")
            c_trf = sem(ctx, "c_trf")
            c_tre = sem(ctx, "c_tre")
            c_qk = sem(ctx, "c_qk")
            c_w = sem(ctx, "c_w")
            c_sum = sem(ctx, "c_sum")
            c_dve = sem(ctx, "c_dve")
            c_nmx = sem(ctx, "c_nmx")
            c_exp = sem(ctx, "c_exp")
            c_pn = sem(ctx, "c_pn")
            c_o = sem(ctx, "c_o")
            c_out = sem(ctx, "c_out")
            CTR = [("q", 0, 0)] + [(k, s, j) for s in range(SEQS) for k, j in (("ki", 0), ("k", 0), ("k", 1))]
            CTR += [x for j in range(2) for x in (("p", j, 0), ("pn", j, 0))]
            CTRN = {k: n for n, k in enumerate(CTR)}

            with nc.Block() as block:
                @block.gpsimd
                def _(pool):
                    g = nc.gpsimd
                    g.memset(qzs[:, :, :], 0.0).then_inc(c_qz, 1)
                    pool.wait_ge(c_qz, 1)
                    dst = qzs[:, :, :].rearrange("p (j b i) w -> p j b i w", j=2, b=2)
                    src = q_nat[0:NS, TILES, :].rearrange("p (j b i w) -> p j b i w", j=2, b=2, i=2)
                    for b in range(2):
                        g.tensor_copy(dst[:, :, b, :, b * HD:(b + 1) * HD], src[:, :, b, :, :]).then_inc(c_qz, 1)

                @block.tensor
                def _(pe):
                    def fill(key, parts, w=P):
                        n = CTRN[key]
                        if n >= 2:
                            pe.wait_ge(c_tre, n - 1)
                        for i, src in enumerate(parts):
                            r, m = src.shape
                            last = nc.tensor.transpose(bank[n % 2][0:m, i * r:(i + 1) * r], src, c("ident", r)[:, 0:r])
                        last.then_inc(c_trf, 1)

                    pe.wait_ge(c_qz, 3)
                    fill(("q", 0, 0), [qzs[:, h, :] for h in range(QH)])
                    for i in range(3):
                        pe.wait_ge(c_pg[i], 16 * SEQS * NPG)
                    for s in range(SEQS + 1):
                        if s < SEQS:
                            fill(("ki", s, 0), [ki_pg[:, NPG * s + k, :] for k in range(NPG)])
                            for j in range(2):
                                fill(("k", s, j), [k_pg[:, NPG * s + k, j * P:(j + 1) * P] for k in range(NPG)])
                        if s >= 1:
                            r = s - 1
                            pe.wait_ge(c_tre, CTRN[("k", r, 1)] + 1)
                            if r == 0:
                                pe.wait_ge(c_sel, IH + QH)
                            new = slice(SEQ + r * DSEQ, SEQ + (r + 1) * DSEQ)
                            f = dict(start=(r == 0), stop=(r == SEQS - 1))
                            nc.tensor.matmul(bank[2][:, :], isel[:, r, :], kipT[:, r % 2, :], **f)
                            nc.tensor.matmul(bank[3][:, 0:DSEQ], isel[:, r, :], kiT[:, new], **f)
                            for j in range(2):
                                nc.tensor.matmul(bank[4 + j][:, :], qsel[:, j, r, :], kpT[:, r % 2, j, :], **f)
                                last = nc.tensor.matmul(bank[6 + j][:, 0:DSEQ], qsel[:, j, r, :], kT[:, j, new], **f)
                            last.then_inc(c_qk, 1)
                    pe.wait_ge(c_w, 2)
                    nc.tensor.matmul(bank[2][:, :], c("sametok"), relw[:, 0:PAST], start=True, stop=True)
                    nc.tensor.matmul(bank[3][:, 0:DSEQ], c("sametok"), relw[:, PAST:L], start=True, stop=True).then_inc(c_sum, 1)
                    for j in range(2):
                        pe.wait_ge(c_pn, j + 1)
                        fill(("p", j, 0), [pr[:, j, k * P:(k + 1) * P] for k in range(NPG)])
                        fill(("pn", j, 0), [pn[:, j, :]])
                    for j in range(2):
                        out = bank[2 + j][:, 0:P]
                        pe.wait_ge(c_tre, CTRN[("pn", j, 0)] + 1)
                        nc.tensor.matmul(out, v_nat[0:NS, TILES, j * P:(j + 1) * P], pnT[:, j, :], start=True, stop=False, skip_group_check=True)
                        o3 = out.rearrange("p (h n) -> p h n", h=4)
                        for s in range(SEQS):
                            for k in range(NPG):
                                m = prT[:, j, k, :].rearrange("p (h n) -> p h n", h=4)[:, :, s * DSEQ:(s + 1) * DSEQ]
                                last = nc.tensor.matmul(o3[:, :, s * DSEQ:(s + 1) * DSEQ], v_pg[:, NPG * s + k, j * P:(j + 1) * P], m,
                                                        start=False, stop=(s == SEQS - 1 and k == NPG - 1), skip_group_check=True)
                        last.then_inc(c_o, 1)

                @block.scalar
                def _(act):
                    s_ = nc.scalar

                    def empty(key, dst, src):
                        n = CTRN[key]
                        act.wait_ge(c_trf, n + 1)
                        s_.activation(dst, src(bank[n % 2]), ACT.Copy).then_inc(c_tre, 1)

                    empty(("q", 0, 0), qzsT[:, :, :], lambda b: b[:, 0:QH * NS].rearrange("p (h n) -> p h n", h=QH))
                    for s in range(SEQS):
                        if s >= 2:
                            act.wait_ge(c_qk, s - 1)
                        empty(("ki", s, 0), kipT[:, s % 2, :], lambda b: b[0:HD, :])
                        for j in range(2):
                            empty(("k", s, j), kpT[:, s % 2, j, :], lambda b: b)
                    for j in range(2):
                        act.wait_ge(c_nmx, j + 1)
                        s_.activation(pr[:, j, :], pr[:, j, :], ACT.Exp, bias=st[:, j, 1:2], scale=HD ** -0.5,
                                      accum_out=st[:, j, 2:3]).then_inc(c_exp, 1)
                    for j in range(2):
                        empty(("p", j, 0), prT[:, j, :, :], lambda b: b.rearrange("p (k n) -> p k n", k=NPG))
                        empty(("pn", j, 0), pnT[:, j, :], lambda b: b[0:NS, 0:P])
                    for j in range(2):
                        act.wait_ge(c_o, j + 1)
                        for hh in range(4):
                            src, dst = HD * (hh // 2), HD * (hh % 2)
                            chunk = 2 * j + hh // 2
                            s_.activation(q_nat[dst:dst + HD, TILES, chunk * P:chunk * P + NS],
                                          bank[2 + j][src:src + HD, hh * NS:(hh + 1) * NS], ACT.Copy).then_inc(c_out, 1)

                @block.vector
                def _(dve):
                    v = nc.vector
                    count = [0]

                    def then(ins):
                        count[0] += 1
                        ins.then_inc(c_dve, 1)
                        dve.wait_ge(c_dve, count[0])

                    def cols(name, r):
                        return c(name, r).rearrange("p (s n) -> p s n", s=SEQS)

                    for h in range(IH):
                        v.tensor_tensor(isel[:, :, h * NS:(h + 1) * NS], qi_s[:, h:h + 1, :].to_broadcast([HD, SEQS, NS]),
                                        cols("seqcol", HD), ALU.mult).then_inc(c_sel, 1)
                        v.tensor_copy(wrow[h * NS:(h + 1) * NS, :], w_i[0:NS, TILES, h:h + 1]).then_inc(c_dve, 1)
                        count[0] += 1
                    dve.wait_ge(c_tre, 1)
                    for h in range(QH):
                        v.tensor_tensor(qsel[:, h // 4, :, (h % 4) * NS:(h % 4 + 1) * NS], qzsT[:, h:h + 1, :].to_broadcast([P, SEQS, NS]),
                                        cols("seqcol", P), ALU.mult).then_inc(c_sel, 1)
                    dve.wait_ge(c_dve, count[0])
                    dve.wait_ge(c_qk, SEQS)
                    v.tensor_scalar(relw[:, 0:PAST], bank[2], 0.0, wrow[:, 0:1], ALU.max, ALU.mult).then_inc(c_w, 1)
                    v.tensor_scalar(relw[:, PAST:L], bank[3][:, 0:DSEQ], 0.0, wrow[:, 0:1], ALU.max, ALU.mult).then_inc(c_w, 1)
                    dve.wait_ge(c_sum, 1)
                    v.tensor_copy(sc[:, 0:PAST], bank[2])
                    then(v.tensor_tensor(sc[:, PAST:L], bank[3][:, 0:DSEQ], c("newneg"), ALU.add))
                    for _ in range(TOPK_S // 8):
                        then(v.max(out=top[:, :], in_=sc[:, :]))
                        then(v.match_replace(out=sc[:, :], in_to_replace=top[:, :], in_values=sc[:, :], imm_value=NEG_TAKEN))
                    then(v.max(out=top[:, :], in_=sc[:, :]))
                    then(v.memset(top[:, TOPK_S % 8:8], NEG_TAKEN))
                    then(v.match_replace(out=sc[:, :], in_to_replace=top[:, :], in_values=sc[:, :], imm_value=NEG_TAKEN))
                    then(v.tensor_scalar(sc[:, :], sc[:, :], NEG_TAKEN, NEG_MASK, ALU.not_equal, ALU.mult))
                    for j in range(2):
                        v.tensor_tensor(pr[:, j, 0:PAST], bank[4 + j], sc[:, 0:PAST], ALU.add)
                        then(v.tensor_tensor(pr[:, j, PAST:L], bank[6 + j][:, 0:DSEQ], sc[:, PAST:L], ALU.add))
                        then(v.tensor_reduce(st[:, j, 0:1], pr[:, j, :], AX, ALU.max))
                        v.tensor_scalar(st[:, j, 1:2], st[:, j, 0:1], -HD ** -0.5, None, ALU.mult).then_inc(c_nmx, 1)
                    for j in range(2):
                        dve.wait_ge(c_exp, j + 1)
                        then(v.reciprocal(st[:, j, 3:4], st[:, j, 2:3]))
                        then(v.tensor_scalar(pr[:, j, :], pr[:, j, :], st[:, j, 3:4], None, ALU.mult))
                        v.tensor_tensor(pn[:, j, :].rearrange("p (s n) -> p s n", s=SEQS),
                                        pr[:, j:j + 1, PAST:L].to_broadcast([P, SEQS, DSEQ]),
                                        c("own").unsqueeze(2).to_broadcast([P, SEQS, DSEQ]), ALU.mult).then_inc(c_pn, 1)

        TA = TILES + 1
        pages.close()
        with ExitStack() as ctx:
            w_o = sb(ctx, "w_o", [P, DC, D])
            xr = sb(ctx, "xr", [P, 2, D])
            z = sb(ctx, "z", [P, 2, D])
            h2 = sb(ctx, "h2", [P, 2, D])
            h2T = sb(ctx, "h2T", [P, DC, P])
            vec = {n: sb(ctx, n, [P, D]) for n in ("gate1", "shift2", "scale2", "ln1_g", "ln1_b")}
            rw = sb(ctx, "rw", [P, DC, NG + NE])
            stat = sb(ctx, "stat", [P, 2, 2, 6])
            mv = sb(ctx, "mv", [P, 2, 2])
            d_w = sem(ctx, "d_w")
            d_v = sem(ctx, "d_v")
            d_x = [sem(ctx, f"d_xr{i}") for i in range(2)]
            d_mm = sem(ctx, "d_mm")
            d_z = sem(ctx, "d_z")
            d_dve = sem(ctx, "d_dve")
            d_mv = sem(ctx, "d_mv")
            d_pool = sem(ctx, "d_pool")
            d_rs = sem(ctx, "d_rs")
            d_x1 = sem(ctx, "d_x1")
            d_h2 = sem(ctx, "d_h2")
            d_st = [sem(ctx, f"d_st{i}") for i in range(2)]
            d_trf = sem(ctx, "d_trf")
            d_tre = sem(ctx, "d_tre")
            d_lg = sem(ctx, "d_lg")
            d_lge = sem(ctx, "d_lge")
            x1_tile = [x1_dram[t * P:t * P + rows(t), :] for t in range(TA)]
            h2_tile = [h2_dram[t * P:t * P + rows(t), :] for t in range(TA)]

            with nc.Block() as block:
                @block.sync
                def _(sp):
                    w = a["w_out"][0].rearrange("(c p) n -> p c n", p=P)
                    for i in range(2):
                        sp.dma_start(xr[:, i, :], x_tile[i]).then_inc(d_x[i], 16)
                        sp.dma_start(w_o[:, :, i * 512:(i + 1) * 512], w[:, :, i * 512:(i + 1) * 512]).then_inc(d_w, 16)
                    mods = (("gate1", 2), ("shift2", 3), ("scale2", 4))
                    for n, j in mods:
                        sp.dma_start(vec[n][:, :], mod_dram[0, j * D:(j + 1) * D].partition_broadcast(P)).then_inc(d_v, 16)
                    for n in ("ln1_g", "ln1_b"):
                        sp.dma_start(vec[n][:, :], a[n][0].partition_broadcast(P)).then_inc(d_v, 16)
                    sp.dma_start(rw[:, :, 0:NG], a["w_group_router"][0].rearrange("(c p) g -> p c g", p=P)).then_inc(d_v, 16)
                    sp.dma_start(rw[:, :, NG:NG + NE], a["w_expert_router"][0].rearrange("(c p) g e -> p c (g e)", p=P)).then_inc(d_v, 16)
                    for t in range(TA):
                        r = rows(t)
                        sp.wait_ge(d_x1, t + 1)
                        sp.dma_start(x1_tile[t], z[0:r, t % 2, :]).then_inc(d_st[t % 2], 16)
                        if t + 2 < TA:
                            sp.dma_start(xr[0:rows(t + 2), t % 2, :], x_tile[t + 2]).then_inc(d_x[t % 2], 16)
                        sp.wait_ge(d_h2, t + 1)
                        sp.dma_start(h2_tile[t], h2[0:r, t % 2, :]).then_inc(d_st[t % 2], 16)
                        if t == TILES - 1:
                            for n, j in mods:
                                for i in range(SEQS):
                                    sp.dma_start(vec[n][i * DSEQ:(i + 1) * DSEQ, :],
                                                 mod_dram[1 + i, j * D:(j + 1) * D].partition_broadcast(DSEQ)).then_inc(d_v, 16)
                    sp.wait_ge(d_st[0], 32 * 5)
                    sp.wait_ge(d_st[1], 32 * 4)

                @block.tensor
                def _(pe):
                    pe.wait_ge(d_w, 32)
                    for t in range(TA + 1):
                        if t < TA:
                            r = rows(t)
                            if t >= 2:
                                pe.wait_ge(d_z, t - 1)
                            for half in range(2):
                                for k in range(DC):
                                    lhs = mixa[:, k, t * P:t * P + r] if k < 4 else q_nat[:, t, (k - 4) * P:(k - 4) * P + r]
                                    last = nc.tensor.matmul(bank[2 + 2 * (t % 2) + half][0:r, :], lhs, w_o[:, k, half * 512:(half + 1) * 512],
                                                            start=(k == 0), stop=(k == DC - 1))
                            last.then_inc(d_mm, 1)
                        if t >= 1:
                            m, r = t - 1, rows(t - 1)
                            pe.wait_ge(d_h2, m + 1)
                            for j in range(2):
                                if m >= 1:
                                    pe.wait_ge(d_tre, 2 * m - 1 + j)
                                for k in range(4):
                                    last = nc.tensor.transpose(bank[j][:, k * P:k * P + r], h2[0:r, m % 2, (4 * j + k) * P:(4 * j + k + 1) * P],
                                                               c("ident", r)[:, 0:r])
                                last.then_inc(d_trf, 1)
                            pe.wait_ge(d_tre, 2 * m + 2)
                            pe.wait_ge(d_v, 16 * 7)
                            if m >= 1:
                                pe.wait_ge(d_lge, m)
                            for k in range(DC):
                                last = nc.tensor.matmul(bank[6][0:r, 0:NG + NE], h2T[:, k, 0:r], rw[:, k, :], start=(k == 0), stop=(k == DC - 1))
                            last.then_inc(d_lg, 1)

                @block.scalar
                def _(act):
                    for t in range(TA):
                        r = rows(t)
                        for j in range(2):
                            act.wait_ge(d_trf, 2 * t + j + 1)
                            if t >= 1:
                                act.wait_ge(d_lg, t)
                            nc.scalar.activation(h2T[:, 4 * j:4 * j + 4, 0:r], bank[j].rearrange("p (k r) -> p k r", k=4)[:, :, 0:r],
                                                 ACT.Copy).then_inc(d_tre, 1)
                        act.wait_ge(d_lg, t + 1)
                        nc.scalar.activation(logit[0:r, t, :], bank[6][0:r, 0:NG + NE], ACT.Copy).then_inc(d_lge, 1)

                @block.gpsimd
                def _(pool):
                    g = nc.gpsimd
                    for t in range(TA):
                        r, b = rows(t), t % 2
                        pool.wait_ge(d_mv, t + 1)
                        g.tensor_scalar(mv[0:r, b, 1:2], mv[0:r, b, 1:2], EPS, None, ALU.add).then_inc(d_pool, 1)
                        pool.wait_ge(d_pool, 2 * t + 1)
                        g.tensor_tensor(mv[0:r, b, 1:2], mv[0:r, b, 1:2], c("minushalf", r)[:, 0:1], ALU.pow).then_inc(d_rs, 1)
                        pool.wait_ge(d_x1, t + 1)
                        if t >= 2:
                            pool.wait_ge(d_st[b], 32 * (t // 2))
                            pool.wait_ge(d_trf, 2 * (t - 1))
                        if t == TILES:
                            pool.wait_ge(d_v, 16 * (7 + 3 * SEQS))
                        g.tensor_tensor(h2[0:r, b, :], z[0:r, b, :], vec["scale2"][0:r, :], ALU.mult).then_inc(d_pool, 1)
                        pool.wait_ge(d_pool, 2 * t + 2)
                        g.tensor_tensor(h2[0:r, b, :], h2[0:r, b, :], vec["shift2"][0:r, :], ALU.add).then_inc(d_h2, 1)

                @block.vector
                def _(dve):
                    v = nc.vector
                    count = [0]

                    def then(ins):
                        count[0] += 1
                        ins.then_inc(d_dve, 1)
                        dve.wait_ge(d_dve, count[0])

                    v.memset(logit[:, TILES, :], 0.0).then_inc(d_dve, 1)
                    count[0] += 1
                    for t in range(TA):
                        r, b = rows(t), t % 2
                        zz = z[0:r, b, :]
                        dve.wait_ge(d_mm, t + 1)
                        dve.wait_ge(d_v, 16 * 7 if t < TILES else 16 * (7 + 3 * SEQS))
                        if t >= 2:
                            dve.wait_ge(d_st[b], 32 * (t // 2))
                            dve.wait_ge(d_h2, t - 1)
                        v.tensor_tensor(zz, psum[0:r, 512 * (2 + 2 * b):512 * (4 + 2 * b)], vec["gate1"][0:r, :], ALU.mult).then_inc(d_z, 1)
                        dve.wait_ge(d_z, t + 1)
                        dve.wait_ge(d_x[b], 16 * (t // 2 + 1))
                        then(v.scalar_tensor_tensor(out=zz, in0=xr[0:r, b, :], scalar=ALPHA, in1=zz, op0=ALU.mult, op1=ALU.add))
                        v.bn_stats(stat[0:r, b, 0, :], z[0:r, b, 0:512])
                        then(v.bn_stats(stat[0:r, b, 1, :], z[0:r, b, 512:1024]))
                        v.bn_aggr(mv[0:r, b, :], stat[0:r, b, :, :]).then_inc(d_mv, 1)
                        dve.wait_ge(d_rs, t + 1)
                        then(v.tensor_scalar(zz, zz, mv[0:r, b, 0:1], mv[0:r, b, 1:2], ALU.subtract, ALU.mult))
                        then(v.tensor_tensor(zz, zz, vec["ln1_g"][0:r, :], ALU.mult))
                        v.tensor_tensor(zz, zz, vec["ln1_b"][0:r, :], ALU.add).then_inc(d_x1, 1)

        tail.close()
        consts.append(sb(keep, "const_r", [P, table.shape[1] - early]))
        vec2 = {n: sb(keep, "v2" + n, [P, D]) for n in ("gate2", "ln2_g", "ln2_b")}
        g_v = sem(keep, "g_v")
        weight = sb(keep, "weight", [P, 2, TILES + 1])
        slot = sb(keep, "slot", [P, 2, TILES + 1], I32)
        tokens = sb(keep, "tokens", [P, SLOTS], I32)
        exi = sb(keep, "exi", [1, MAXEXTRA + 1], I32)
        x1 = sb(keep, "x1", [P, 4, D])
        g_x = [sem(keep, f"g_x{i}") for i in range(4)]

        weights = keep.enter_context(ExitStack())
        wg = sb(weights, "wg", [P, 2, DC, DE])
        wu = sb(weights, "wu", [P, 2, DC, DE])
        wd = sb(weights, "wd", [P, 2, DE // P, D])
        KD = DE // P
        wg_v = a["w_gate"][0].rearrange("e (p k) f -> e p k f", k=DC)
        wu_v = a["w_up"][0].rearrange("e (p k) f -> e p k f", k=DC)
        wd_v = a["w_down"][0].rearrange("e (p k) n -> e p k n", k=KD)
        f_w = {n: [sem(keep, f"f_w{n}{i}") for i in range(2)] for n in "gud"}

        with ExitStack() as ctx:
            R = [P, TA]
            t3 = lambda n, k: sb(ctx, n, [P, TA, k])
            gmax, gsum, gw = sb(ctx, "gmax", R), sb(ctx, "gsum", R), sb(ctx, "gw", R)
            gs, ohg, gpri = t3("gs", NG), t3("ohg", NG), t3("gpri", NG)
            prod = sb(ctx, "prod", [P, TA, NG, EPG])
            el = t3("el", EPG)
            pri = t3("pri", EPG)
            oh = [t3("oh1", EPG), t3("oh2", EPG)]
            m12 = sb(ctx, "m12", [P, 2, TA])
            pm = sb(ctx, "pm", R)
            ex = sb(ctx, "ex", R)
            mk = [sb(ctx, f"mk{k}", [P, TA, NE]) for k in range(2)]
            msum = sb(ctx, "msum", [P, TA, NE])
            base = sb(ctx, "base", [P, TA + 1, NE])
            rank = sb(ctx, "rank", [P, TA, NE])
            over = sb(ctx, "over", [P, NE, 8])
            extra = sb(ctx, "extra", [P, NE])
            incl = sb(ctx, "incl", [P, NE])
            ebase = sb(ctx, "ebase", [P, NE])
            rr, eb, ei, jj, j0 = (sb(ctx, n, R) for n in ("rr", "eb", "ei", "jj", "j0"))
            ge = sb(ctx, "ge", [P, TA, 8])
            tile_of = sb(ctx, "tile_of", [P, 2, TA])
            pos_of = sb(ctx, "pos_of", [P, 2, TA])
            slot_f = sb(ctx, "slot_f", [P, 2, TA])
            onepos = sb(ctx, "onepos", [P, 2 * TA, P])
            onetile = sb(ctx, "onetile", [P, 2 * TA, SLOTS])
            below = sb(ctx, "below", [1, MAXEXTRA, NE])
            exf = sb(ctx, "exf", [1, MAXEXTRA + 1])
            prod2 = prod[:, :, :, :].rearrange("p t g e -> p t (g e)")
            e_const = sem(ctx, "e_const")
            e_dve = sem(ctx, "e_dve")
            e_exp = sem(ctx, "e_exp")
            e_m = sem(ctx, "e_m")
            e_pre = sem(ctx, "e_pre")
            e_one = sem(ctx, "e_one")
            e_list = sem(ctx, "e_list")
            DV = {}

            with nc.Block() as block:
                @block.sync
                def _(sp):
                    sp.dma_start(consts[1][:, :], a["table"][:, early:table.shape[1]]).then_inc(e_const, 16)
                    for e in range(2):
                        for w, view, n in ((wg, wg_v, "g"), (wu, wu_v, "u"), (wd, wd_v, "d")):
                            sp.dma_start(w[:, e, :, :], view[e]).then_inc(f_w[n][e], 16)

                @block.vector
                def _(dve):
                    v = nc.vector
                    count = [0]
                    dve.wait_ge(e_const, 16)

                    def then(ins):
                        count[0] += 1
                        ins.then_inc(e_dve, 1)
                        dve.wait_ge(e_dve, count[0])

                    def bc(x, *shape):
                        return x.to_broadcast(list(shape))

                    def one_hot(dst, x, top, n, priority, scratch):
                        then(v.tensor_tensor(scratch, x, bc(top.unsqueeze(2), P, TA, n), ALU.is_equal))
                        then(v.tensor_tensor(scratch, scratch, bc(priority.unsqueeze(1), P, TA, n), ALU.mult))
                        then(v.tensor_reduce(pm[:, :], scratch, AX, ALU.max))
                        then(v.tensor_tensor(dst, scratch, bc(pm[:, :].unsqueeze(2), P, TA, n), ALU.is_equal))

                    G = logit[:, :, 0:NG]
                    E = logit[:, :, NG:NG + NE].rearrange("p t (g e) -> p t g e", g=NG)
                    first = c("first")
                    then(v.tensor_reduce(gmax[:, :], G, AX, ALU.max))
                    then(v.tensor_tensor(gs[:, :, :], G, bc(gmax[:, :].unsqueeze(2), P, TA, NG), ALU.subtract))
                    DV["gs"] = count[0]
                    one_hot(ohg[:, :, :], G, gmax[:, :], NG, first[:, 0:NG], gpri[:, :, :])
                    then(v.tensor_tensor(prod[:, :, :, :], E, bc(ohg[:, :, :].unsqueeze(3), P, TA, NG, EPG), ALU.mult))
                    then(v.tensor_reduce(el[:, :, :], prod[:, :, :, :].rearrange("p t g e -> p t e g"), AX, ALU.add))
                    for k in range(2):
                        then(v.tensor_reduce(m12[:, k, :], el[:, :, :], AX, ALU.max))
                        one_hot(oh[k][:, :, :], el[:, :, :], m12[:, k, :], EPG, first, pri[:, :, :])
                        if k == 0:
                            then(v.scalar_tensor_tensor(out=el[:, :, :], in0=oh[0][:, :, :], scalar=NEG_INADM, in1=el[:, :, :],
                                                        op0=ALU.mult, op1=ALU.add))
                    then(v.tensor_tensor(ex[:, :], m12[:, 1, :], m12[:, 0, :], ALU.subtract))
                    DV["ex"] = count[0]
                    for k in range(2):
                        then(v.tensor_tensor(mk[k][:, :, :].rearrange("p t (g e) -> p t g e", g=NG),
                                             bc(oh[k][:, :, :].unsqueeze(2), P, TA, NG, EPG), bc(ohg[:, :, :].unsqueeze(3), P, TA, NG, EPG), ALU.mult))
                        then(v.tensor_tensor(mk[k][:, :, :], mk[k][:, :, :], bc(c("valid").unsqueeze(2), P, TA, NE), ALU.mult))
                    v.tensor_tensor(msum[:, :, :], mk[0][:, :, :], mk[1][:, :, :], ALU.add).then_inc(e_m, 1)
                    dve.wait_ge(e_exp, 2)
                    then(v.tensor_reduce(gsum[:, :], gs[:, :, :], AX, ALU.add))
                    then(v.reciprocal(gw[:, :], gsum[:, :]))
                    then(v.tensor_scalar(pm[:, :], ex[:, :], 1.0, None, ALU.add))
                    then(v.reciprocal(pm[:, :], pm[:, :]))
                    then(v.tensor_tensor(weight[:, 0, :], gw[:, :], pm[:, :], ALU.mult))
                    then(v.tensor_tensor(weight[:, 1, :], weight[:, 0, :], ex[:, :], ALU.mult))
                    dve.wait_ge(e_pre, 2)
                    then(v.memset(base[:, 0, :], 0.0))
                    for t in range(TA):
                        then(v.tensor_tensor(base[:, t + 1, :], base[:, t, :], bank[3][:, t * NE:(t + 1) * NE], ALU.add))
                    then(v.tensor_tensor(rank[:, :, :], bank[2][:, 0:TA * NE].rearrange("p (t e) -> p t e", e=NE), base[:, 0:TA, :], ALU.add))
                    then(v.tensor_tensor(over[:, :, :], bc(base[:, TA, :].unsqueeze(2), P, NE, 8), bc(c("steps").unsqueeze(1), P, NE, 8), ALU.is_gt))
                    then(v.tensor_reduce(extra[:, :], over[:, :, :], AX, ALU.add))
                    then(v.tensor_tensor_scan(incl[:, :], c("ones")[:, 0:NE], extra[:, :], 0.0, ALU.mult, ALU.add))
                    then(v.tensor_tensor(ebase[:, :], incl[:, :], extra[:, :], ALU.subtract))
                    then(v.tensor_scalar(ebase[:, :], ebase[:, :], float(NE - 1), None, ALU.add))
                    for k in range(2):
                        for dst, src in ((rr, rank[:, :, :]), (eb, bc(ebase[:, :].unsqueeze(1), P, TA, NE)),
                                         (ei, bc(c("iota")[:, 0:NE].unsqueeze(1), P, TA, NE))):
                            then(v.tensor_tensor(prod2, mk[k][:, :, :], src, ALU.mult))
                            then(v.tensor_reduce(dst[:, :], prod2, AX, ALU.add))
                        then(v.tensor_tensor(ge[:, :, :], bc(rr[:, :].unsqueeze(2), P, TA, 8), bc(c("steps").unsqueeze(1), P, TA, 8), ALU.is_ge))
                        then(v.tensor_reduce(jj[:, :], ge[:, :, :], AX, ALU.add))
                        then(v.tensor_scalar(j0[:, :], jj[:, :], 0.0, None, ALU.is_equal))
                        then(v.tensor_tensor(eb[:, :], eb[:, :], jj[:, :], ALU.add))
                        then(v.tensor_tensor(ei[:, :], ei[:, :], eb[:, :], ALU.subtract))
                        then(v.tensor_tensor(ei[:, :], ei[:, :], j0[:, :], ALU.mult))
                        then(v.tensor_tensor(tile_of[:, k, :], ei[:, :], eb[:, :], ALU.add))
                        then(v.scalar_tensor_tensor(out=pos_of[:, k, :], in0=jj[:, :], scalar=-float(P), in1=rr[:, :], op0=ALU.mult, op1=ALU.add))
                        then(v.scalar_tensor_tensor(out=slot_f[:, k, :], in0=tile_of[:, k, :], scalar=float(P), in1=pos_of[:, k, :],
                                                    op0=ALU.mult, op1=ALU.add))
                    then(v.tensor_copy(slot[:, :, :], slot_f[:, :, :]))
                    for k in range(2):
                        for t in range(TA):
                            v.tensor_scalar(onepos[:, k * TA + t, :], c("iota"), pos_of[:, k, t:t + 1], None, ALU.is_equal).then_inc(e_one, 1)
                            v.tensor_scalar(onetile[:, k * TA + t, :], c("iota")[:, 0:SLOTS], tile_of[:, k, t:t + 1], c("token")[:, t:t + 1],
                                            ALU.is_equal, ALU.mult).then_inc(e_one, 1)
                    then(v.tensor_tensor(below[:, :, :], bc(incl[0:1, :].unsqueeze(1), 1, MAXEXTRA, NE),
                                         bc(c("iota", 1)[:, 0:MAXEXTRA].unsqueeze(2), 1, MAXEXTRA, NE), ALU.is_le))
                    then(v.tensor_reduce(exf[:, 0:MAXEXTRA], below[:, :, :], AX, ALU.add))
                    then(v.tensor_scalar(exf[:, 0:MAXEXTRA], exf[:, 0:MAXEXTRA], float(NE - 1), None, ALU.min))
                    then(v.tensor_copy(exf[:, MAXEXTRA:MAXEXTRA + 1], incl[0:1, NE - 1:NE]))
                    then(v.tensor_copy(exi[:, :], exf[:, :]))
                    dve.wait_ge(e_list, 1)
                    then(v.tensor_copy(tokens[:, :], bank[4][:, 0:SLOTS]))

                @block.scalar
                def _(act):
                    act.wait_ge(e_dve, DV["gs"])
                    nc.scalar.activation(gs[:, :, :], gs[:, :, :], ACT.Exp).then_inc(e_exp, 1)
                    act.wait_ge(e_dve, DV["ex"])
                    nc.scalar.activation(ex[:, :], ex[:, :], ACT.Exp).then_inc(e_exp, 1)

                @block.tensor
                def _(pe):
                    pe.wait_ge(e_m, 1)
                    m = msum[:, :, :].rearrange("p t e -> p (t e)")
                    nc.tensor.matmul(bank[2][:, 0:TA * NE], c("before"), m, start=True, stop=True).then_inc(e_pre, 1)
                    nc.tensor.matmul(bank[3][:, 0:TA * NE], c("ones"), m, start=True, stop=True).then_inc(e_pre, 1)
                    for n in range(2 * TA):
                        pe.wait_ge(e_one, 2 * n + 2)
                        last = nc.tensor.matmul(bank[4][:, 0:SLOTS], onepos[:, n, :], onetile[:, n, :], start=(n == 0), stop=(n == 2 * TA - 1))
                    last.then_inc(e_list, 1)

        with ExitStack() as ctx:
            xg = sb(ctx, "xg", [P, 2, D])
            xgT = sb(ctx, "xgT", [P, 2, DC, P])
            silu = sb(ctx, "silu", [P, 2, DE])
            hid = sb(ctx, "hid", [P, 2, DE])
            hidT = sb(ctx, "hidT", [P, 2, DE // P, P])
            yy = sb(ctx, "yy", [P, 2, D])
            ys_v = ys_dram.rearrange("(e p) n -> e p n", p=P)
            f_x = [sem(ctx, f"f_x{i}") for i in range(2)]
            f_tx = sem(ctx, "f_tx")
            f_xa = sem(ctx, "f_xa")
            f_xv = sem(ctx, "f_xv")
            f_g = sem(ctx, "f_g")
            f_u = sem(ctx, "f_u")
            f_silu = sem(ctx, "f_silu")
            f_hid = sem(ctx, "f_hid")
            f_th = sem(ctx, "f_th")
            f_ht = sem(ctx, "f_ht")
            f_d = sem(ctx, "f_d")
            f_ya = sem(ctx, "f_ya")
            f_yv = sem(ctx, "f_yv")
            f_st = [sem(ctx, f"f_st{i}") for i in range(2)]
            x_st = sem(ctx, "x_st")

            def steps(eng, step):
                step(0, 0, 0)
                step(1, 1, 0)
                step(2, 0, 1)
                with eng.Fori(1, (NE - 2) // 2) as i:
                    step(2 * i + 1, 1, i)
                    step(2 * i + 2, 0, i + 1)
                step(NE - 1, 1, (NE - 2) // 2)

            def at_least(e, n):
                return e >= n if type(e) is int else n <= 1

            def extras(eng, body):
                n = eng.value_load(exi[0:1, MAXEXTRA:MAXEXTRA + 1], min_val=0, max_val=MAXEXTRA)
                for b in range(2):
                    with eng.If(n > b):
                        body(NE + b, b, NE // 2)
                with eng.Fori(1, MAXEXTRA // 2) as i:
                    for b in range(2):
                        with eng.If(n > 2 * i + b):
                            body(2 * i + NE + b, b, i + NE // 2)
                return n

            def gate_mm(b):
                for k in range(DC):
                    last = nc.tensor.matmul(bank[2], xgT[:, b, k, :], wg[:, b, k, :], start=(k == 0), stop=(k == DC - 1))
                return last

            def up_mm(b):
                for k in range(DC):
                    last = nc.tensor.matmul(bank[3], xgT[:, b, k, :], wu[:, b, k, :], start=(k == 0), stop=(k == DC - 1))
                return last

            def down_mm(b):
                for half in range(2):
                    for k in range(KD):
                        last = nc.tensor.matmul(bank[4 + half], hidT[:, b, k, :], wd[:, b, k, half * 512:(half + 1) * 512],
                                                start=(k == 0), stop=(k == KD - 1))
                return last

            def x_transposes(b):
                x = xg[:, b, :].rearrange("p (m k) -> p k m", k=DC)
                for k in range(DC):
                    last = nc.tensor.transpose(bank[1 if k < 4 else 7][:, (k % 4) * P:(k % 4 + 1) * P], x[:, k, :], c("ident"))
                return last

            def hid_transposes(b):
                h = hid[:, b, :].rearrange("p (m k) -> p k m", k=KD)
                for k in range(KD):
                    last = nc.tensor.transpose(bank[0][:, k * P:(k + 1) * P], h[:, k, :], c("ident"))
                return last

            with nc.Block() as block:
                @block.sync
                def _(sp):
                    sp.dma_start(vec2["gate2"][:, :], mod_dram[0, 5 * D:6 * D].partition_broadcast(P)).then_inc(x_st, 16)
                    for n in ("ln2_g", "ln2_b"):
                        sp.dma_start(vec2[n][:, :], a[n][0].partition_broadcast(P)).then_inc(g_v, 16)
                    with sp.Fori(0, (NE - 2) // 2) as i:
                        for b in range(2):
                            e = 2 * i + b
                            for n, w, used in (("g", wg, f_g), ("u", wu, f_u), ("d", wd, f_d)):
                                src = {"g": wg_v, "u": wu_v, "d": wd_v}[n][bass.ds(e + 2, 1), :, :, :].rearrange("e p k n -> p (e k) n")
                                sp.wait_ge(used, e + 1)
                                sp.dma_start(w[:, b, :, :], src).then_inc(f_w[n][b], 16)

                    def extra(e, b, half):
                        owner = sp.value_load(exi[0:1, bass.ds(e - NE, 1)], min_val=0, max_val=NE - 1)
                        for n, w, view, used in (("g", wg, wg_v, f_g), ("u", wu, wu_v, f_u), ("d", wd, wd_v, f_d)):
                            sp.wait_ge(used, e - 1)
                            sp.dma_start(w[:, b, :, :], view[bass.ds(owner, 1), :, :, :].rearrange("e p k n -> p (e k) n")).then_inc(f_w[n][b], 16)
                    n = extras(sp, extra)
                    sp.wait_ge(x_st, 16 * (n + 1))
                    for t in range(4):
                        sp.dma_start(x1[:, t, :], x1_dram[t * P:(t + 1) * P, :]).then_inc(g_x[t], 16)

                @block.gpsimd
                def _(pool):
                    for e in range(NE):
                        if e >= 2:
                            pool.wait_ge(f_tx, e - 1)
                        nc.gpsimd.indirect_dma_start(out=xg[:, e % 2, :], out_offset=None, in_=h2_dram[:, :],
                                                     in_offset=bass.IndirectOffsetOnAxis(ap=tokens[:, e:e + 1].bitcast(U32), axis=0)).then_inc(f_x[e % 2], 16)
                    n = pool.value_load(exi[0:1, MAXEXTRA:MAXEXTRA + 1], min_val=0, max_val=MAXEXTRA)
                    for i in range(MAXEXTRA):
                        with pool.If(n > i):
                            pool.wait_ge(f_tx, NE + i - 1)
                            nc.gpsimd.indirect_dma_start(out=xg[:, i % 2, :], out_offset=None, in_=h2_dram[:, :],
                                                         in_offset=bass.IndirectOffsetOnAxis(ap=tokens[:, NE + i:NE + i + 1].bitcast(U32), axis=0)).then_inc(f_x[i % 2], 16)

                @block.tensor
                def _(pe):
                    pe.wait_ge(f_x[0], 16)
                    x_transposes(0).then_inc(f_tx, 1)

                    def step(e, b, half):
                        pe.wait_ge(f_xa, e + 1)
                        pe.wait_ge(f_xv, e + 1)
                        pe.wait_ge(f_w["g"][b], 16 * (half + 1))
                        if at_least(e, 1):
                            pe.wait_ge(f_silu, e)
                        gate_mm(b).then_inc(f_g, 1)
                        if at_least(e, 1):
                            pe.wait_ge(f_hid, e)
                            hid_transposes(1 - b).then_inc(f_th, 1)
                        pe.wait_ge(f_w["u"][b], 16 * (half + 1))
                        up_mm(b).then_inc(f_u, 1)
                        if not (type(e) is int and e == NE - 1):
                            pe.wait_ge(f_x[1 - b], 16 * (half + 1 + b))
                            x_transposes(1 - b).then_inc(f_tx, 1)
                        if at_least(e, 1):
                            down(e, 1 - b, half + (b - 1))

                    def down(e, b, half):
                        pe.wait_ge(f_ht, e)
                        pe.wait_ge(f_w["d"][b], 16 * (half + 1))
                        if type(e) is not int or e >= 2:
                            pe.wait_ge(f_ya, e - 1)
                            pe.wait_ge(f_yv, e - 1)
                        down_mm(b).then_inc(f_d, 1)

                    steps(pe, step)
                    pe.wait_ge(f_hid, NE)
                    hid_transposes(1).then_inc(f_th, 1)
                    down(NE, 1, NE // 2 - 1)

                    def extra(e, b, half):
                        pe.wait_ge(f_x[b], 16 * (half + 1))
                        x_transposes(b).then_inc(f_tx, 1)
                        pe.wait_ge(f_xa, e + 1)
                        pe.wait_ge(f_xv, e + 1)
                        pe.wait_ge(f_w["g"][b], 16 * (half + 1))
                        gate_mm(b).then_inc(f_g, 1)
                        pe.wait_ge(f_w["u"][b], 16 * (half + 1))
                        up_mm(b).then_inc(f_u, 1)
                        pe.wait_ge(f_hid, e + 1)
                        hid_transposes(b).then_inc(f_th, 1)
                        pe.wait_ge(f_ht, e + 1)
                        pe.wait_ge(f_w["d"][b], 16 * (half + 1))
                        pe.wait_ge(f_ya, e)
                        pe.wait_ge(f_yv, e)
                        down_mm(b).then_inc(f_d, 1)
                    extras(pe, extra)

                @block.scalar
                def _(act):
                    s = nc.scalar

                    def x_part(e, b):
                        act.wait_ge(f_tx, e + 1)
                        s.activation(xgT[:, b, 0:4, :], bank[1], ACT.Copy).then_inc(f_xa, 1)

                    def hid_part(e, b):
                        act.wait_ge(f_th, e)
                        s.activation(hidT[:, b, :, :], bank[0], ACT.Copy).then_inc(f_ht, 1)

                    def y_part(e, b, half):
                        act.wait_ge(f_d, e)
                        if type(e) is not int or e >= 3:
                            act.wait_ge(f_st[b], 16 * half)
                        s.activation(yy[:, b, 0:512], bank[4], ACT.Copy).then_inc(f_ya, 1)
                        act.wait_ge(f_ya, e)
                        act.wait_ge(f_yv, e)
                        dst = ys_v[e - 1] if type(e) is int else ys_v[bass.ds(e - 1, 1), :, :].rearrange("e p n -> p (e n)")
                        act.dma_start(dst, yy[:, b, :]).then_inc(f_st[b], 16)

                    x_part(0, 0)

                    def step(e, b, half):
                        act.wait_ge(f_g, e + 1)
                        s.activation(silu[:, b, :], bank[2], ACT.Silu).then_inc(f_silu, 1)
                        if at_least(e, 1):
                            hid_part(e, 1 - b)
                        if not (type(e) is int and e == NE - 1):
                            x_part(e + 1, 1 - b)
                        if at_least(e, 1):
                            y_part(e, 1 - b, half + b - 1)

                    steps(act, step)
                    hid_part(NE, 1)
                    y_part(NE, 1, NE // 2 - 1)
                    for b in range(2):
                        act.wait_ge(f_st[b], 16 * NE // 2)

                    def extra(e, b, half):
                        x_part(e, b)
                        act.wait_ge(f_g, e + 1)
                        s.activation(silu[:, b, :], bank[2], ACT.Silu).then_inc(f_silu, 1)
                        hid_part(e + 1, b)
                        act.wait_ge(x_st, 16 * (e - NE + 1))
                        act.wait_ge(f_d, e + 1)
                        s.activation(yy[:, b, 0:512], bank[4], ACT.Copy).then_inc(f_ya, 1)
                        act.wait_ge(f_ya, e + 1)
                        act.wait_ge(f_yv, e + 1)
                        dst = ys_v[e] if type(e) is int else ys_v[bass.ds(e, 1), :, :].rearrange("e p n -> p (e n)")
                        act.dma_start(dst, yy[:, b, :]).then_inc(x_st, 16)
                    extras(act, extra)

                @block.vector
                def _(dve):
                    v = nc.vector

                    def x_part(e, b):
                        dve.wait_ge(f_tx, e + 1)
                        v.tensor_copy(xgT[:, b, 4:8, :], bank[7]).then_inc(f_xv, 1)

                    def y_part(e, b, half):
                        dve.wait_ge(f_d, e)
                        if type(e) is not int or e >= 3:
                            dve.wait_ge(f_st[b], 16 * half)
                        v.tensor_copy(yy[:, b, 512:1024], bank[5]).then_inc(f_yv, 1)

                    x_part(0, 0)

                    def step(e, b, half):
                        dve.wait_ge(f_silu, e + 1)
                        dve.wait_ge(f_u, e + 1)
                        v.tensor_tensor(hid[:, b, :], silu[:, b, :], bank[3], ALU.mult).then_inc(f_hid, 1)
                        if not (type(e) is int and e == NE - 1):
                            x_part(e + 1, 1 - b)
                        if at_least(e, 1):
                            y_part(e, 1 - b, half + b - 1)

                    steps(dve, step)
                    y_part(NE, 1, NE // 2 - 1)

                    def extra(e, b, half):
                        x_part(e, b)
                        dve.wait_ge(f_silu, e + 1)
                        dve.wait_ge(f_u, e + 1)
                        v.tensor_tensor(hid[:, b, :], silu[:, b, :], bank[3], ALU.mult).then_inc(f_hid, 1)
                        if type(e) is int:
                            dve.wait_ge(f_st[b], 16 * NE // 2)
                        else:
                            dve.wait_ge(x_st, 16 * (e - NE))
                        dve.wait_ge(f_d, e + 1)
                        v.tensor_copy(yy[:, b, 512:1024], bank[5]).then_inc(f_yv, 1)
                    extras(dve, extra)

        weights.close()
        with ExitStack() as ctx:
            y1 = sb(ctx, "y1", [P, 4, D])
            y2 = sb(ctx, "y2", [P, 4, D])
            gate2_s = sb(ctx, "gate2_s", [NS, D])
            stat = sb(ctx, "stat2", [P, 2, 6])
            mv = sb(ctx, "mv2", [P, 2, 2])
            y_tile = [outs[0][0, t * P:(t + 1) * P, :] for t in range(TILES)] + [outs[1].rearrange("b t d -> (b t) d")]
            g_gv = sem(ctx, "g_gv")
            g_y = [sem(ctx, f"g_y{i}") for i in range(4)]
            g_dve = sem(ctx, "g_dve")
            g_w1 = sem(ctx, "g_w1")
            g_both = sem(ctx, "g_both")
            g_gated = sem(ctx, "g_gated")
            g_sum = sem(ctx, "g_sum")
            g_mv = sem(ctx, "g_mv")
            g_ctr = sem(ctx, "g_ctr")
            g_eps = sem(ctx, "g_eps")
            g_rs = sem(ctx, "g_rs")
            g_norm = sem(ctx, "g_norm")
            g_out = sem(ctx, "g_out")
            g_st = [sem(ctx, f"g_st{i}") for i in range(4)]

            with nc.Block() as block:
                @block.sync
                def _(sp):
                    for i in range(SEQS):
                        sp.dma_start(gate2_s[i * DSEQ:(i + 1) * DSEQ, :],
                                     mod_dram[1 + i, 5 * D:6 * D].partition_broadcast(DSEQ)).then_inc(g_gv, 16)
                    for t in range(TA):
                        r = rows(t)
                        sp.wait_ge(g_x[t % 4], 16 * (t // 4 + 1))
                        sp.wait_ge(g_out, t + 1)
                        sp.dma_start(y_tile[t], x1[0:r, t % 4, :]).then_inc(g_st[t % 4], 16)
                        if t + 4 < TA:
                            sp.wait_ge(g_st[t % 4], 16 * (t // 4 + 1))
                            r4 = rows(t + 4)
                            sp.dma_start(x1[0:r4, t % 4, :], x1_dram[(t + 4) * P:(t + 4) * P + r4, :]).then_inc(g_x[t % 4], 16)
                    for i in range(4):
                        sp.wait_ge(g_st[i], 16 * len(range(i, TA, 4)))

                @block.gpsimd
                def _(pool):
                    g = nc.gpsimd

                    def gather(t):
                        r = rows(t)
                        for k, y in enumerate((y1, y2)):
                            g.indirect_dma_start(out=y[0:r, t % 4, :], out_offset=None, in_=ys_dram[:, :],
                                                 in_offset=bass.IndirectOffsetOnAxis(ap=slot[0:r, k, t:t + 1].bitcast(U32), axis=0)).then_inc(g_y[t % 4], 16)

                    for t in range(3):
                        gather(t)
                    for t in range(TA + 2):
                        if t < TA:
                            r, f = rows(t), y1[0:rows(t), t % 4, :]
                            pool.wait_ge(g_both, t + 1)
                            if t == TILES:
                                pool.wait_ge(g_gv, 16 * SEQS)
                            gate = vec2["gate2"] if t < TILES else gate2_s
                            g.tensor_tensor(f, f, gate[0:r, :], ALU.mult).then_inc(g_gated, 1)
                        if 1 <= t <= TA:
                            r, b = rows(t - 1), (t - 1) % 2
                            pool.wait_ge(g_mv, t)
                            g.tensor_scalar(mv[0:r, b, 1:2], mv[0:r, b, 1:2], EPS, None, ALU.add).then_inc(g_eps, 1)
                            pool.wait_ge(g_eps, t)
                            g.tensor_tensor(mv[0:r, b, 1:2], mv[0:r, b, 1:2], c("minushalf", r)[:, 0:1], ALU.pow).then_inc(g_rs, 1)
                        if t + 3 < TA:
                            gather(t + 3)
                        if t >= 2:
                            r = rows(t - 2)
                            x = x1[0:r, (t - 2) % 4, :]
                            pool.wait_ge(g_norm, t - 1)
                            g.tensor_tensor(x, x, vec2["ln2_b"][0:r, :], ALU.add).then_inc(g_out, 1)

                @block.scalar
                def _(act):
                    for t in range(TA + 2):
                        if t < TA:
                            r, b = rows(t), t % 4
                            act.wait_ge(g_y[b], 32 * (t // 4 + 1))
                            nc.scalar.activation(y1[0:r, b, :], y1[0:r, b, :], ACT.Copy, scale=weight[0:r, 0, t:t + 1]).then_inc(g_w1, 1)
                        if t >= 2:
                            r, x = rows(t - 2), x1[0:rows(t - 2), (t - 2) % 4, :]
                            act.wait_ge(g_ctr, t - 1)
                            act.wait_ge(g_rs, t - 1)
                            nc.scalar.activation(x, x, ACT.Copy, scale=mv[0:r, t % 2, 1:2]).then_inc(g_norm, 1)

                @block.vector
                def _(dve):
                    v = nc.vector
                    count = [0]

                    def then(ins):
                        count[0] += 1
                        ins.then_inc(g_dve, 1)
                        dve.wait_ge(g_dve, count[0])

                    for t in range(TA + 1):
                        if t < TA:
                            r, b = rows(t), t % 4
                            dve.wait_ge(g_w1, t + 1)
                            dve.wait_ge(g_y[b], 32 * (t // 4 + 1))
                            v.scalar_tensor_tensor(out=y1[0:r, b, :], in0=y2[0:r, b, :], scalar=weight[0:r, 1, t:t + 1],
                                                   in1=y1[0:r, b, :], op0=ALU.mult, op1=ALU.add).then_inc(g_both, 1)
                        if t >= 1:
                            r, b = rows(t - 1), (t - 1) % 4
                            f, x, m = y1[0:r, b, :], x1[0:r, b, :], mv[0:r, (t - 1) % 2, :]
                            dve.wait_ge(g_gated, t)
                            dve.wait_ge(g_x[b], 16 * ((t - 1) // 4 + 1))
                            then(v.scalar_tensor_tensor(out=x, in0=x, scalar=ALPHA, in1=f, op0=ALU.mult, op1=ALU.add))
                            v.bn_stats(stat[0:r, 0, :], x[:, 0:512])
                            then(v.bn_stats(stat[0:r, 1, :], x[:, 512:1024]))
                            if t >= 3:
                                dve.wait_ge(g_norm, t - 2)
                            v.bn_aggr(m, stat[0:r, :, :]).then_inc(g_mv, 1)
                            dve.wait_ge(g_mv, t)
                            v.scalar_tensor_tensor(out=x, in0=x, scalar=m[:, 0:1], in1=vec2["ln2_g"][0:r, :],
                                                   op0=ALU.subtract, op1=ALU.mult).then_inc(g_ctr, 1)


_INS = ['x_prompt', 'x_sample', 'cache_k', 'cache_v', 'cache_kidx', 'page_table', 'c_prompt', 'c_sample',
        'w_ada', 'b_ada', 'w_in', 'a_ln_g', 'a_ln_b', 'w_spatial', 'b_spatial', 'w_out', 'ln1_g', 'ln1_b',
        'w_group_router', 'w_expert_router', 'w_gate', 'w_up', 'w_down', 'ln2_g', 'ln2_b']
_OUTS = [(1, SEQ, D), (SEQS, DSEQ, D), (1, 1, SEQ, KVH, HD), (1, 1, SEQ, KVH, HD), (1, 1, SEQ, HD),
         (1, SEQS, DSEQ, KVH, HD), (1, SEQS, DSEQ, KVH, HD), (1, SEQS, DSEQ, HD), (1, SEQS, DSEQ, AH, HD)]


def kernel(**inputs):
    import concourse.bacc as _bacc
    from concourse.bass_utils import run_bass_kernel_spmd as _run

    nc = _bacc.Bacc("TRN2", target_bir_lowering=False, num_devices=1)
    arrays, args = {}, {}
    given = {name: np.ascontiguousarray(inputs[name]) for name in _INS}
    given["table"] = constants()[1]
    for name, x in given.items():
        arrays[f"in_{name}_dram"] = x
        args[name] = nc.dram_tensor(f"in_{name}_dram", x.shape, mybir.dt.from_np(x.dtype), kind="ExternalInput").ap()
    outs = [nc.dram_tensor(f"out_{i}_dram", shape, F32, kind="ExternalOutput").ap() for i, shape in enumerate(_OUTS)]
    step_kernel(nc, args, outs)
    r = _run(nc, [arrays], core_ids=[0])
    return tuple(r.results[0][f"out_{i}_dram"] for i in range(len(_OUTS)))
```

```python
from contextlib import ExitStack

import numpy as np
import concourse.bass as bass
from concourse import mybir

F32 = mybir.dt.float32
I32 = mybir.dt.int32
U32 = mybir.dt.uint32
ALU = mybir.AluOpType
ACT = mybir.ActivationFunctionType
AX = mybir.AxisListType.X

P = 128
D = 1024
DC = D // P
SEQ = 1024
SEQS, DSEQ = 8, 4
NS = SEQS * DSEQ
TILES = SEQ // P
TOK = SEQ + NS
HD = 64
AH = 8
QH, KVH, IH = 8, 4, 4
PAST, PAGE = 512, 128
NPG = PAST // PAGE
TOPK_P, TOPK_S = 256, (PAST + DSEQ) // 4
HALF = 8
THETA = 500000.0
NG, EPG = 4, 8
NE = NG * EPG
DE = 512
ALPHA = 2.0 ** 0.25
EPS = 1e-5
NEG_MASK = -1.0e30
NEG_INADM = -3.0e38
NEG_TAKEN = -3.4e38
MAXEXTRA = (2 * TOK) // P
SLOTS = NE + MAXEXTRA

GROUPS = [("idx", 2048, 324), ("q", 1024, 512), ("av", 512, 512), ("kv", 1536, 512), ("au", 0, 512)]


SEARCH = 32
ROUTING = ("before", "ones", "iota", "token", "valid", "steps", "first")
BIG = 3.0e38


def rows(t):
    return P if t < TILES else NS


def constants():
    p = np.arange(P)
    inv = np.float32(THETA) ** (-np.arange(HALF, dtype=np.float32) * np.float32(2.0) / np.float32(2 * HALF))
    pos = np.zeros((P, TILES + 1), np.float32)
    for t in range(TILES):
        pos[:, t] = t * P + p
    pos[:, TILES] = PAST + p % DSEQ
    ang = (pos[:, :, None] * inv[None, None, :]).astype(np.float32)
    own = (p[:, None] % NS // DSEQ == np.arange(SEQS)[None]).astype(np.float32)
    blk = np.zeros((P, NS))
    blk[:NS] = (p[:NS, None] // DSEQ == p[None, :NS] // DSEQ) & (p[:NS, None] >= p[None, :NS])
    later = p[None, :] > p[:, None]
    newer = np.arange(DSEQ)[None] > (p % DSEQ)[:, None]
    c = {
        "ident": np.eye(P),
        "before": p[:, None] < p[None],
        "ones": np.ones((P, P)),
        "sametok": p[:, None] % NS == p[None] % NS,
        "cos": np.cos(ang), "sin": np.sin(ang),
        "later": later,
        "newneg": newer * NEG_INADM,
        "tril": p[:, None] >= p[None],
        "blktril": blk,
        "seqcol": np.broadcast_to((p[None, None, :NS] // DSEQ == np.arange(SEQS)[None, :, None]), (P, SEQS, NS)),
        "own": own,
        "iota": np.broadcast_to(p[None], (P, P)),
        "token": (np.arange(TILES + 1)[None] * P + p[:, None]) * ((np.arange(TILES + 1)[None] < TILES) | (p[:, None] < NS)),
        "valid": np.concatenate([np.ones((P, TILES)), (p < NS)[:, None]], axis=1),
        "steps": np.broadcast_to(P * np.arange(1, 9)[None], (P, 8)),
        "first": np.broadcast_to(8 - np.arange(8)[None], (P, 8)),
        "one": np.ones((P, 1)),
        "minushalf": np.full((P, 16), -0.5),
    }
    c["halvings"] = np.broadcast_to(2.0 ** (1 - np.arange(SEARCH + 1))[None], (P, SEARCH + 1))
    order = [k for k in c if k not in ROUTING] + [k for k in c if k in ROUTING]
    at, parts, n = {}, [], 0
    for k, v in ((k, c[k]) for k in order):
        v = np.ascontiguousarray(v, dtype=np.float32).reshape(P, -1)
        at[k] = (n, v.shape[1])
        n += v.shape[1]
        parts.append(v)
    return at, np.concatenate(parts, axis=1)


def step_kernel(nc, a, outs):
    at, table = constants()
    xs = a["x_sample"].rearrange("b t d -> (b t) d")
    x_tile = [a["x_prompt"][0, t * P:(t + 1) * P, :] for t in range(TILES)] + [xs]
    w_in = a["w_in"][0].rearrange("(c p) n -> p c n", p=P)
    w_ada = a["w_ada"][0].rearrange("(c p) n -> p c n", p=P)
    b_ada = a["b_ada"][0]
    new_k = [outs[2].rearrange("a b t h d -> (a b t) (h d)")[t * P:(t + 1) * P, :] for t in range(TILES)] + \
            [outs[5].rearrange("a b t h d -> (a b t) (h d)")]
    new_v = [outs[3].rearrange("a b t h d -> (a b t) (h d)")[t * P:(t + 1) * P, :] for t in range(TILES)] + \
            [outs[6].rearrange("a b t h d -> (a b t) (h d)")]
    new_kidx = [outs[4].rearrange("a b t d -> (a b t) d")[t * P:(t + 1) * P, :] for t in range(TILES)] + \
               [outs[7].rearrange("a b t d -> (a b t) d")]
    chunk_v = outs[8].rearrange("a b t h d -> (a b t) (h d)")

    mod_dram = nc.dram_tensor("mod_dram", (1 + SEQS, 6 * D), F32).ap()

    x1_dram = nc.dram_tensor("x1_dram", (TOK, D), F32).ap()
    h2_dram = nc.dram_tensor("h2_dram", (TOK, D), F32).ap()
    ys_dram = nc.dram_tensor("ys_dram", (SLOTS * P, D), F32).ap()

    with ExitStack() as keep, ExitStack() as tail:
        def sb(ctx, name, shape, dt=F32):
            return ctx.enter_context(nc.sbuf_tensor(name, shape, dt))

        def sem(ctx, name):
            return ctx.enter_context(nc.semaphore(name))

        psum = keep.enter_context(nc.psum_tensor("psum", [P, 8 * 512], F32))
        bank = [psum[:, 512 * i:512 * (i + 1)] for i in range(8)]
        banks56 = psum[:, 5 * 512:7 * 512]
        early = at[ROUTING[0]][0]
        const = sb(keep, "const", [P, early])
        consts = [const]

        def c(name, r=P):
            n, w = at[name]
            return consts[0][0:r, n:n + w] if n < early else consts[1][0:r, n - early:n - early + w]

        logit = sb(keep, "logit", [P, TILES + 1, NG + NE])

        q_nat = sb(tail, "q_nat", [P, TILES + 1, QH * HD])
        kT = sb(tail, "kT", [P, 2, TOK])
        kiT = sb(tail, "kiT", [HD, TOK])
        v_nat = sb(tail, "v_nat", [P, TILES + 1, KVH * HD])
        mixa = sb(tail, "mixa", [P, 4, TOK])
        bias_at = [P * (t * (t + 1) // 2 - 3) for t in range(TILES)]
        bias = sb(tail, "bias", [P, bias_at[TILES - 1] + P * TILES])
        qi_s = sb(tail, "qi_s", [HD, IH, NS])
        w_i = sb(tail, "w_i", [P, TILES + 1, IH])
        above = sb(tail, "above", [P, SEQ], mybir.dt.int8)
        near = sb(tail, "near", [P, SEQ], mybir.dt.int8)
        steps_ = sb(tail, "steps_", [P, 2, SEARCH + 1])
        low = sb(tail, "low", [P, 2])
        cand = sb(tail, "cand", [P, 2])
        under = sb(tail, "under", [P, 2])
        miss = sb(tail, "miss", [P, 2])
        nabove = sb(tail, "nabove", [P, 2])
        cT = sb(tail, "cT", [P, DC, 1 + SEQS])
        s_cand = sem(tail, "s_cand")
        s_under = sem(tail, "s_under")

        def score_of(b):
            return bias[:, bias_at[b]:bias_at[b] + (b + 1) * P]

        def search_begin(dve, v, then, m):
            for k in range(2):
                b = 2 * m + k
                score = score_of(b)
                diag = score[:, b * P:(b + 1) * P]
                then(v.tensor_reduce(low[:, k:k + 1], score, AX, ALU.max, apply_absolute_value=True))
                then(v.scalar_tensor_tensor(out=diag, in0=c("later"), scalar=NEG_INADM, in1=diag, op0=ALU.mult, op1=ALU.add))
            then(v.tensor_scalar(low[:, :].bitcast(I32), low[:, :].bitcast(I32), 0x7F800000, None, ALU.bitwise_and))
            for k in range(2):
                then(v.tensor_scalar(steps_[:, k, :], c("halvings"), low[:, k:k + 1], None, ALU.mult))
            then(v.tensor_scalar(low[:, :], steps_[:, :, 0], -1.0, None, ALU.mult))
            v.tensor_tensor(cand[:, :], low[:, :], steps_[:, :, 0], ALU.add).then_inc(s_cand, 1)
            dve.wait_ge(s_cand, SEARCH * (m - 1) + 1)

        def search_count(dve, v, then, m):
            na, nb = (2 * m + 1) * P, (2 * m + 2) * P
            bound = float(nb - 2 * TOPK_P + 1)
            then(v.tensor_scalar(above[:, 0:na], score_of(2 * m), cand[:, 0:1], bound - (na - TOPK_P), ALU.is_lt, ALU.add,
                                 accum_out=under[:, 0:1]))

        def search_step(dve, v, then, m, i):
            bound = float((2 * m + 2) * P - 2 * TOPK_P + 1)
            dve.wait_ge(s_under, SEARCH * (m - 1) + i + 1)
            then(v.tensor_scalar(miss[:, :], under[:, :], bound, -BIG, ALU.is_gt, ALU.mult))
            then(v.tensor_tensor(miss[:, :], cand[:, :], miss[:, :], ALU.add))
            then(v.tensor_tensor(low[:, :], low[:, :], miss[:, :], ALU.max))
            if i + 1 < SEARCH:
                v.tensor_tensor(cand[:, :], low[:, :], steps_[:, :, i + 1], ALU.add).then_inc(s_cand, 1)
                dve.wait_ge(s_cand, SEARCH * (m - 1) + i + 2)

        def search_count_act(act, s, m, i):
            b = 2 * m + 1
            keys = (b + 1) * P
            act.wait_ge(s_cand, SEARCH * (m - 1) + i + 1)
            s.activation(near[:, 0:keys], bias[:, bias_at[b]:bias_at[b] + keys], ACT.Sign, bias=cand[:, 1:2], scale=-1.0,
                         accum_out=under[:, 1:2]).then_inc(s_under, 1)

        def search_end(dve, v, then, m):
            then(v.tensor_tensor(cand[:, :], low[:, :], steps_[:, :, SEARCH - 1], ALU.add))
            then(v.tensor_scalar(miss[:, 1:2].bitcast(I32), low[:, 1:2].bitcast(I32), 0x7FFFFFFF, None, ALU.bitwise_and))
            then(v.scalar_tensor_tensor(out=miss[:, 1:2], in0=miss[:, 1:2], scalar=2.0 ** -23, in1=low[:, 1:2], op0=ALU.mult, op1=ALU.add))
            then(v.tensor_tensor(cand[:, 1:2], cand[:, 1:2], miss[:, 1:2], ALU.max))

        PICK = 7

        def pick(dve, v, then, m, k, part):
            b = 2 * m + k
            n = (b + 1) * P
            score, a_, n_, count_ = score_of(b), above[:, 0:n], near[:, 0:n], nabove[:, k:k + 1]
            if part == 0:
                ins = v.tensor_scalar(a_, score, cand[:, k:k + 1], 0.0, ALU.is_gt, ALU.add, accum_out=count_)
            elif part == 1:
                ins = v.scalar_tensor_tensor(out=n_, in0=score, scalar=low[:, k:k + 1], in1=a_, op0=ALU.is_ge, op1=ALU.subtract)
            elif part == 2:
                ins = v.tensor_scalar(count_, count_, -1.0, float(TOPK_P), ALU.mult, ALU.add)
            elif part == 3:
                ins = v.tensor_tensor_scan(score, c("one").to_broadcast([P, n]), n_, 0.0, ALU.mult, ALU.add)
            elif part == 4:
                ins = v.scalar_tensor_tensor(out=n_, in0=score, scalar=count_, in1=n_, op0=ALU.is_le, op1=ALU.mult)
            elif part == 5:
                ins = v.tensor_tensor(a_, a_, n_, ALU.add)
            else:
                ins = v.tensor_scalar(score, a_, -1.0, -NEG_MASK, ALU.add, ALU.mult)
            then(ins)

        with ExitStack() as ctx:
            w_sb = sb(ctx, "w_sb", [P, DC, 2372])
            ada_at = [q_nat[:, :, :].rearrange("p t n -> p (t n)")[:, 0:4096].rearrange("p (c n) -> p c n", c=DC),
                      mixa[:, :, :].rearrange("p t n -> p (t n)")[:, 0:4096].rearrange("p (c n) -> p c n", c=DC),
                      w_sb[:, :, 0:512], w_sb[:, :, 512:1024]]
            x_nat = sb(ctx, "x_nat", [P, 2, D])
            hT = sb(ctx, "hT", [P, 2, DC, P])
            scale1 = sb(ctx, "scale1", [P, D])
            shift1 = sb(ctx, "shift1", [P, D])
            idx_nat = sb(ctx, "idx_nat", [P, 2, 324])
            k_nat = sb(ctx, "k_nat", [P, 2, KVH * HD])
            u = sb(ctx, "u", [P, 2, 512])
            vg = sb(ctx, "vg", [P, 2, 512])
            spat = sb(ctx, "spat", [P, 512])
            tmp = sb(ctx, "tmp", [P, 512])
            rot = tmp[:, 0:4 * QH * HALF].rearrange("p (i n) -> p i n", i=4)
            st8 = sb(ctx, "st8", [P, 3, AH])
            wspT = sb(ctx, "wspT", [P, AH, P])
            wsb4 = sb(ctx, "wsb4", [NS, AH, DSEQ])
            wsbd = tmp[0:NS, 0:AH * NS].rearrange("p (h t) -> p h t", h=AH)
            wsbdT = sb(ctx, "wsbdT", [NS, AH, NS])
            bsp = sb(ctx, "bsp", [P, AH])
            bsp_s = sb(ctx, "bsp_s", [NS, AH])
            aln_g = sb(ctx, "aln_g", [P, 512])
            aln_b = sb(ctx, "aln_b", [P, 512])
            qiT = sb(ctx, "qiT", [HD, IH, P])
            cnat = x_nat[0:1 + SEQS, 0, :]
            modn = [x[0:1 + SEQS, i, :] for x in (u, vg) for i in range(2)]
            wsp = hT[:, 0, :, :]

            s_const = sem(ctx, "s_const")
            s_c = sem(ctx, "s_c")
            s_silu = sem(ctx, "s_silu")
            s_ada = [sem(ctx, f"s_ada{i}") for i in range(4)]
            s_adamm = sem(ctx, "s_adamm")
            s_modn = sem(ctx, "s_modn")
            s_modst = sem(ctx, "s_modst")
            s_win = [sem(ctx, f"s_win{g}") for g in range(5)]
            s_bc = sem(ctx, "s_bc")
            s_sp = sem(ctx, "s_sp")
            s_aln = sem(ctx, "s_aln")
            s_tril = sem(ctx, "s_tril")
            s_x = [sem(ctx, f"s_x{i}") for i in range(2)]
            s_h = sem(ctx, "s_h")
            s_trf = sem(ctx, "s_trf")
            s_tre = sem(ctx, "s_tre")
            s_mm = sem(ctx, "s_mm")
            s_ev = sem(ctx, "s_ev")
            s_rot = sem(ctx, "s_rot")
            s_ln = sem(ctx, "s_ln")
            s_idxp = sem(ctx, "s_idxp")
            s_relu = sem(ctx, "s_relu")
            s_acc = sem(ctx, "s_acc")
            s_spm = sem(ctx, "s_spm")
            s_spe = sem(ctx, "s_spe")
            s_am = sem(ctx, "s_am")
            s_st = [sem(ctx, f"s_st{i}") for i in range(2)]
            s_stv = sem(ctx, "s_stv")
            dvec = sem(ctx, "dvec")
            poolc = sem(ctx, "poolc")
            IDX0 = 2
            RATE = {"group": 3, "score": 1, "mix": 2, "post": 1, "aT": 1}
            CH = [2, 3, 0, 1, 4, 5, 6, 7, 8, 9, 10, 11]

            TR = [("c", 0, 0)] + [("sp", 0, i) for i in range(2)] + [("spbd", 0, 0)] + [("h", 0, 0), ("h", 0, 1)]
            STEPS = []
            for t in range(TILES + 3):
                if t <= TILES:
                    STEPS.append(("group", t, 0))
                    if t + 1 <= TILES:
                        STEPS.append(("h", t + 1, 0))
                    STEPS.append(("group", t, 1))
                if 1 <= t <= TILES + 1:
                    STEPS.append(("post", t - 1, 0))
                if t <= TILES:
                    STEPS.append(("group", t, 2))
                if 3 <= t <= TILES:
                    STEPS += [("score", t - 1, 0), ("score", t - 1, 1)]
                if 2 <= t:
                    STEPS.append(("aT", t - 2, 0))
                if t <= TILES:
                    STEPS.append(("group", t, 3))
                if 3 <= t <= TILES:
                    STEPS += [("score", t - 1, 2), ("score", t - 1, 3)]
                if t <= TILES:
                    STEPS.append(("group", t, 4))
                if 1 <= t <= TILES + 1:
                    STEPS.append(("mix", t - 1, 0))
            merged, queue = [], []
            for x in STEPS:
                merged.append(x)
                if x[0] == "score" and x[2] == IH - 1 and x[1] in (3, 5):
                    m = x[1] // 2
                    queue += [("begin", m, 0)] + [("try", m, i) for i in range(SEARCH)] + [("end", m, 0)]
                    queue += [("pick", m, i) for i in range(2 * PICK)]
                rate = RATE.get(x[0], 0)
                merged += queue[0:rate]
                queue = queue[rate:]
            STEPS = merged + queue
            for kind, t, _ in STEPS:
                if kind == "h" or kind == "post":
                    TR += [(kind, t, 0), (kind, t, 1)]
                if kind == "aT":
                    TR.append((kind, t, 0))
            TRN = {k: n for n, k in enumerate(TR)}

            with nc.Block() as block:
                @block.sync
                def _(sp):
                    sp.dma_start(cnat[0:1, :], a["c_prompt"]).then_inc(s_c, 16)
                    sp.dma_start(cnat[1:1 + SEQS, :], a["c_sample"]).then_inc(s_c, 16)

                    sp.dma_start(const[:, :], a["table"][:, 0:early]).then_inc(s_const, 16)

                    def ada_load(n):
                        j = CH[n]
                        sp.dma_start(ada_at[n], w_ada[:, :, j * 512:(j + 1) * 512]).then_inc(s_ada[n], 16)
                        sp.dma_start(modn[n], b_ada[j * 512:(j + 1) * 512].partition_broadcast(1 + SEQS)).then_inc(s_ada[n], 16)

                    for n in range(4):
                        ada_load(n)
                    sp.dma_start(wsp, a["w_spatial"][0].rearrange("h t s -> t h s")).then_inc(s_sp, 16)
                    sp.dma_start(bsp[:, :], a["b_spatial"][0].rearrange("h t -> t h"),
                                 allow_slow_non_contiguous=True).then_inc(s_sp, 16)
                    for s in range(SEQS):
                        sp.dma_start(wsb4[s * DSEQ:(s + 1) * DSEQ, :, :],
                                     a["w_spatial"][0, :, 0:DSEQ, 0:DSEQ].rearrange("h t s -> t h s")).then_inc(s_sp, 16)
                        sp.dma_start(bsp_s[s * DSEQ:(s + 1) * DSEQ, :],
                                     a["b_spatial"][0, :, 0:DSEQ].rearrange("h t -> t h"),
                                 allow_slow_non_contiguous=True).then_inc(s_sp, 16)
                    sp.dma_start(aln_g[:, :], a["a_ln_g"][0].rearrange("h d -> (h d)").partition_broadcast(P)).then_inc(s_aln, 16)
                    sp.dma_start(aln_b[:, :], a["a_ln_b"][0].rearrange("h d -> (h d)").partition_broadcast(P)).then_inc(s_aln, 16)
                    sp.wait_ge(s_trf, 1)
                    for t in range(2):
                        sp.dma_start(x_nat[:, t, :], x_tile[t]).then_inc(s_x[t], 16)

                    def w_load(g):
                        _, n0, w = GROUPS[g]
                        sp.dma_start(w_sb[:, :, n0:n0 + w], w_in[:, :, n0:n0 + w]).then_inc(s_win[g], 16)

                    w_load(0)
                    w_load(1)
                    for n in range(4):
                        j = CH[n]
                        sp.wait_ge(s_modn, n + 1)
                        sp.dma_start(mod_dram[:, j * 512:(j + 1) * 512], modn[n]).then_inc(s_modst, 16)
                    sp.wait_ge(s_modst, 16 * 4)
                    sp.dma_start(shift1[:, :], mod_dram[0, 0:D].partition_broadcast(P)).then_inc(s_bc, 16)
                    sp.dma_start(scale1[:, :], mod_dram[0, D:2 * D].partition_broadcast(P)).then_inc(s_bc, 16)
                    w_load(2)
                    w_load(3)
                    w_load(4)
                    for t in range(TILES + 1):
                        r = rows(t)
                        if t + 2 <= TILES:
                            sp.wait_ge(s_trf, TRN[("h", t, 1)] + 1)
                            sp.dma_start(x_nat[0:rows(t + 2), t % 2, :], x_tile[t + 2]).then_inc(s_x[t % 2], 16)
                        if t == TILES - 1:
                            sp.wait_ge(s_h, TILES)
                            for i in range(SEQS):
                                sp.dma_start(shift1[i * DSEQ:(i + 1) * DSEQ, :],
                                             mod_dram[1 + i, 0:D].partition_broadcast(DSEQ)).then_inc(s_bc, 16)
                                sp.dma_start(scale1[i * DSEQ:(i + 1) * DSEQ, :],
                                             mod_dram[1 + i, D:2 * D].partition_broadcast(DSEQ)).then_inc(s_bc, 16)
                        sp.wait_ge(s_rot, t + 1)
                        sp.dma_start(new_k[t], k_nat[0:r, t % 2, :]).then_inc(s_st[t % 2], 16)
                        sp.dma_start(new_kidx[t], idx_nat[0:r, t % 2, 256:320]).then_inc(s_st[t % 2], 16)
                        sp.dma_start(new_v[t], v_nat[0:r, t, :]).then_inc(s_stv, 16)
                    sp.wait_ge(s_ln, TILES + 1)
                    sp.dma_start(chunk_v, vg[0:NS, TILES % 2, :]).then_inc(s_stv, 16)
                    sp.wait_ge(s_stv, 16 * (TILES + 2))
                    sp.wait_ge(s_st[0], 32 * 5)
                    sp.wait_ge(s_st[1], 32 * 4)

                @block.gpsimd
                def _(pool):
                    g = nc.gpsimd
                    count = [0]

                    def then(ins):
                        count[0] += 1
                        ins.then_inc(poolc, 1)
                        pool.wait_ge(poolc, count[0])

                    pool.wait_ge(s_const, 16)
                    pool.wait_ge(s_sp, 16 * (2 + 2 * SEQS))
                    g.tensor_tensor(wsp, wsp, c("tril").unsqueeze(1).to_broadcast([P, AH, P]), ALU.mult).then_inc(s_tril, 1)
                    g.tensor_tensor(wsbd[:, :, :].rearrange("p h (s i) -> p h s i", i=DSEQ),
                                    wsb4[:, :, :].unsqueeze(2).to_broadcast([NS, AH, SEQS, DSEQ]),
                                    c("blktril", NS).rearrange("p (s i) -> p s i", i=DSEQ).unsqueeze(1).to_broadcast([NS, AH, SEQS, DSEQ]),
                                    ALU.mult).then_inc(s_tril, 1)

                    def modulate(t):
                        r = rows(t)
                        pool.wait_ge(s_x[t % 2], 16 * (t // 2 + 1))
                        pool.wait_ge(s_bc, 32 if t < TILES else 32 + 32 * SEQS)
                        then(g.tensor_tensor(x_nat[0:r, t % 2, :], x_nat[0:r, t % 2, :], scale1[0:r, :], ALU.mult))
                        g.tensor_tensor(x_nat[0:r, t % 2, :], x_nat[0:r, t % 2, :], shift1[0:r, :], ALU.add).then_inc(s_h, 1)

                    def rotate(x, t, r, n):
                        cos = c("cos", r).rearrange("p (t k) -> p t k", k=HALF)[:, t:t + 1, :].to_broadcast([r, n, HALF])
                        sin = c("sin", r).rearrange("p (t k) -> p t k", k=HALF)[:, t:t + 1, :].to_broadcast([r, n, HALF])
                        m = [rot[0:r, i, 0:n * HALF].rearrange("p (n k) -> p n k", k=HALF) for i in range(4)]
                        g.tensor_tensor(m[0], x[:, :, 0:HALF], cos, ALU.mult)
                        g.tensor_tensor(m[1], x[:, :, HALF:2 * HALF], sin, ALU.mult)
                        g.tensor_tensor(m[2], x[:, :, HALF:2 * HALF], cos, ALU.mult)
                        then(g.tensor_tensor(m[3], x[:, :, 0:HALF], sin, ALU.mult))
                        g.tensor_tensor(x[:, :, 0:HALF], m[0], m[1], ALU.subtract)
                        return g.tensor_tensor(x[:, :, HALF:2 * HALF], m[2], m[3], ALU.add)

                    def head_sums(dst, x, r):
                        half = HD // 2
                        y = tmp[0:r, 0:AH * half].rearrange("p (h d) -> p h d", h=AH)
                        then(g.tensor_tensor(y, x[:, :, 0:half], x[:, :, half:HD], ALU.add))
                        while half > 2:
                            half //= 2
                            then(g.tensor_tensor(y[:, :, 0:half], y[:, :, 0:half], y[:, :, half:2 * half], ALU.add))
                        then(g.tensor_tensor(dst, y[:, :, 0], y[:, :, 1], ALU.add))

                    def gate(t):
                        r = rows(t)
                        b = (bsp if t < TILES else bsp_s)[0:r, :].unsqueeze(2).to_broadcast([r, AH, HD])
                        s = spat[0:r, :].rearrange("p (h d) -> p h d", h=AH)
                        pool.wait_ge(s_spe, t + 1)
                        then(g.tensor_tensor(s, s, b, ALU.add))
                        g.tensor_tensor(u[0:r, t % 2, :], u[0:r, t % 2, :], spat[0:r, :], ALU.mult).then_inc(s_am, 1)

                    modulate(0)
                    modulate(1)
                    for t in range(TILES + 1):
                        r = rows(t)
                        pool.wait_ge(s_ev, 5 * t + 1)
                        then(rotate(idx_nat[0:r, t % 2, 0:320].rearrange("p (n d) -> p n d", d=HD), t, r, 5))
                        g.tensor_copy(w_i[0:r, t, :], idx_nat[0:r, t % 2, 320:324])
                        pool.wait_ge(s_ev, 5 * t + 2)
                        then(rotate(q_nat[0:r, t, :].rearrange("p (n d) -> p n d", d=HD), t, r, QH))
                        x = vg[0:r, t % 2, :]
                        x3 = x.rearrange("p (h d) -> p h d", h=AH)
                        sq = tmp[0:r, :]
                        mean, var = st8[0:r, 0, :], st8[0:r, 1, :]
                        bc = lambda y: y.unsqueeze(2).to_broadcast([r, AH, HD])
                        pool.wait_ge(s_ev, 5 * t + 3)
                        pool.wait_ge(s_aln, 32)
                        head_sums(mean, x3, r)
                        then(g.tensor_scalar(mean, mean, 1.0 / HD, None, ALU.mult))
                        then(g.tensor_tensor(x3, x3, bc(mean), ALU.subtract))
                        then(g.tensor_tensor(sq, x, x, ALU.mult))
                        head_sums(var, sq.rearrange("p (h d) -> p h d", h=AH), r)
                        then(g.tensor_scalar(var, var, 1.0 / HD, EPS, ALU.mult, ALU.add))
                        then(g.tensor_tensor(var, var, c("minushalf", r)[:, 0:AH], ALU.pow))
                        then(g.tensor_tensor(x3, x3, bc(var), ALU.mult))
                        then(g.tensor_tensor(x, x, aln_g[0:r, :], ALU.mult))
                        g.tensor_tensor(x, x, aln_b[0:r, :], ALU.add).then_inc(s_ln, 1)
                        pool.wait_ge(s_ev, 5 * t + 4)
                        rotate(k_nat[0:r, t % 2, :].rearrange("p (n d) -> p n d", d=HD), t, r, KVH).then_inc(s_rot, 1)
                        pool.wait_ge(s_rot, t + 1)
                        if t + 2 <= TILES:
                            modulate(t + 2)
                        if t >= 1:
                            gate(t - 1)
                    gate(TILES)

                @block.tensor
                def _(pe):
                    def fill(key, parts):
                        n = TRN[key]
                        if n >= 2:
                            pe.wait_ge(s_tre, n - 1)
                        for i, (col, src) in enumerate(parts):
                            r, w = src.shape[0], src.shape[-1]
                            last = nc.tensor.transpose(bank[n % 2][0:w, col:col + r], src, c("ident", r)[:, 0:r])
                        last.then_inc(s_trf, 1)

                    pe.wait_ge(s_const, 16)
                    pe.wait_ge(s_silu, 1)
                    fill(("c", 0, 0), [(16 * i, cnat[:, i * P:(i + 1) * P]) for i in range(DC)])
                    pe.wait_ge(s_tre, 1)
                    for n in range(4):
                        pe.wait_ge(s_ada[n], 32)
                        for i in range(DC):
                            last = nc.tensor.matmul(bank[2 + n][0:1 + SEQS, :], cT[:, i, :], ada_at[n][:, i, :],
                                                    start=(i == 0), stop=(i == DC - 1))
                        last.then_inc(s_adamm, 1)
                    pe.wait_ge(s_tril, 2)
                    for j in range(2):
                        fill(("sp", 0, j), [(P * i, wsp[:, 4 * j + i, :]) for i in range(4)])
                    fill(("spbd", 0, 0), [(NS * i, wsbd[:, i, :]) for i in range(AH)])
                    pe.wait_ge(s_modn, 4)

                    def h_steps(t):
                        r = rows(t)
                        pe.wait_ge(s_h, t + 1)
                        for j in range(2):
                            fill(("h", t, j), [(P * i, x_nat[0:r, t % 2, (4 * j + i) * P:(4 * j + i + 1) * P]) for i in range(4)])

                    h_steps(0)
                    for kind, t, i in STEPS:
                        r = rows(t) if t <= TILES else 0
                        if kind == "h":
                            h_steps(t)
                        elif kind == "group":
                            n = 5 * t + i
                            _, n0, w = GROUPS[i]
                            if t == 0:
                                pe.wait_ge(s_win[i], 16)
                            if i == 0:
                                pe.wait_ge(s_tre, TRN[("h", t, 1)] + 1)
                            if n >= 3:
                                pe.wait_ge(s_ev, n - 2)
                            for k in range(DC):
                                last = nc.tensor.matmul(bank[2 + n % 3][0:r, 0:w], hT[:, t % 2, k, 0:r], w_sb[:, k, n0:n0 + w],
                                                        start=(k == 0), stop=(k == DC - 1))
                            last.then_inc(s_mm, 1)
                        elif kind == "post":
                            pe.wait_ge(s_rot, t + 1)
                            ix = idx_nat[0:r, t % 2, :]
                            fill(("post", t, 0), [(0, k_nat[0:r, t % 2, 0:P]), (P, k_nat[0:r, t % 2, P:2 * P]), (2 * P, ix[:, 256:320])])
                            fill(("post", t, 1), [(P * h, ix[:, h * HD:(h + 1) * HD]) for h in range(IH)])
                        elif kind == "score":
                            keys = (t + 1) * P
                            m = IH * (t - IDX0) + i
                            if i == 0:
                                pe.wait_ge(s_tre, TRN[("post", t, 1)] + 1)
                            if m >= 1:
                                pe.wait_ge(s_acc, m)
                            for b in range((keys + 511) // 512):
                                w = min(512, keys - 512 * b)
                                last = nc.tensor.matmul(bank[5 + b][:, 0:w], qiT[:, i, :], kiT[:, 512 * b:512 * b + w],
                                                        start=True, stop=True)
                            last.then_inc(s_idxp, 1)
                        elif kind == "mix":
                            pe.wait_ge(s_ln, t + 1)
                            if t >= 1:
                                pe.wait_ge(s_spe, t)
                            for h in range(AH):
                                w = wspT[:, h, :] if t < TILES else wsbdT[:, h, :]
                                last = nc.tensor.matmul(bank[7][0:r, h * HD:(h + 1) * HD], w, vg[0:r, t % 2, h * HD:(h + 1) * HD],
                                                        start=True, stop=True)
                            last.then_inc(s_spm, 1)
                        elif kind == "aT":
                            pe.wait_ge(s_am, t + 1)
                            fill(("aT", t, 0), [(P * j, u[0:r, t % 2, j * P:(j + 1) * P]) for j in range(4)])

                @block.scalar
                def _(act):
                    s = nc.scalar

                    def empty(key, parts):
                        n = TRN[key]
                        act.wait_ge(s_trf, n + 1)
                        for dst, src in parts:
                            last = s.activation(dst, src(bank[n % 2]), ACT.Copy)
                        last.then_inc(s_tre, 1)

                    act.wait_ge(s_c, 32)
                    s.activation(cnat, cnat, ACT.Silu).then_inc(s_silu, 1)
                    act.wait_ge(s_trf, 1)
                    s.activation(cT[:, :, :], bank[0][:, 0:16 * DC].rearrange("p (c n) -> p c n", n=16)[:, :, 0:1 + SEQS], ACT.Copy).then_inc(s_tre, 1)
                    for j in range(2):
                        empty(("sp", 0, j), [(wspT[:, 4 * j:4 * j + 4, :], lambda b: b[:, :].rearrange("p (h t) -> p h t", h=4))])
                    empty(("spbd", 0, 0), [(wsbdT[:, :, :], lambda b: b[0:NS, 0:AH * NS].rearrange("p (h t) -> p h t", h=AH))])

                    def h_steps(t):
                        r = rows(t)
                        if t >= 2:
                            act.wait_ge(s_mm, 5 * (t - 1))
                        for j in range(2):
                            empty(("h", t, j), [(hT[:, t % 2, 4 * j:4 * j + 4, 0:r],
                                                 lambda b: b[:, :].rearrange("p (i r) -> p i r", i=4)[:, :, 0:r])])

                    act.wait_ge(s_trf, TRN[("spbd", 0, 0)] + 1)
                    h_steps(0)
                    for kind, t, i in STEPS:
                        r = rows(t) if t <= TILES else 0
                        if kind == "h":
                            h_steps(t)
                        elif kind == "group":
                            n = 5 * t + i
                            name, n0, w = GROUPS[i]
                            act.wait_ge(s_mm, n + 1)
                            src = bank[2 + n % 3][0:r, 0:w]
                            if name == "idx":
                                if t >= 2:
                                    act.wait_ge(s_trf, TRN[("post", t - 2, 1)] + 1)
                                    act.wait_ge(s_st[t % 2], 32 * (t // 2))
                                last = s.activation(idx_nat[0:r, t % 2, :], src, ACT.Copy)
                            elif name == "q":
                                last = s.activation(q_nat[0:r, t, :], src, ACT.Copy)
                            elif name == "kv":
                                s.activation(k_nat[0:r, t % 2, :], src[:, 0:256], ACT.Copy)
                                last = s.activation(v_nat[0:r, t, :], src[:, 256:512], ACT.Copy)
                            elif name == "au":
                                if t >= 2:
                                    act.wait_ge(s_trf, TRN[("aT", t - 2, 0)] + 1)
                                last = s.activation(u[0:r, t % 2, :], src, ACT.Gelu_apprx_tanh)
                            else:
                                if t >= 2:
                                    act.wait_ge(s_spm, t - 1)
                                last = s.activation(vg[0:r, t % 2, :], src, ACT.Gelu_apprx_tanh)
                            last.then_inc(s_ev, 1)
                        elif kind == "post":
                            tok = slice(t * P, t * P + r)
                            empty(("post", t, 0), [(kT[:, :, tok], lambda b: b[:, 0:2 * P].rearrange("p (j r) -> p j r", j=2)[:, :, 0:r]),
                                                   (kiT[:, tok], lambda b: b[0:HD, 2 * P:2 * P + r])])
                            if IDX0 < t < TILES:
                                act.wait_ge(s_idxp, IH * (t - IDX0))
                            dst = qiT[:, :, :] if t < TILES else qi_s[:, :, :]
                            empty(("post", t, 1), [(dst, lambda b: b[0:HD, :].rearrange("p (h r) -> p h r", h=IH)[:, :, 0:r])])
                        elif kind == "score":
                            keys = (t + 1) * P
                            m = IH * (t - IDX0) + i
                            act.wait_ge(s_idxp, m + 1)
                            for b in range((keys + 511) // 512):
                                w = min(512, keys - 512 * b)
                                last = s.activation(bank[5 + b][:, 0:w], bank[5 + b][:, 0:w], ACT.Relu)
                            last.then_inc(s_relu, 1)
                        elif kind == "try":
                            search_count_act(act, s, t, i)
                        elif kind == "mix":
                            act.wait_ge(s_spm, t + 1)
                            if t >= 1:
                                act.wait_ge(s_am, t)
                            s.activation(spat[0:r, :], bank[7][0:r, :], ACT.Copy).then_inc(s_spe, 1)
                        elif kind == "aT":
                            empty(("aT", t, 0), [(mixa[:, :, t * P:t * P + r],
                                                  lambda b: b[:, :].rearrange("p (j r) -> p j r", j=4)[:, :, 0:r])])

                @block.vector
                def _(dve):
                    v = nc.vector
                    count = [0]

                    def then(ins):
                        count[0] += 1
                        ins.then_inc(dvec, 1)
                        dve.wait_ge(dvec, count[0])

                    for n in range(4):
                        dve.wait_ge(s_adamm, n + 1)
                        v.scalar_tensor_tensor(out=modn[n], in0=bank[2 + n][0:1 + SEQS, :], scalar=1.0 if CH[n] in (2, 3, 8, 9) else 0.0,
                                               in1=modn[n], op0=ALU.add, op1=ALU.add).then_inc(s_modn, 1)
                    dve.wait_ge(s_const, 16)

                    for kind, t, i in STEPS:
                        if kind == "score":
                            keys = (t + 1) * P
                            m = IH * (t - IDX0) + i
                            score, w = score_of(t), w_i[:, t, i:i + 1]
                            dve.wait_ge(s_relu, m + 1)
                            if i == 0:
                                v.tensor_scalar(score, banks56[:, 0:keys], w, None, ALU.mult).then_inc(s_acc, 1)
                            else:
                                v.scalar_tensor_tensor(out=score, in0=banks56[:, 0:keys], scalar=w, in1=score,
                                                       op0=ALU.mult, op1=ALU.add).then_inc(s_acc, 1)
                            dve.wait_ge(s_acc, m + 1)
                        elif kind == "begin":
                            search_begin(dve, v, then, t)
                        elif kind == "try":
                            search_count(dve, v, then, t)
                            search_step(dve, v, then, t, i)
                        elif kind == "end":
                            search_end(dve, v, then, t)
                        elif kind == "pick":
                            pick(dve, v, then, t, i // PICK, i % PICK)

        pages = tail.enter_context(ExitStack())
        pt = sb(pages, "pt", [1, SEQS * NPG], I32)
        v_pg = sb(pages, "v_pg", [P, SEQS * NPG, KVH * HD])
        top = sb(pages, "top", [P, 8])
        st = sb(pages, "st", [P, 2, 4])
        zero = sb(pages, "zero", [P, D])
        b_zero = sem(pages, "b_zero")
        b_fill = sem(pages, "b_fill")
        key_pages = pages.enter_context(ExitStack())
        ki_pg = sb(key_pages, "ki_pg", [P, SEQS * NPG, HD])
        k_pg = sb(key_pages, "k_pg", [P, SEQS * NPG, KVH * HD])
        c_pt = sem(pages, "c_pt")
        c_pg = [sem(pages, f"c_pg{i}") for i in range(3)]

        with ExitStack() as ctx:
            qz = sb(ctx, "qz", [P, 2, QH, P])
            qzT = sb(ctx, "qzT", [P, 2, QH, P])
            prob = sb(ctx, "prob", [P, 3, SEQ])
            pT = sb(ctx, "pT", [P, 2, TILES, P])
            o_nat = sb(ctx, "o_nat", [P, 2, QH * HD])
            mx = sb(ctx, "mx", [P, TILES * QH])
            nmx = sb(ctx, "nmx", [P, TILES * QH])
            den = sb(ctx, "den", [P, TILES * QH])
            rden = sb(ctx, "rden", [P, TILES * QH])
            causal = sb(ctx, "causal", [P, 3 * P])
            ring = v_pg[:, :, :].rearrange("p (b t) n -> p b (t n)", b=2).rearrange("p b (c n) -> p b c n", c=DC)
            modrow = sb(ctx, "modrow", [1 + SEQS, 2, 512])
            b_ada_w = [sem(pages, f"b_ada_w{i}") for i in range(2)]
            b_adamm = sem(ctx, "b_adamm")
            b_mod = sem(ctx, "b_mod")
            b_modst = [sem(ctx, f"b_modst{i}") for i in range(2)]
            b_causal = sem(ctx, "b_causal")
            b_dve = sem(ctx, "b_dve")
            b_z = sem(ctx, "b_z")
            b_qz = sem(ctx, "b_qz")
            b_trf = sem(ctx, "b_trf")
            b_tre = [sem(ctx, f"b_tre{i}") for i in range(2)]
            b_s = sem(ctx, "b_s")
            b_add = sem(ctx, "b_add")
            b_nmx = sem(ctx, "b_nmx")
            b_exp = sem(ctx, "b_exp")
            b_pv = sem(ctx, "b_pv")
            b_rd = sem(ctx, "b_rd")
            b_o = sem(ctx, "b_o")
            ITEMS = [(t, h) for t in range(TILES) for h in range(QH)]
            ADA_AT = {7 * n // 4: (n,) for n in range(16)}
            TRY_AT = {n * 5 // 4: n for n in range(SEARCH)}
            LAST_TRY = max(TRY_AT)
            ORDER = [("q", 0), ("S", 0), ("S", 1)]
            for m, (t, h) in enumerate(ITEMS):
                if h == 4 and t + 1 < TILES:
                    ORDER.append(("q", t + 1))
                if m + 2 < len(ITEMS):
                    ORDER.append(("S", m + 2))
                ORDER.append(("pT", m))
                ORDER += [("ada", n) for n in ADA_AT.get(m, ())]
                if m >= 1:
                    ORDER.append(("pv", m - 1))
                if h == 3 and t >= 1:
                    ORDER.append(("oT", t - 1))
            ORDER += [("pv", len(ITEMS) - 1), ("oT", TILES - 1)]
            BTR = []
            for kind, m in ORDER:
                if kind == "q":
                    BTR += [("q", m, 0), ("q", m, 1)]
                elif kind == "oT":
                    BTR.append(("oT", m, 0))
                elif kind == "pT":
                    BTR += [("pT", m, i) for i in range(1 + ITEMS[m][0] // 4)]
            BTRN = {k: n for n, k in enumerate(BTR)}

            with nc.Block() as block:
                @block.sync
                def _(sp):
                    sp.dma_start(pt[:, :], a["page_table"].rearrange("b n -> (b n)").unsqueeze(0)).then_inc(c_pt, 16)
                    sp.wait_ge(c_pt, 16)

                    def mod_store(n):
                        j = CH[n]
                        sp.wait_ge(b_mod, n - 3)
                        sp.dma_start(mod_dram[:, j * 512:(j + 1) * 512], modrow[:, n % 2, :]).then_inc(b_modst[n % 2], 16)

                    for n in range(4, 12):
                        if n >= 6:
                            mod_store(n - 2)
                            sp.wait_ge(b_adamm, n - 5)
                        j = CH[n]
                        sp.dma_start(ring[:, n % 2, :, :], w_ada[:, :, j * 512:(j + 1) * 512]).then_inc(b_ada_w[n % 2], 16)
                        if n >= 6:
                            sp.wait_ge(b_modst[n % 2], 16 * (n // 2 - 2))
                        sp.dma_start(modrow[:, n % 2, :], b_ada[j * 512:(j + 1) * 512].partition_broadcast(1 + SEQS)).then_inc(b_ada_w[n % 2], 16)
                    mod_store(10)
                    mod_store(11)
                    with sp.Fori(0, SEQS * NPG) as i:
                        page = sp.value_load(pt[0:1, bass.ds(i, 1)], min_val=0, max_val=a["cache_k"].shape[1] - 1)
                        sp.dma_start(ki_pg[:, bass.ds(i, 1), :], a["cache_kidx"][0, bass.ds(page, 1), :, :].rearrange("n p d -> p n d")).then_inc(c_pg[0], 16)
                        sp.dma_start(k_pg[:, bass.ds(i, 1), :], a["cache_k"][0, bass.ds(page, 1), :, :, :].rearrange("n p h d -> p n (h d)")).then_inc(c_pg[1], 16)
                    for i in range(2):
                        sp.wait_ge(b_ada_w[i], 32 * 4)
                    sp.wait_ge(b_adamm, 8)
                    with sp.Fori(0, SEQS * NPG) as i:
                        page = sp.value_load(pt[0:1, bass.ds(i, 1)], min_val=0, max_val=a["cache_v"].shape[1] - 1)
                        sp.dma_start(v_pg[:, bass.ds(i, 1), :], a["cache_v"][0, bass.ds(page, 1), :, :, :].rearrange("n p h d -> p n (h d)")).then_inc(c_pg[2], 16)
                    for i in range(2):
                        sp.wait_ge(b_modst[i], 16 * 4)
                @block.gpsimd
                def _(pool):
                    g = nc.gpsimd
                    g.memset(qz[:, :, :, :], 0.0).then_inc(b_z, 1)
                    pool.wait_ge(b_z, 1)
                    for t in range(TILES):
                        if t >= 2:
                            pool.wait_ge(b_trf, BTRN[("q", t - 2, 1)] + 1)
                        dst = qz[:, t % 2, :, :].rearrange("p (j b i) w -> p j b i w", j=2, b=2)
                        src = q_nat[:, t, :].rearrange("p (j b i w) -> p j b i w", j=2, b=2, i=2)
                        for b in range(2):
                            g.tensor_copy(dst[:, :, b, :, b * HD:(b + 1) * HD], src[:, :, b, :, :]).then_inc(b_qz, 1)
                        if t == 1:
                            g.memset(zero[:, :], 0.0).then_inc(b_zero, 1)

                @block.tensor
                def _(pe):
                    def fill(key, parts):
                        n = BTRN[key]
                        if n >= 2:
                            pe.wait_ge(b_tre[n % 2], n // 2)
                        for i, src in enumerate(parts):
                            last = nc.tensor.transpose(bank[n % 2][:, i * P:(i + 1) * P], src, c("ident"))
                        last.then_inc(b_trf, 1)

                    for kind, m in ORDER:
                        t, h = ITEMS[m] if kind in ("S", "pT", "pv") else (m, 0)
                        if kind == "q":
                            pe.wait_ge(b_qz, 2 * (t + 1))
                            for i in range(2):
                                fill(("q", t, i), [qz[:, t % 2, 4 * i + k, :] for k in range(4)])
                        elif kind == "S":
                            keys = (t + 1) * P
                            if h == 0:
                                n = BTRN[("q", t, 1)]
                                pe.wait_ge(b_tre[n % 2], n // 2 + 1)
                                pe.wait_ge(b_tre[1 - n % 2], (n - 1) // 2 + 1)
                            if m >= 2:
                                pe.wait_ge(b_add, m - 1)
                            if keys > 512 and h < 2:
                                pe.wait_ge(b_mod, 8)
                            for b in range((keys + 511) // 512):
                                w = min(512, keys - 512 * b)
                                last = nc.tensor.matmul(bank[2 + 2 * (m % 2) + b][:, 0:w], qzT[:, t % 2, h, :],
                                                        kT[:, h // 4, 512 * b:512 * b + w], start=True, stop=True)
                            last.then_inc(b_s, 1)
                        elif kind == "pT":
                            pe.wait_ge(b_exp, m + 1)
                            for i in range(1 + t // 4):
                                fill(("pT", m, i), [prob[:, m % 3, k * P:(k + 1) * P] for k in range(4 * i, min(4 * i + 4, t + 1))])
                        elif kind == "pv":
                            n = BTRN[("pT", m, t // 4)]
                            pe.wait_ge(b_tre[n % 2], n // 2 + 1)
                            if t >= 4:
                                pe.wait_ge(b_tre[1 - n % 2], (n - 1) // 2 + 1)
                            if h == 0 and t >= 2:
                                pe.wait_ge(b_o, t - 1)
                            kv = h // 2
                            for k in range(t + 1):
                                last = nc.tensor.matmul(bank[6 + t % 2][:, h * HD:(h + 1) * HD], pT[:, m % 2, k, :],
                                                        v_nat[:, k, kv * HD:(kv + 1) * HD], start=(k == 0), stop=(k == t))
                            last.then_inc(b_pv, 1)
                        elif kind == "ada":
                            n, half = 4 + m // 2, m % 2
                            if half == 0:
                                pe.wait_ge(b_ada_w[n % 2], 32 * (n // 2 - 1))
                                if n >= 6:
                                    pe.wait_ge(b_mod, n - 5)
                            for k in range(half * DC // 2, (half + 1) * DC // 2):
                                last = nc.tensor.matmul(bank[3 + 2 * (n % 2)][0:1 + SEQS, :], cT[:, k, :], ring[:, n % 2, k, :],
                                                        start=(k == 0), stop=(k == DC - 1))
                            if half == 1:
                                last.then_inc(b_adamm, 1)
                        else:
                            pe.wait_ge(b_o, t + 1)
                            fill(("oT", t, 0), [o_nat[:, t % 2, k * P:(k + 1) * P] for k in range(4)])

                @block.scalar
                def _(act):
                    s = nc.scalar

                    def empty(key, dst, w):
                        n = BTRN[key]
                        act.wait_ge(b_trf, n + 1)
                        s.activation(dst, bank[n % 2][:, 0:w], ACT.Copy).then_inc(b_tre[n % 2], 1)

                    for kind, m in ORDER:
                        if kind == "q":
                            if m >= 2:
                                act.wait_ge(b_s, QH * (m - 1))
                            for i in range(2):
                                empty(("q", m, i), qzT[:, m % 2, 4 * i:4 * i + 4, :], 512)
                        elif kind == "oT":
                            empty(("oT", m, 0), q_nat[:, m, :], 512)
                        elif kind == "pT":
                            t, h = ITEMS[m]
                            keys = (t + 1) * P
                            act.wait_ge(b_nmx, m + 1)
                            s.activation(prob[:, m % 3, 0:keys], prob[:, m % 3, 0:keys], ACT.Exp, bias=nmx[:, m:m + 1],
                                         scale=HD ** -0.5, accum_out=den[:, m:m + 1]).then_inc(b_exp, 1)
                            if m in TRY_AT:
                                search_count_act(act, s, 3, TRY_AT[m])
                            if m >= 2:
                                act.wait_ge(b_pv, m - 1)
                            w = min(512, keys)
                            empty(("pT", m, 0), pT[:, m % 2, 0:w // P, :], w)

                @block.vector
                def _(dve):
                    v = nc.vector
                    v.memset(causal[:, P:2 * P], 0.0).then_inc(b_causal, 1)
                    for k in (0, 2):
                        v.tensor_scalar(causal[:, k * P:(k + 1) * P], c("later"), NEG_MASK, None, ALU.mult).then_inc(b_causal, 1)
                    dve.wait_ge(b_causal, 3)
                    count = [0]

                    def then(ins):
                        count[0] += 1
                        ins.then_inc(b_dve, 1)
                        dve.wait_ge(b_dve, count[0])

                    search_begin(dve, v, then, 3)
                    for m in range(len(ITEMS) + 2):
                        if m < len(ITEMS):
                            t, h = ITEMS[m]
                            keys = (t + 1) * P
                            dve.wait_ge(b_s, m + 1)
                            if m >= 3:
                                t3 = ITEMS[m - 3][0]
                                dve.wait_ge(b_trf, BTRN[("pT", m - 3, t3 // 4)] + 1)
                            src = psum[:, 512 * (2 + 2 * (m % 2)):512 * (2 + 2 * (m % 2)) + keys]
                            v.tensor_tensor_reduce(out=prob[:, m % 3, 0:keys], in0=src, in1=(bias[:, bias_at[t]:bias_at[t] + keys] if t >= 2 else causal[:, t * P:t * P + keys]),
                                                   scale=1.0, scalar=NEG_TAKEN, op0=ALU.add, op1=ALU.max,
                                                   accum_out=mx[:, m:m + 1]).then_inc(b_add, 1)
                            dve.wait_ge(b_add, m + 1)
                            v.tensor_scalar(nmx[:, m:m + 1], mx[:, m:m + 1], -HD ** -0.5, None, ALU.mult).then_inc(b_nmx, 1)
                        if m - 1 in ADA_AT and ADA_AT[m - 1][0] % 2 == 1:
                            n = 4 + ADA_AT[m - 1][0] // 2
                            dve.wait_ge(b_adamm, n - 3)
                            v.scalar_tensor_tensor(out=modrow[:, n % 2, :], in0=bank[3 + 2 * (n % 2)][0:1 + SEQS, :],
                                                   scalar=1.0 if CH[n] in (2, 3, 8, 9) else 0.0, in1=modrow[:, n % 2, :],
                                                   op0=ALU.add, op1=ALU.add).then_inc(b_mod, 1)
                        if m >= 2:
                            t, h = ITEMS[m - 2]
                            if t >= 4:
                                n = BTRN[("pT", m - 2, 1)]
                                dve.wait_ge(b_trf, n + 1)
                                if m >= 4:
                                    dve.wait_ge(b_pv, m - 3)
                                w = (t + 1) * P - 512
                                v.tensor_copy(pT[:, m % 2, 4:4 + w // P, :], bank[n % 2][:, 0:w]).then_inc(b_tre[n % 2], 1)
                            if h == QH - 1:
                                e = slice(t * QH, (t + 1) * QH)
                                dve.wait_ge(b_exp, m - 1)
                                v.reciprocal(rden[:, e], den[:, e]).then_inc(b_rd, 1)
                                dve.wait_ge(b_rd, t + 1)
                                dve.wait_ge(b_pv, m - 1)
                                if t >= 2:
                                    dve.wait_ge(b_trf, BTRN[("oT", t - 2, 0)] + 1)
                                v.tensor_tensor(o_nat[:, t % 2, :].rearrange("p (h d) -> p h d", h=QH),
                                                bank[6 + t % 2].rearrange("p (h d) -> p h d", h=QH),
                                                rden[:, e].unsqueeze(2).to_broadcast([P, QH, HD]), ALU.mult).then_inc(b_o, 1)
                        if m in TRY_AT:
                            if m >= 1:
                                search_step(dve, v, then, 3, TRY_AT[m] - 1)
                            search_count(dve, v, then, 3)
                        elif m == LAST_TRY + 1:
                            search_step(dve, v, then, 3, SEARCH - 1)
                            search_end(dve, v, then, 3)
                        elif LAST_TRY + 2 <= m < LAST_TRY + 2 + 2 * PICK:
                            k, part = divmod(m - LAST_TRY - 2, PICK)
                            pick(dve, v, then, 3, k, part)

        L = PAST + DSEQ
        sc = bias[:, 0:L]
        pr = bias[:, L:3 * L].rearrange("p (j n) -> p j n", j=2)
        pn = bias[:, 3 * L:3 * L + 2 * NS].rearrange("p (j n) -> p j n", j=2)
        pnT = bias[0:NS, 4 * L:4 * L + 2 * P].rearrange("p (j n) -> p j n", j=2)
        prT = bias[:, 5 * L:5 * L + 2 * PAST].rearrange("p (j k n) -> p j k n", j=2, k=NPG)
        c_nmx, c_exp, c_pn, c_trp, c_trpe, c_o, c_out = (sem(pages, n) for n in ("c_nmx", "c_exp", "c_pn", "c_trp", "c_trpe", "c_o", "c_out"))
        with ExitStack() as ctx:
            qzs = sb(ctx, "qzs", [NS, QH, P])
            qzsT = sb(ctx, "qzsT", [P, QH, NS])
            qsel = sb(ctx, "qsel", [P, 2, SEQS, P])
            isel = sb(ctx, "isel", [HD, SEQS, P])
            kipT = sb(ctx, "kipT", [HD, 2, PAST])
            kpT = sb(ctx, "kpT", [P, 2, 2, PAST])
            wrow = sb(ctx, "wrow", [P, 1])
            relw = sb(ctx, "relw", [P, L])
            c_qz = sem(ctx, "c_qz")
            c_sel = sem(ctx, "c_sel")
            c_trf = sem(ctx, "c_trf")
            c_tre = sem(ctx, "c_tre")
            c_qk = sem(ctx, "c_qk")
            c_w = sem(ctx, "c_w")
            c_sum = sem(ctx, "c_sum")
            c_dve = sem(ctx, "c_dve")
            CTR = [("q", 0, 0)] + [(k, s, j) for s in range(SEQS) for k, j in (("ki", 0), ("k", 0), ("k", 1))]
            CTRN = {k: n for n, k in enumerate(CTR)}

            with nc.Block() as block:
                @block.sync
                def _(sp):
                    sp.wait_ge(b_zero, 1)
                    with sp.Fori(NE, SLOTS) as i:
                        sp.dma_start(ys_dram.rearrange("(e p) n -> e p n", p=P)[bass.ds(i, 1), :, :].rearrange("e p n -> p (e n)"),
                                     zero[:, :]).then_inc(b_fill, 16)
                    sp.wait_ge(b_fill, 16 * MAXEXTRA)

                @block.gpsimd
                def _(pool):
                    g = nc.gpsimd
                    g.memset(qzs[:, :, :], 0.0).then_inc(c_qz, 1)
                    pool.wait_ge(c_qz, 1)
                    dst = qzs[:, :, :].rearrange("p (j b i) w -> p j b i w", j=2, b=2)
                    src = q_nat[0:NS, TILES, :].rearrange("p (j b i w) -> p j b i w", j=2, b=2, i=2)
                    for b in range(2):
                        g.tensor_copy(dst[:, :, b, :, b * HD:(b + 1) * HD], src[:, :, b, :, :]).then_inc(c_qz, 1)

                @block.tensor
                def _(pe):
                    def fill(key, parts, w=P):
                        n = CTRN[key]
                        if n >= 2:
                            pe.wait_ge(c_tre, n - 1)
                        for i, src in enumerate(parts):
                            r, m = src.shape
                            last = nc.tensor.transpose(bank[n % 2][0:m, i * r:(i + 1) * r], src, c("ident", r)[:, 0:r])
                        last.then_inc(c_trf, 1)

                    pe.wait_ge(c_qz, 3)
                    fill(("q", 0, 0), [qzs[:, h, :] for h in range(QH)])
                    for i in range(2):
                        pe.wait_ge(c_pg[i], 16 * SEQS * NPG)
                    for s in range(SEQS + 1):
                        if s < SEQS:
                            fill(("ki", s, 0), [ki_pg[:, NPG * s + k, :] for k in range(NPG)])
                            for j in range(2):
                                fill(("k", s, j), [k_pg[:, NPG * s + k, j * P:(j + 1) * P] for k in range(NPG)])
                        if s >= 1:
                            r = s - 1
                            pe.wait_ge(c_tre, CTRN[("k", r, 1)] + 1)
                            if r == 0:
                                pe.wait_ge(c_sel, IH + QH)
                            new = slice(SEQ + r * DSEQ, SEQ + (r + 1) * DSEQ)
                            f = dict(start=(r == 0), stop=(r == SEQS - 1))
                            nc.tensor.matmul(bank[2][:, :], isel[:, r, :], kipT[:, r % 2, :], **f)
                            nc.tensor.matmul(bank[3][:, 0:DSEQ], isel[:, r, :], kiT[:, new], **f)
                            for j in range(2):
                                nc.tensor.matmul(bank[4 + j][:, :], qsel[:, j, r, :], kpT[:, r % 2, j, :], **f)
                                last = nc.tensor.matmul(bank[6 + j][:, 0:DSEQ], qsel[:, j, r, :], kT[:, j, new], **f)
                            last.then_inc(c_qk, 1)
                    pe.wait_ge(c_w, 2)
                    nc.tensor.matmul(bank[2][:, :], c("sametok"), relw[:, 0:PAST], start=True, stop=True)
                    nc.tensor.matmul(bank[3][:, 0:DSEQ], c("sametok"), relw[:, PAST:L], start=True, stop=True).then_inc(c_sum, 1)
                @block.scalar
                def _(act):
                    s_ = nc.scalar

                    def empty(key, dst, src):
                        n = CTRN[key]
                        act.wait_ge(c_trf, n + 1)
                        s_.activation(dst, src(bank[n % 2]), ACT.Copy).then_inc(c_tre, 1)

                    empty(("q", 0, 0), qzsT[:, :, :], lambda b: b[:, 0:QH * NS].rearrange("p (h n) -> p h n", h=QH))
                    for s in range(SEQS):
                        if s >= 2:
                            act.wait_ge(c_qk, s - 1)
                        empty(("ki", s, 0), kipT[:, s % 2, :], lambda b: b[0:HD, :])
                        for j in range(2):
                            empty(("k", s, j), kpT[:, s % 2, j, :], lambda b: b)
                @block.vector
                def _(dve):
                    v = nc.vector
                    count = [0]

                    def then(ins):
                        count[0] += 1
                        ins.then_inc(c_dve, 1)
                        dve.wait_ge(c_dve, count[0])

                    def cols(name, r):
                        return c(name, r).rearrange("p (s n) -> p s n", s=SEQS)

                    for h in range(IH):
                        v.tensor_tensor(isel[:, :, h * NS:(h + 1) * NS], qi_s[:, h:h + 1, :].to_broadcast([HD, SEQS, NS]),
                                        cols("seqcol", HD), ALU.mult).then_inc(c_sel, 1)
                        v.tensor_copy(wrow[h * NS:(h + 1) * NS, :], w_i[0:NS, TILES, h:h + 1]).then_inc(c_dve, 1)
                        count[0] += 1
                    dve.wait_ge(c_tre, 1)
                    for h in range(QH):
                        v.tensor_tensor(qsel[:, h // 4, :, (h % 4) * NS:(h % 4 + 1) * NS], qzsT[:, h:h + 1, :].to_broadcast([P, SEQS, NS]),
                                        cols("seqcol", P), ALU.mult).then_inc(c_sel, 1)
                    dve.wait_ge(c_dve, count[0])
                    dve.wait_ge(c_qk, SEQS)
                    v.tensor_scalar(relw[:, 0:PAST], bank[2], 0.0, wrow[:, 0:1], ALU.max, ALU.mult).then_inc(c_w, 1)
                    v.tensor_scalar(relw[:, PAST:L], bank[3][:, 0:DSEQ], 0.0, wrow[:, 0:1], ALU.max, ALU.mult).then_inc(c_w, 1)
                    dve.wait_ge(c_sum, 1)
                    v.tensor_copy(sc[:, 0:PAST], bank[2])
                    then(v.tensor_tensor(sc[:, PAST:L], bank[3][:, 0:DSEQ], c("newneg"), ALU.add))
                    for j in range(2):
                        v.tensor_copy(pr[:, j, 0:PAST], bank[4 + j])
                        v.tensor_copy(pr[:, j, PAST:L], bank[6 + j][:, 0:DSEQ])

        TA = TILES + 1
        key_pages.close()
        with ExitStack() as ctx:
            w_o = sb(ctx, "w_o", [P, DC, D])
            xr = sb(ctx, "xr", [P, 2, D])
            z = sb(ctx, "z", [P, 2, D])
            h2 = sb(ctx, "h2", [P, 2, D])
            h2T = sb(ctx, "h2T", [P, DC, P])
            vec = {n: sb(ctx, n, [P, D]) for n in ("gate1", "shift2", "scale2", "ln1_g", "ln1_b")}
            rw = sb(ctx, "rw", [P, DC, NG + NE])
            stat = sb(ctx, "stat", [P, 2, 2, 6])
            mv = sb(ctx, "mv", [P, 2, 2])
            d_w = [sem(ctx, f"d_w{i}") for i in range(2)]
            d_v = sem(ctx, "d_v")
            d_x = [sem(ctx, f"d_xr{i}") for i in range(2)]
            d_mm = sem(ctx, "d_mm")
            d_z = sem(ctx, "d_z")
            d_dve = sem(ctx, "d_dve")
            d_mv = sem(ctx, "d_mv")
            d_pool = sem(ctx, "d_pool")
            d_rs = sem(ctx, "d_rs")
            d_x1 = sem(ctx, "d_x1")
            d_h2 = sem(ctx, "d_h2")
            d_st = [sem(ctx, f"d_st{i}") for i in range(2)]
            d_trf = sem(ctx, "d_trf")
            d_tre = sem(ctx, "d_tre")
            d_lg = sem(ctx, "d_lg")
            d_lge = sem(ctx, "d_lge")
            x1_tile = [x1_dram[t * P:t * P + rows(t), :] for t in range(TA)]
            h2_tile = [h2_dram[t * P:t * P + rows(t), :] for t in range(TA)]

            with nc.Block() as block:
                @block.sync
                def _(sp):
                    w = a["w_out"][0].rearrange("(c p) n -> p c n", p=P)
                    for i in range(2):
                        sp.dma_start(w_o[:, :, i * 512:(i + 1) * 512], w[:, :, i * 512:(i + 1) * 512]).then_inc(d_w[i], 16)
                    for i in range(2):
                        sp.dma_start(xr[:, i, :], x_tile[i]).then_inc(d_x[i], 16)
                    mods = (("gate1", 2), ("shift2", 3), ("scale2", 4))
                    for n, j in mods:
                        sp.dma_start(vec[n][:, :], mod_dram[0, j * D:(j + 1) * D].partition_broadcast(P)).then_inc(d_v, 16)
                    for n in ("ln1_g", "ln1_b"):
                        sp.dma_start(vec[n][:, :], a[n][0].partition_broadcast(P)).then_inc(d_v, 16)
                    sp.dma_start(rw[:, :, 0:NG], a["w_group_router"][0].rearrange("(c p) g -> p c g", p=P)).then_inc(d_v, 16)
                    sp.dma_start(rw[:, :, NG:NG + NE], a["w_expert_router"][0].rearrange("(c p) g e -> p c (g e)", p=P)).then_inc(d_v, 16)
                    for t in range(TA):
                        r = rows(t)
                        sp.wait_ge(d_x1, t + 1)
                        sp.dma_start(x1_tile[t], z[0:r, t % 2, :]).then_inc(d_st[t % 2], 16)
                        if t + 2 < TA:
                            sp.dma_start(xr[0:rows(t + 2), t % 2, :], x_tile[t + 2]).then_inc(d_x[t % 2], 16)
                        sp.wait_ge(d_h2, t + 1)
                        sp.dma_start(h2_tile[t], h2[0:r, t % 2, :]).then_inc(d_st[t % 2], 16)
                        if t == TILES - 1:
                            for n, j in mods:
                                for i in range(SEQS):
                                    sp.dma_start(vec[n][i * DSEQ:(i + 1) * DSEQ, :],
                                                 mod_dram[1 + i, j * D:(j + 1) * D].partition_broadcast(DSEQ)).then_inc(d_v, 16)
                    sp.wait_ge(d_st[0], 32 * 5)
                    sp.wait_ge(d_st[1], 32 * 4)

                @block.tensor
                def _(pe):
                    def sample_part(n):
                        each = 2 * SEQS * NPG // (2 * DC)
                        for j, page in (divmod(m, SEQS * NPG) for m in range(n * each, (n + 1) * each)):
                            out = bank[7][:, j * P:(j + 1) * P]
                            if page == 0:
                                nc.tensor.matmul(out, v_nat[0:NS, TILES, j * P:(j + 1) * P], pnT[:, j, :], start=True, stop=False, skip_group_check=True)
                            s, k = divmod(page, NPG)
                            mine = slice(s * DSEQ, (s + 1) * DSEQ)
                            last = nc.tensor.matmul(out.rearrange("p (h n) -> p h n", h=4)[:, :, mine], v_pg[:, page, j * P:(j + 1) * P],
                                                    prT[:, j, k, :].rearrange("p (h n) -> p h n", h=4)[:, :, mine],
                                                    start=False, stop=(page == SEQS * NPG - 1), skip_group_check=True)
                            if page == SEQS * NPG - 1:
                                last.then_inc(c_o, 1)

                    for t in range(TA + 1):
                        if t < TA:
                            r = rows(t)
                            if t >= 2:
                                pe.wait_ge(d_z, t - 1)
                            if t == TILES - 1:
                                pe.wait_ge(c_trpe, 4)
                                pe.wait_ge(c_pg[2], 16 * SEQS * NPG)
                            if t == TILES:
                                pe.wait_ge(c_out, QH)
                            for half in range(2):
                                if t == 0:
                                    pe.wait_ge(d_w[half], 16)
                                for k in range(DC):
                                    lhs = mixa[:, k, t * P:t * P + r] if k < 4 else q_nat[:, t, (k - 4) * P:(k - 4) * P + r]
                                    last = nc.tensor.matmul(bank[2 + 2 * (t % 2) + half][0:r, :], lhs, w_o[:, k, half * 512:(half + 1) * 512],
                                                            start=(k == 0), stop=(k == DC - 1))
                                    if t == TILES - 1:
                                        sample_part(half * DC + k)
                            last.then_inc(d_mm, 1)
                        if t == TILES - 2:
                            for j in range(2):
                                pe.wait_ge(c_pn, j + 1)
                                if j >= 1:
                                    pe.wait_ge(c_trpe, 2 * j)
                                for k in range(NPG):
                                    last = nc.tensor.transpose(bank[7][:, k * P:(k + 1) * P], pr[:, j, k * P:(k + 1) * P], c("ident"))
                                last.then_inc(c_trp, 1)
                                pe.wait_ge(c_trpe, 2 * j + 1)
                                nc.tensor.transpose(bank[7][0:NS, 0:P], pn[:, j, :], c("ident")).then_inc(c_trp, 1)
                        if t >= 1:
                            m, r = t - 1, rows(t - 1)
                            pe.wait_ge(d_h2, m + 1)
                            for j in range(2):
                                if m >= 1:
                                    pe.wait_ge(d_tre, 2 * m - 1 + j)
                                for k in range(4):
                                    last = nc.tensor.transpose(bank[j][:, k * P:k * P + r], h2[0:r, m % 2, (4 * j + k) * P:(4 * j + k + 1) * P],
                                                               c("ident", r)[:, 0:r])
                                last.then_inc(d_trf, 1)
                            pe.wait_ge(d_tre, 2 * m + 2)
                            pe.wait_ge(d_v, 16 * 7)
                            if m >= 1:
                                pe.wait_ge(d_lge, m)
                            for k in range(DC):
                                last = nc.tensor.matmul(bank[6][0:r, 0:NG + NE], h2T[:, k, 0:r], rw[:, k, :], start=(k == 0), stop=(k == DC - 1))
                            last.then_inc(d_lg, 1)
                @block.scalar
                def _(act):
                    for t in range(TA):
                        r = rows(t)
                        for j in range(2):
                            act.wait_ge(d_trf, 2 * t + j + 1)
                            if t >= 1:
                                act.wait_ge(d_lg, t)
                            nc.scalar.activation(h2T[:, 4 * j:4 * j + 4, 0:r], bank[j].rearrange("p (k r) -> p k r", k=4)[:, :, 0:r],
                                                 ACT.Copy).then_inc(d_tre, 1)
                        act.wait_ge(d_lg, t + 1)
                        nc.scalar.activation(logit[0:r, t, :], bank[6][0:r, 0:NG + NE], ACT.Copy).then_inc(d_lge, 1)
                        if t == TILES - 5:
                            for j in range(2):
                                act.wait_ge(c_nmx, j + 1)
                                nc.scalar.activation(pr[:, j, :], pr[:, j, :], ACT.Exp, bias=st[:, j, 1:2], scale=HD ** -0.5,
                                                     accum_out=st[:, j, 2:3]).then_inc(c_exp, 1)
                        if t == TILES - 4:
                            for j in range(2):
                                act.wait_ge(c_trp, 2 * j + 1)
                                nc.scalar.activation(prT[:, j, :, :], bank[7].rearrange("p (k n) -> p k n", k=NPG), ACT.Copy).then_inc(c_trpe, 1)
                                act.wait_ge(c_trp, 2 * j + 2)
                                nc.scalar.activation(pnT[:, j, :], bank[7][0:NS, 0:P], ACT.Copy).then_inc(c_trpe, 1)
                        if t == TILES - 3:
                            act.wait_ge(c_o, 2)
                            for j in range(2):
                                for hh in range(4):
                                    src, dst = HD * (hh // 2), HD * (hh % 2)
                                    chunk = 2 * j + hh // 2
                                    nc.scalar.activation(q_nat[dst:dst + HD, TILES, chunk * P:chunk * P + NS],
                                                         bank[7][src:src + HD, j * P + hh * NS:j * P + (hh + 1) * NS], ACT.Copy).then_inc(c_out, 1)

                @block.gpsimd
                def _(pool):
                    g = nc.gpsimd
                    for t in range(TA):
                        r, b = rows(t), t % 2
                        pool.wait_ge(d_mv, t + 1)
                        g.tensor_scalar(mv[0:r, b, 1:2], mv[0:r, b, 1:2], EPS, None, ALU.add).then_inc(d_pool, 1)
                        pool.wait_ge(d_pool, 2 * t + 1)
                        g.tensor_tensor(mv[0:r, b, 1:2], mv[0:r, b, 1:2], c("minushalf", r)[:, 0:1], ALU.pow).then_inc(d_rs, 1)
                        pool.wait_ge(d_x1, t + 1)
                        if t >= 2:
                            pool.wait_ge(d_st[b], 32 * (t // 2))
                            pool.wait_ge(d_trf, 2 * (t - 1))
                        if t == TILES:
                            pool.wait_ge(d_v, 16 * (7 + 3 * SEQS))
                        g.tensor_tensor(h2[0:r, b, :], z[0:r, b, :], vec["scale2"][0:r, :], ALU.mult).then_inc(d_pool, 1)
                        pool.wait_ge(d_pool, 2 * t + 2)
                        g.tensor_tensor(h2[0:r, b, :], h2[0:r, b, :], vec["shift2"][0:r, :], ALU.add).then_inc(d_h2, 1)

                @block.vector
                def _(dve):
                    v = nc.vector
                    count = [0]

                    def then(ins):
                        count[0] += 1
                        ins.then_inc(d_dve, 1)
                        dve.wait_ge(d_dve, count[0])

                    ROUNDS = TOPK_S // 8 + 1

                    def select(first, end):
                        for n in range(first, end):
                            then(v.max(out=top[:, :], in_=sc))
                            if n == ROUNDS - 1:
                                then(v.memset(top[:, TOPK_S % 8:8], NEG_TAKEN))
                            then(v.match_replace(out=sc, in_to_replace=top[:, :], in_values=sc, imm_value=NEG_TAKEN))

                    def mask_scores():
                        then(v.tensor_scalar(sc, sc, NEG_TAKEN, NEG_MASK, ALU.not_equal, ALU.mult))
                        for j in range(2):
                            then(v.tensor_tensor(pr[:, j, :], pr[:, j, :], sc, ALU.add))
                            then(v.tensor_reduce(st[:, j, 0:1], pr[:, j, :], AX, ALU.max))
                            v.tensor_scalar(st[:, j, 1:2], st[:, j, 0:1], -HD ** -0.5, None, ALU.mult).then_inc(c_nmx, 1)

                    def normalise():
                        for j in range(2):
                            dve.wait_ge(c_exp, j + 1)
                            then(v.reciprocal(st[:, j, 3:4], st[:, j, 2:3]))
                            then(v.tensor_scalar(pr[:, j, :], pr[:, j, :], st[:, j, 3:4], None, ALU.mult))
                            v.tensor_tensor(pn[:, j, :].rearrange("p (s n) -> p s n", s=SEQS),
                                            pr[:, j:j + 1, PAST:L].to_broadcast([P, SEQS, DSEQ]),
                                            c("own").unsqueeze(2).to_broadcast([P, SEQS, DSEQ]), ALU.mult).then_inc(c_pn, 1)

                    v.memset(logit[:, TILES, :], 0.0).then_inc(d_dve, 1)
                    count[0] += 1
                    for t in range(TA):
                        r, b = rows(t), t % 2
                        zz = z[0:r, b, :]
                        dve.wait_ge(d_mm, t + 1)
                        dve.wait_ge(d_v, 16 * 7 if t < TILES else 16 * (7 + 3 * SEQS))
                        if t >= 2:
                            dve.wait_ge(d_st[b], 32 * (t // 2))
                            dve.wait_ge(d_h2, t - 1)
                        v.tensor_tensor(zz, psum[0:r, 512 * (2 + 2 * b):512 * (4 + 2 * b)], vec["gate1"][0:r, :], ALU.mult).then_inc(d_z, 1)
                        dve.wait_ge(d_z, t + 1)
                        dve.wait_ge(d_x[b], 16 * (t // 2 + 1))
                        then(v.scalar_tensor_tensor(out=zz, in0=xr[0:r, b, :], scalar=ALPHA, in1=zz, op0=ALU.mult, op1=ALU.add))
                        v.bn_stats(stat[0:r, b, 0, :], z[0:r, b, 0:512])
                        then(v.bn_stats(stat[0:r, b, 1, :], z[0:r, b, 512:1024]))
                        v.bn_aggr(mv[0:r, b, :], stat[0:r, b, :, :]).then_inc(d_mv, 1)
                        if t < TILES - 4:
                            select(t * ROUNDS // (TILES - 4), (t + 1) * ROUNDS // (TILES - 4))
                        elif t == TILES - 4:
                            mask_scores()
                        elif t == TILES - 3:
                            normalise()
                        dve.wait_ge(d_rs, t + 1)
                        then(v.tensor_scalar(zz, zz, mv[0:r, b, 0:1], mv[0:r, b, 1:2], ALU.subtract, ALU.mult))
                        then(v.tensor_tensor(zz, zz, vec["ln1_g"][0:r, :], ALU.mult))
                        v.tensor_tensor(zz, zz, vec["ln1_b"][0:r, :], ALU.add).then_inc(d_x1, 1)

        tail.close()
        consts.append(sb(keep, "const_r", [P, table.shape[1] - early]))
        vec2 = {n: sb(keep, "v2" + n, [P, D]) for n in ("gate2", "ln2_g", "ln2_b")}
        g_v = sem(keep, "g_v")
        weight = sb(keep, "weight", [P, 2, TILES + 1])
        slot = sb(keep, "slot", [P, 2, TILES + 1], I32)
        tokens = sb(keep, "tokens", [P, SLOTS], I32)
        exi = sb(keep, "exi", [1, MAXEXTRA + 1], I32)
        x1 = sb(keep, "x1", [P, 4, D])
        g_x = [sem(keep, f"g_x{i}") for i in range(4)]

        weights = keep.enter_context(ExitStack())
        wg = sb(weights, "wg", [P, 2, DC, DE])
        wu = sb(weights, "wu", [P, 2, DC, DE])
        wd = sb(weights, "wd", [P, 2, DE // P, D])
        KD = DE // P
        wg_v = a["w_gate"][0].rearrange("e (p k) f -> e p k f", k=DC)
        wu_v = a["w_up"][0].rearrange("e (p k) f -> e p k f", k=DC)
        wd_v = a["w_down"][0].rearrange("e (p k) n -> e p k n", k=KD)
        f_w = {n: [sem(keep, f"f_w{n}{i}") for i in range(2)] for n in "gud"}

        with ExitStack() as ctx:
            R = [P, TA]
            t3 = lambda n, k: sb(ctx, n, [P, TA, k])
            gmax, gsum, gw = sb(ctx, "gmax", R), sb(ctx, "gsum", R), sb(ctx, "gw", R)
            gs, ohg, gpri = t3("gs", NG), t3("ohg", NG), t3("gpri", NG)
            prod = sb(ctx, "prod", [P, TA, NG, EPG])
            el = t3("el", EPG)
            pri = t3("pri", EPG)
            oh = [t3("oh1", EPG), t3("oh2", EPG)]
            m12 = sb(ctx, "m12", [P, 2, TA])
            pm = sb(ctx, "pm", R)
            ex = sb(ctx, "ex", R)
            mk = [sb(ctx, f"mk{k}", [P, TA, NE]) for k in range(2)]
            msum = sb(ctx, "msum", [P, TA, NE])
            base = sb(ctx, "base", [P, TA + 1, NE])
            rank = sb(ctx, "rank", [P, TA, NE])
            over = sb(ctx, "over", [P, NE, 8])
            extra = sb(ctx, "extra", [P, NE])
            incl = sb(ctx, "incl", [P, NE])
            ebase = sb(ctx, "ebase", [P, NE])
            rr, eb, ei, jj, j0 = (sb(ctx, n, R) for n in ("rr", "eb", "ei", "jj", "j0"))
            ge = sb(ctx, "ge", [P, TA, 8])
            tile_of = sb(ctx, "tile_of", [P, 2, TA])
            pos_of = sb(ctx, "pos_of", [P, 2, TA])
            slot_f = sb(ctx, "slot_f", [P, 2, TA])
            onepos = sb(ctx, "onepos", [P, 2 * TA, P])
            onetile = sb(ctx, "onetile", [P, 2 * TA, SLOTS])
            below = sb(ctx, "below", [1, MAXEXTRA, NE])
            exf = sb(ctx, "exf", [1, MAXEXTRA + 1])
            prod2 = prod[:, :, :, :].rearrange("p t g e -> p t (g e)")
            e_const = sem(ctx, "e_const")
            e_dve = sem(ctx, "e_dve")
            e_exp = sem(ctx, "e_exp")
            e_m = sem(ctx, "e_m")
            e_pre = sem(ctx, "e_pre")
            e_one = sem(ctx, "e_one")
            e_list = sem(ctx, "e_list")
            DV = {}

            with nc.Block() as block:
                @block.sync
                def _(sp):
                    sp.dma_start(consts[1][:, :], a["table"][:, early:table.shape[1]]).then_inc(e_const, 16)
                    for e in range(2):
                        for w, view, n in ((wg, wg_v, "g"), (wu, wu_v, "u"), (wd, wd_v, "d")):
                            sp.dma_start(w[:, e, :, :], view[e]).then_inc(f_w[n][e], 16)

                @block.vector
                def _(dve):
                    v = nc.vector
                    count = [0]
                    dve.wait_ge(e_const, 16)

                    def then(ins):
                        count[0] += 1
                        ins.then_inc(e_dve, 1)
                        dve.wait_ge(e_dve, count[0])

                    def bc(x, *shape):
                        return x.to_broadcast(list(shape))

                    def one_hot(dst, x, top, n, priority, scratch):
                        then(v.tensor_tensor(scratch, x, bc(top.unsqueeze(2), P, TA, n), ALU.is_equal))
                        then(v.tensor_tensor(scratch, scratch, bc(priority.unsqueeze(1), P, TA, n), ALU.mult))
                        then(v.tensor_reduce(pm[:, :], scratch, AX, ALU.max))
                        then(v.tensor_tensor(dst, scratch, bc(pm[:, :].unsqueeze(2), P, TA, n), ALU.is_equal))

                    G = logit[:, :, 0:NG]
                    E = logit[:, :, NG:NG + NE].rearrange("p t (g e) -> p t g e", g=NG)
                    first = c("first")
                    then(v.tensor_reduce(gmax[:, :], G, AX, ALU.max))
                    then(v.tensor_tensor(gs[:, :, :], G, bc(gmax[:, :].unsqueeze(2), P, TA, NG), ALU.subtract))
                    DV["gs"] = count[0]
                    one_hot(ohg[:, :, :], G, gmax[:, :], NG, first[:, 0:NG], gpri[:, :, :])
                    then(v.tensor_tensor(prod[:, :, :, :], E, bc(ohg[:, :, :].unsqueeze(3), P, TA, NG, EPG), ALU.mult))
                    then(v.tensor_reduce(el[:, :, :], prod[:, :, :, :].rearrange("p t g e -> p t e g"), AX, ALU.add))
                    for k in range(2):
                        then(v.tensor_reduce(m12[:, k, :], el[:, :, :], AX, ALU.max))
                        one_hot(oh[k][:, :, :], el[:, :, :], m12[:, k, :], EPG, first, pri[:, :, :])
                        if k == 0:
                            then(v.scalar_tensor_tensor(out=el[:, :, :], in0=oh[0][:, :, :], scalar=NEG_INADM, in1=el[:, :, :],
                                                        op0=ALU.mult, op1=ALU.add))
                    then(v.tensor_tensor(ex[:, :], m12[:, 1, :], m12[:, 0, :], ALU.subtract))
                    DV["ex"] = count[0]
                    for k in range(2):
                        then(v.tensor_tensor(mk[k][:, :, :].rearrange("p t (g e) -> p t g e", g=NG),
                                             bc(oh[k][:, :, :].unsqueeze(2), P, TA, NG, EPG), bc(ohg[:, :, :].unsqueeze(3), P, TA, NG, EPG), ALU.mult))
                        then(v.tensor_tensor(mk[k][:, :, :], mk[k][:, :, :], bc(c("valid").unsqueeze(2), P, TA, NE), ALU.mult))
                    v.tensor_tensor(msum[:, :, :], mk[0][:, :, :], mk[1][:, :, :], ALU.add).then_inc(e_m, 1)
                    dve.wait_ge(e_exp, 2)
                    then(v.tensor_reduce(gsum[:, :], gs[:, :, :], AX, ALU.add))
                    then(v.reciprocal(gw[:, :], gsum[:, :]))
                    then(v.tensor_scalar(pm[:, :], ex[:, :], 1.0, None, ALU.add))
                    then(v.reciprocal(pm[:, :], pm[:, :]))
                    then(v.tensor_tensor(weight[:, 0, :], gw[:, :], pm[:, :], ALU.mult))
                    then(v.tensor_tensor(weight[:, 1, :], weight[:, 0, :], ex[:, :], ALU.mult))
                    dve.wait_ge(e_pre, 2)
                    then(v.memset(base[:, 0, :], 0.0))
                    for t in range(TA):
                        then(v.tensor_tensor(base[:, t + 1, :], base[:, t, :], bank[3][:, t * NE:(t + 1) * NE], ALU.add))
                    then(v.tensor_tensor(rank[:, :, :], bank[2][:, 0:TA * NE].rearrange("p (t e) -> p t e", e=NE), base[:, 0:TA, :], ALU.add))
                    then(v.tensor_tensor(over[:, :, :], bc(base[:, TA, :].unsqueeze(2), P, NE, 8), bc(c("steps").unsqueeze(1), P, NE, 8), ALU.is_gt))
                    then(v.tensor_reduce(extra[:, :], over[:, :, :], AX, ALU.add))
                    then(v.tensor_tensor_scan(incl[:, :], c("ones")[:, 0:NE], extra[:, :], 0.0, ALU.mult, ALU.add))
                    then(v.tensor_tensor(ebase[:, :], incl[:, :], extra[:, :], ALU.subtract))
                    then(v.tensor_scalar(ebase[:, :], ebase[:, :], float(NE - 1), None, ALU.add))
                    for k in range(2):
                        for dst, src in ((rr, rank[:, :, :]), (eb, bc(ebase[:, :].unsqueeze(1), P, TA, NE)),
                                         (ei, bc(c("iota")[:, 0:NE].unsqueeze(1), P, TA, NE))):
                            then(v.tensor_tensor(prod2, mk[k][:, :, :], src, ALU.mult))
                            then(v.tensor_reduce(dst[:, :], prod2, AX, ALU.add))
                        then(v.tensor_tensor(ge[:, :, :], bc(rr[:, :].unsqueeze(2), P, TA, 8), bc(c("steps").unsqueeze(1), P, TA, 8), ALU.is_ge))
                        then(v.tensor_reduce(jj[:, :], ge[:, :, :], AX, ALU.add))
                        then(v.tensor_scalar(j0[:, :], jj[:, :], 0.0, None, ALU.is_equal))
                        then(v.tensor_tensor(eb[:, :], eb[:, :], jj[:, :], ALU.add))
                        then(v.tensor_tensor(ei[:, :], ei[:, :], eb[:, :], ALU.subtract))
                        then(v.tensor_tensor(ei[:, :], ei[:, :], j0[:, :], ALU.mult))
                        then(v.tensor_tensor(tile_of[:, k, :], ei[:, :], eb[:, :], ALU.add))
                        then(v.scalar_tensor_tensor(out=pos_of[:, k, :], in0=jj[:, :], scalar=-float(P), in1=rr[:, :], op0=ALU.mult, op1=ALU.add))
                        then(v.scalar_tensor_tensor(out=slot_f[:, k, :], in0=tile_of[:, k, :], scalar=float(P), in1=pos_of[:, k, :],
                                                    op0=ALU.mult, op1=ALU.add))
                    then(v.tensor_copy(slot[:, :, :], slot_f[:, :, :]))
                    for k in range(2):
                        for t in range(TA):
                            v.tensor_scalar(onepos[:, k * TA + t, :], c("iota"), pos_of[:, k, t:t + 1], None, ALU.is_equal).then_inc(e_one, 1)
                            v.tensor_scalar(onetile[:, k * TA + t, :], c("iota")[:, 0:SLOTS], tile_of[:, k, t:t + 1], c("token")[:, t:t + 1],
                                            ALU.is_equal, ALU.mult).then_inc(e_one, 1)
                    then(v.tensor_tensor(below[:, :, :], bc(incl[0:1, :].unsqueeze(1), 1, MAXEXTRA, NE),
                                         bc(c("iota", 1)[:, 0:MAXEXTRA].unsqueeze(2), 1, MAXEXTRA, NE), ALU.is_le))
                    then(v.tensor_reduce(exf[:, 0:MAXEXTRA], below[:, :, :], AX, ALU.add))
                    then(v.tensor_scalar(exf[:, 0:MAXEXTRA], exf[:, 0:MAXEXTRA], float(NE - 1), None, ALU.min))
                    then(v.tensor_copy(exf[:, MAXEXTRA:MAXEXTRA + 1], incl[0:1, NE - 1:NE]))
                    then(v.tensor_copy(exi[:, :], exf[:, :]))
                    dve.wait_ge(e_list, 1)
                    then(v.tensor_copy(tokens[:, :], bank[4][:, 0:SLOTS]))

                @block.scalar
                def _(act):
                    act.wait_ge(e_dve, DV["gs"])
                    nc.scalar.activation(gs[:, :, :], gs[:, :, :], ACT.Exp).then_inc(e_exp, 1)
                    act.wait_ge(e_dve, DV["ex"])
                    nc.scalar.activation(ex[:, :], ex[:, :], ACT.Exp).then_inc(e_exp, 1)

                @block.tensor
                def _(pe):
                    pe.wait_ge(e_m, 1)
                    m = msum[:, :, :].rearrange("p t e -> p (t e)")
                    nc.tensor.matmul(bank[2][:, 0:TA * NE], c("before"), m, start=True, stop=True).then_inc(e_pre, 1)
                    nc.tensor.matmul(bank[3][:, 0:TA * NE], c("ones"), m, start=True, stop=True).then_inc(e_pre, 1)
                    for n in range(2 * TA):
                        pe.wait_ge(e_one, 2 * n + 2)
                        last = nc.tensor.matmul(bank[4][:, 0:SLOTS], onepos[:, n, :], onetile[:, n, :], start=(n == 0), stop=(n == 2 * TA - 1))
                    last.then_inc(e_list, 1)

        with ExitStack() as ctx:
            xg = sb(ctx, "xg", [P, 2, D])
            xgT = sb(ctx, "xgT", [P, 2, DC, P])
            silu = sb(ctx, "silu", [P, 2, DE])
            hid = sb(ctx, "hid", [P, 2, DE])
            hidT = sb(ctx, "hidT", [P, 2, DE // P, P])
            yy = sb(ctx, "yy", [P, 2, D])
            ys_v = ys_dram.rearrange("(e p) n -> e p n", p=P)
            f_x = [sem(ctx, f"f_x{i}") for i in range(2)]
            f_tx = sem(ctx, "f_tx")
            f_xa = sem(ctx, "f_xa")
            f_xv = sem(ctx, "f_xv")
            f_g = sem(ctx, "f_g")
            f_u = sem(ctx, "f_u")
            f_silu = sem(ctx, "f_silu")
            f_hid = sem(ctx, "f_hid")
            f_th = sem(ctx, "f_th")
            f_ht = sem(ctx, "f_ht")
            f_d = sem(ctx, "f_d")
            f_ya = sem(ctx, "f_ya")
            f_yv = sem(ctx, "f_yv")
            f_st = [sem(ctx, f"f_st{i}") for i in range(2)]
            x_st = sem(ctx, "x_st")

            def steps(eng, step):
                step(0, 0, 0)
                step(1, 1, 0)
                step(2, 0, 1)
                with eng.Fori(1, (NE - 2) // 2) as i:
                    step(2 * i + 1, 1, i)
                    step(2 * i + 2, 0, i + 1)
                step(NE - 1, 1, (NE - 2) // 2)

            def at_least(e, n):
                return e >= n if type(e) is int else n <= 1

            def count_extras(eng):
                return eng.value_load(exi[0:1, MAXEXTRA:MAXEXTRA + 1], min_val=0, max_val=MAXEXTRA)

            def extras(eng, n, body):
                for b in range(2):
                    with eng.If(n > b):
                        body(NE + b, b, NE // 2)
                with eng.Fori(1, MAXEXTRA // 2) as i:
                    for b in range(2):
                        with eng.If(n > 2 * i + b):
                            body(2 * i + NE + b, b, i + NE // 2)

            def gate_mm(b):
                for k in range(DC):
                    last = nc.tensor.matmul(bank[2], xgT[:, b, k, :], wg[:, b, k, :], start=(k == 0), stop=(k == DC - 1))
                return last

            def up_mm(b):
                for k in range(DC):
                    last = nc.tensor.matmul(bank[3], xgT[:, b, k, :], wu[:, b, k, :], start=(k == 0), stop=(k == DC - 1))
                return last

            def down_mm(b):
                for half in range(2):
                    for k in range(KD):
                        last = nc.tensor.matmul(bank[4 + half], hidT[:, b, k, :], wd[:, b, k, half * 512:(half + 1) * 512],
                                                start=(k == 0), stop=(k == KD - 1))
                return last

            def x_transposes(b):
                x = xg[:, b, :].rearrange("p (m k) -> p k m", k=DC)
                for k in range(DC):
                    last = nc.tensor.transpose(bank[1 if k < 4 else 7][:, (k % 4) * P:(k % 4 + 1) * P], x[:, k, :], c("ident"))
                return last

            def hid_transposes(b):
                h = hid[:, b, :].rearrange("p (m k) -> p k m", k=KD)
                for k in range(KD):
                    last = nc.tensor.transpose(bank[0][:, k * P:(k + 1) * P], h[:, k, :], c("ident"))
                return last

            with nc.Block() as block:
                @block.sync
                def _(sp):
                    n_extra = count_extras(sp)
                    first_two = [sp.value_load(exi[0:1, b:b + 1], min_val=0, max_val=NE - 1) for b in range(2)]
                    sp.dma_start(vec2["gate2"][:, :], mod_dram[0, 5 * D:6 * D].partition_broadcast(P)).then_inc(x_st, 16)
                    for n in ("ln2_g", "ln2_b"):
                        sp.dma_start(vec2[n][:, :], a[n][0].partition_broadcast(P)).then_inc(g_v, 16)
                    with sp.Fori(0, (NE - 2) // 2) as i:
                        for b in range(2):
                            e = 2 * i + b
                            for n, w, used in (("g", wg, f_g), ("u", wu, f_u), ("d", wd, f_d)):
                                src = {"g": wg_v, "u": wu_v, "d": wd_v}[n][bass.ds(e + 2, 1), :, :, :].rearrange("e p k n -> p (e k) n")
                                sp.wait_ge(used, e + 1)
                                sp.dma_start(w[:, b, :, :], src).then_inc(f_w[n][b], 16)

                    def extra(e, b, half):
                        owner = first_two[b] if type(e) is int else sp.value_load(exi[0:1, bass.ds(e - NE, 1)], min_val=0, max_val=NE - 1)
                        for n, w, view, used in (("g", wg, wg_v, f_g), ("u", wu, wu_v, f_u), ("d", wd, wd_v, f_d)):
                            sp.wait_ge(used, e - 1)
                            sp.dma_start(w[:, b, :, :], view[bass.ds(owner, 1), :, :, :].rearrange("e p k n -> p (e k) n")).then_inc(f_w[n][b], 16)
                    extras(sp, n_extra, extra)
                    sp.wait_ge(x_st, 16 * (n_extra + 1))
                    for t in range(4):
                        sp.dma_start(x1[:, t, :], x1_dram[t * P:(t + 1) * P, :]).then_inc(g_x[t], 16)

                @block.gpsimd
                def _(pool):
                    n_extra = count_extras(pool)
                    for e in range(NE):
                        if e >= 2:
                            pool.wait_ge(f_tx, e - 1)
                        nc.gpsimd.indirect_dma_start(out=xg[:, e % 2, :], out_offset=None, in_=h2_dram[:, :],
                                                     in_offset=bass.IndirectOffsetOnAxis(ap=tokens[:, e:e + 1].bitcast(U32), axis=0)).then_inc(f_x[e % 2], 16)
                    for i in range(MAXEXTRA):
                        with pool.If(n_extra > i):
                            pool.wait_ge(f_tx, NE + i - 1)
                            nc.gpsimd.indirect_dma_start(out=xg[:, i % 2, :], out_offset=None, in_=h2_dram[:, :],
                                                         in_offset=bass.IndirectOffsetOnAxis(ap=tokens[:, NE + i:NE + i + 1].bitcast(U32), axis=0)).then_inc(f_x[i % 2], 16)

                @block.tensor
                def _(pe):
                    n_extra = count_extras(pe)
                    pe.wait_ge(f_x[0], 16)
                    x_transposes(0).then_inc(f_tx, 1)

                    def step(e, b, half):
                        pe.wait_ge(f_xa, e + 1)
                        pe.wait_ge(f_xv, e + 1)
                        pe.wait_ge(f_w["g"][b], 16 * (half + 1))
                        if at_least(e, 1):
                            pe.wait_ge(f_silu, e)
                        gate_mm(b).then_inc(f_g, 1)
                        if at_least(e, 1):
                            pe.wait_ge(f_hid, e)
                            hid_transposes(1 - b).then_inc(f_th, 1)
                        pe.wait_ge(f_w["u"][b], 16 * (half + 1))
                        up_mm(b).then_inc(f_u, 1)
                        if not (type(e) is int and e == NE - 1):
                            pe.wait_ge(f_x[1 - b], 16 * (half + 1 + b))
                            x_transposes(1 - b).then_inc(f_tx, 1)
                        if at_least(e, 1):
                            down(e, 1 - b, half + (b - 1))

                    def down(e, b, half):
                        pe.wait_ge(f_ht, e)
                        pe.wait_ge(f_w["d"][b], 16 * (half + 1))
                        if type(e) is not int or e >= 2:
                            pe.wait_ge(f_ya, e - 1)
                            pe.wait_ge(f_yv, e - 1)
                        down_mm(b).then_inc(f_d, 1)

                    steps(pe, step)
                    pe.wait_ge(f_hid, NE)
                    hid_transposes(1).then_inc(f_th, 1)
                    down(NE, 1, NE // 2 - 1)

                    def extra(e, b, half):
                        pe.wait_ge(f_x[b], 16 * (half + 1))
                        x_transposes(b).then_inc(f_tx, 1)
                        pe.wait_ge(f_xa, e + 1)
                        pe.wait_ge(f_xv, e + 1)
                        pe.wait_ge(f_w["g"][b], 16 * (half + 1))
                        gate_mm(b).then_inc(f_g, 1)
                        pe.wait_ge(f_w["u"][b], 16 * (half + 1))
                        up_mm(b).then_inc(f_u, 1)
                        pe.wait_ge(f_hid, e + 1)
                        hid_transposes(b).then_inc(f_th, 1)
                        pe.wait_ge(f_ht, e + 1)
                        pe.wait_ge(f_w["d"][b], 16 * (half + 1))
                        pe.wait_ge(f_ya, e)
                        pe.wait_ge(f_yv, e)
                        down_mm(b).then_inc(f_d, 1)
                    extras(pe, n_extra, extra)

                @block.scalar
                def _(act):
                    s = nc.scalar

                    def x_part(e, b):
                        act.wait_ge(f_tx, e + 1)
                        s.activation(xgT[:, b, 0:4, :], bank[1], ACT.Copy).then_inc(f_xa, 1)

                    def hid_part(e, b):
                        act.wait_ge(f_th, e)
                        s.activation(hidT[:, b, :, :], bank[0], ACT.Copy).then_inc(f_ht, 1)

                    def y_part(e, b, half):
                        act.wait_ge(f_d, e)
                        if type(e) is not int or e >= 3:
                            act.wait_ge(f_st[b], 16 * half)
                        s.activation(yy[:, b, 0:512], bank[4], ACT.Copy).then_inc(f_ya, 1)
                        act.wait_ge(f_ya, e)
                        act.wait_ge(f_yv, e)
                        dst = ys_v[e - 1] if type(e) is int else ys_v[bass.ds(e - 1, 1), :, :].rearrange("e p n -> p (e n)")
                        act.dma_start(dst, yy[:, b, :]).then_inc(f_st[b], 16)

                    n_extra = count_extras(act)
                    x_part(0, 0)

                    def step(e, b, half):
                        act.wait_ge(f_g, e + 1)
                        s.activation(silu[:, b, :], bank[2], ACT.Silu).then_inc(f_silu, 1)
                        if at_least(e, 1):
                            hid_part(e, 1 - b)
                        if not (type(e) is int and e == NE - 1):
                            x_part(e + 1, 1 - b)
                        if at_least(e, 1):
                            y_part(e, 1 - b, half + b - 1)

                    steps(act, step)
                    hid_part(NE, 1)
                    y_part(NE, 1, NE // 2 - 1)
                    def extra(e, b, half):
                        x_part(e, b)
                        act.wait_ge(f_g, e + 1)
                        s.activation(silu[:, b, :], bank[2], ACT.Silu).then_inc(f_silu, 1)
                        hid_part(e + 1, b)
                        act.wait_ge(x_st, 16 * (e - NE + 1))
                        if type(e) is int:
                            act.wait_ge(f_st[b], 16 * NE // 2)
                        act.wait_ge(f_d, e + 1)
                        s.activation(yy[:, b, 0:512], bank[4], ACT.Copy).then_inc(f_ya, 1)
                        act.wait_ge(f_ya, e + 1)
                        act.wait_ge(f_yv, e + 1)
                        dst = ys_v[e] if type(e) is int else ys_v[bass.ds(e, 1), :, :].rearrange("e p n -> p (e n)")
                        act.dma_start(dst, yy[:, b, :]).then_inc(x_st, 16)
                    extras(act, n_extra, extra)
                    for b in range(2):
                        act.wait_ge(f_st[b], 16 * NE // 2)

                @block.vector
                def _(dve):
                    v = nc.vector

                    def x_part(e, b):
                        dve.wait_ge(f_tx, e + 1)
                        v.tensor_copy(xgT[:, b, 4:8, :], bank[7]).then_inc(f_xv, 1)

                    def y_part(e, b, half):
                        dve.wait_ge(f_d, e)
                        if type(e) is not int or e >= 3:
                            dve.wait_ge(f_st[b], 16 * half)
                        v.tensor_copy(yy[:, b, 512:1024], bank[5]).then_inc(f_yv, 1)

                    n_extra = count_extras(dve)
                    x_part(0, 0)

                    def step(e, b, half):
                        dve.wait_ge(f_silu, e + 1)
                        dve.wait_ge(f_u, e + 1)
                        v.tensor_tensor(hid[:, b, :], silu[:, b, :], bank[3], ALU.mult).then_inc(f_hid, 1)
                        if not (type(e) is int and e == NE - 1):
                            x_part(e + 1, 1 - b)
                        if at_least(e, 1):
                            y_part(e, 1 - b, half + b - 1)

                    steps(dve, step)
                    y_part(NE, 1, NE // 2 - 1)

                    def extra(e, b, half):
                        x_part(e, b)
                        dve.wait_ge(f_silu, e + 1)
                        dve.wait_ge(f_u, e + 1)
                        v.tensor_tensor(hid[:, b, :], silu[:, b, :], bank[3], ALU.mult).then_inc(f_hid, 1)
                        if type(e) is int:
                            dve.wait_ge(f_st[b], 16 * NE // 2)
                        else:
                            dve.wait_ge(x_st, 16 * (e - NE))
                        dve.wait_ge(f_d, e + 1)
                        v.tensor_copy(yy[:, b, 512:1024], bank[5]).then_inc(f_yv, 1)
                    extras(dve, n_extra, extra)

        weights.close()
        with ExitStack() as ctx:
            y1 = sb(ctx, "y1", [P, 4, D])
            y2 = sb(ctx, "y2", [P, 4, D])
            gate2_s = sb(ctx, "gate2_s", [NS, D])
            stat = sb(ctx, "stat2", [P, 2, 6])
            mv = sb(ctx, "mv2", [P, 2, 2])
            y_tile = [outs[0][0, t * P:(t + 1) * P, :] for t in range(TILES)] + [outs[1].rearrange("b t d -> (b t) d")]
            g_gv = sem(ctx, "g_gv")
            g_y = [sem(ctx, f"g_y{i}") for i in range(4)]
            g_dve = sem(ctx, "g_dve")
            g_w1 = sem(ctx, "g_w1")
            g_both = sem(ctx, "g_both")
            g_gated = sem(ctx, "g_gated")
            g_sum = sem(ctx, "g_sum")
            g_mv = sem(ctx, "g_mv")
            g_ctr = sem(ctx, "g_ctr")
            g_eps = sem(ctx, "g_eps")
            g_rs = sem(ctx, "g_rs")
            g_norm = sem(ctx, "g_norm")
            g_out = sem(ctx, "g_out")
            g_outv = sem(ctx, "g_outv")
            g_st = [sem(ctx, f"g_st{i}") for i in range(4)]

            with nc.Block() as block:
                @block.sync
                def _(sp):
                    for i in range(SEQS):
                        sp.dma_start(gate2_s[i * DSEQ:(i + 1) * DSEQ, :],
                                     mod_dram[1 + i, 5 * D:6 * D].partition_broadcast(DSEQ)).then_inc(g_gv, 16)
                    for t in range(TA):
                        r = rows(t)
                        sp.wait_ge(g_x[t % 4], 16 * (t // 4 + 1))
                        sp.wait_ge(g_out, t + 1)
                        sp.wait_ge(g_outv, t + 1)
                        sp.dma_start(y_tile[t], x1[0:r, t % 4, :]).then_inc(g_st[t % 4], 16)
                        if t + 4 < TA:
                            sp.wait_ge(g_st[t % 4], 16 * (t // 4 + 1))
                            r4 = rows(t + 4)
                            sp.dma_start(x1[0:r4, t % 4, :], x1_dram[(t + 4) * P:(t + 4) * P + r4, :]).then_inc(g_x[t % 4], 16)
                    for i in range(4):
                        sp.wait_ge(g_st[i], 16 * len(range(i, TA, 4)))

                @block.gpsimd
                def _(pool):
                    g = nc.gpsimd

                    def gather(t):
                        r = rows(t)
                        for k, y in enumerate((y1, y2)):
                            g.indirect_dma_start(out=y[0:r, t % 4, :], out_offset=None, in_=ys_dram[:, :],
                                                 in_offset=bass.IndirectOffsetOnAxis(ap=slot[0:r, k, t:t + 1].bitcast(U32), axis=0)).then_inc(g_y[t % 4], 16)

                    for t in range(3):
                        gather(t)
                    for t in range(TA + 2):
                        if t < TA:
                            r, f = rows(t), y1[0:rows(t), t % 4, :]
                            pool.wait_ge(g_both, t + 1)
                            if t == TILES:
                                pool.wait_ge(g_gv, 16 * SEQS)
                            gate = vec2["gate2"] if t < TILES else gate2_s
                            g.tensor_tensor(f, f, gate[0:r, :], ALU.mult).then_inc(g_gated, 1)
                        if 1 <= t <= TA:
                            r, b = rows(t - 1), (t - 1) % 2
                            pool.wait_ge(g_mv, t)
                            g.tensor_scalar(mv[0:r, b, 1:2], mv[0:r, b, 1:2], EPS, None, ALU.add).then_inc(g_eps, 1)
                            pool.wait_ge(g_eps, t)
                            g.tensor_tensor(mv[0:r, b, 1:2], mv[0:r, b, 1:2], c("minushalf", r)[:, 0:1], ALU.pow).then_inc(g_rs, 1)
                        if t + 3 < TA:
                            gather(t + 3)
                        if t >= 2:
                            r = rows(t - 2)
                            x = x1[0:r, (t - 2) % 4, :]
                            pool.wait_ge(g_norm, t - 1)
                            g.tensor_tensor(x[:, 0:512], x[:, 0:512], vec2["ln2_b"][0:r, 0:512], ALU.add).then_inc(g_out, 1)

                @block.scalar
                def _(act):
                    for t in range(TA + 2):
                        if t < TA:
                            r, b = rows(t), t % 4
                            act.wait_ge(g_y[b], 32 * (t // 4 + 1))
                            nc.scalar.activation(y1[0:r, b, :], y1[0:r, b, :], ACT.Copy, scale=weight[0:r, 0, t:t + 1]).then_inc(g_w1, 1)
                        if t >= 2:
                            r, x = rows(t - 2), x1[0:rows(t - 2), (t - 2) % 4, :]
                            act.wait_ge(g_ctr, t - 1)
                            act.wait_ge(g_rs, t - 1)
                            nc.scalar.activation(x, x, ACT.Copy, scale=mv[0:r, t % 2, 1:2]).then_inc(g_norm, 1)

                @block.vector
                def _(dve):
                    v = nc.vector
                    count = [0]

                    def then(ins):
                        count[0] += 1
                        ins.then_inc(g_dve, 1)
                        dve.wait_ge(g_dve, count[0])

                    for t in range(TA + 2):
                        if t < TA:
                            r, b = rows(t), t % 4
                            dve.wait_ge(g_w1, t + 1)
                            dve.wait_ge(g_y[b], 32 * (t // 4 + 1))
                            v.scalar_tensor_tensor(out=y1[0:r, b, :], in0=y2[0:r, b, :], scalar=weight[0:r, 1, t:t + 1],
                                                   in1=y1[0:r, b, :], op0=ALU.mult, op1=ALU.add).then_inc(g_both, 1)
                        if t >= 2:
                            r = rows(t - 2)
                            x = x1[0:r, (t - 2) % 4, 512:1024]
                            dve.wait_ge(g_norm, t - 1)
                            v.tensor_tensor(x, x, vec2["ln2_b"][0:r, 512:1024], ALU.add).then_inc(g_outv, 1)
                        if 1 <= t <= TA:
                            r, b = rows(t - 1), (t - 1) % 4
                            f, x, m = y1[0:r, b, :], x1[0:r, b, :], mv[0:r, (t - 1) % 2, :]
                            dve.wait_ge(g_gated, t)
                            dve.wait_ge(g_x[b], 16 * ((t - 1) // 4 + 1))
                            then(v.scalar_tensor_tensor(out=x, in0=x, scalar=ALPHA, in1=f, op0=ALU.mult, op1=ALU.add))
                            v.bn_stats(stat[0:r, 0, :], x[:, 0:512])
                            then(v.bn_stats(stat[0:r, 1, :], x[:, 512:1024]))
                            if t >= 3:
                                dve.wait_ge(g_norm, t - 2)
                            v.bn_aggr(m, stat[0:r, :, :]).then_inc(g_mv, 1)
                            dve.wait_ge(g_mv, t)
                            v.scalar_tensor_tensor(out=x, in0=x, scalar=m[:, 0:1], in1=vec2["ln2_g"][0:r, :],
                                                   op0=ALU.subtract, op1=ALU.mult).then_inc(g_ctr, 1)


_INS = ['x_prompt', 'x_sample', 'cache_k', 'cache_v', 'cache_kidx', 'page_table', 'c_prompt', 'c_sample',
        'w_ada', 'b_ada', 'w_in', 'a_ln_g', 'a_ln_b', 'w_spatial', 'b_spatial', 'w_out', 'ln1_g', 'ln1_b',
        'w_group_router', 'w_expert_router', 'w_gate', 'w_up', 'w_down', 'ln2_g', 'ln2_b']
_OUTS = [(1, SEQ, D), (SEQS, DSEQ, D), (1, 1, SEQ, KVH, HD), (1, 1, SEQ, KVH, HD), (1, 1, SEQ, HD),
         (1, SEQS, DSEQ, KVH, HD), (1, SEQS, DSEQ, KVH, HD), (1, SEQS, DSEQ, HD), (1, SEQS, DSEQ, AH, HD)]


def kernel(**inputs):
    import concourse.bacc as _bacc
    from concourse.bass_utils import run_bass_kernel_spmd as _run

    nc = _bacc.Bacc("TRN2", target_bir_lowering=False, num_devices=1)
    arrays, args = {}, {}
    given = {name: np.ascontiguousarray(inputs[name]) for name in _INS}
    given["table"] = constants()[1]
    for name, x in given.items():
        arrays[f"in_{name}_dram"] = x
        args[name] = nc.dram_tensor(f"in_{name}_dram", x.shape, mybir.dt.from_np(x.dtype), kind="ExternalInput").ap()
    outs = [nc.dram_tensor(f"out_{i}_dram", shape, F32, kind="ExternalOutput").ap() for i, shape in enumerate(_OUTS)]
    step_kernel(nc, args, outs)
    r = _run(nc, [arrays], core_ids=[0])
    return tuple(r.results[0][f"out_{i}_dram"] for i in range(len(_OUTS)))
```
